# Optimizing a Trainium2 kernel written in Bass

```python
import math
import jax
import jax.numpy as jnp
from jax import lax
import numpy as np

D_MODEL = 1024
BATCH = 1
SEQ = 128
DEPTH = 2
DEC_BATCH = 1
DEC_SEQ = 128
PAST_LEN = 128

GRID_W = 64
ROPE_THETA = 10000.0
EPS = 1e-6
Q_BLOCK = 128

A_HEADS = 4
A_QK_DIM = 64
A_V_DIM = 2 * A_QK_DIM
B_HEADS = 4
B_NOPE = 64
B_ROPE = 32
B_QK_DIM = B_NOPE + B_ROPE
B_V_DIM = 64
B_Q_LORA = 256
B_KV_LORA = 128
C_CH = 256
C_CONV_WIDTH = 31
POOL_WINDOWS = (2, 4, 8, 16)
D_GROUP = 64
D_CH = D_GROUP * len(POOL_WINDOWS)
N_BRANCH = 4
FFN_DIM = 2816
N_EXPERTS = 8
TOP_K = 2
EXPERT_DIM = 3584
N_DENSE = (DEPTH + 1) // 2
N_MOE = DEPTH // 2

IN_SPLIT = (
    2 * A_HEADS * A_QK_DIM,
    2 * A_HEADS * A_QK_DIM,
    A_HEADS * A_V_DIM,
    B_Q_LORA,
    B_KV_LORA,
    B_ROPE,
    2 * C_CH,
    D_CH,
    N_BRANCH * D_MODEL,
)
IN_DIM = sum(IN_SPLIT)

kernel_name = 'hybrid_diffusion_prefix_trunk_step'

def split_columns(p, sizes):
    out, start = [], 0
    for s in sizes:
        out.append(p[..., start:start + s])
        start += s
    return out

def rms_norm(x, g):
    xf = x.astype(jnp.float32)
    y = xf * lax.rsqrt(jnp.mean(xf * xf, axis=-1, keepdims=True) + EPS)
    return (y * g.astype(jnp.float32)).astype(x.dtype)

def layer_norm(x, g, b):
    xf = x.astype(jnp.float32)
    mu = jnp.mean(xf, axis=-1, keepdims=True)
    xc = xf - mu
    y = xc * lax.rsqrt(jnp.mean(xc * xc, axis=-1, keepdims=True) + EPS)
    return (y * g.astype(jnp.float32) + b.astype(jnp.float32)).astype(x.dtype)

def axial_rope(x, rows):
    nf = x.shape[-1] // 4
    freqs = ROPE_THETA ** (-jnp.arange(nf, dtype=jnp.float32) / nf)
    row = jnp.repeat(jnp.arange(rows, dtype=jnp.float32), GRID_W)
    col = jnp.tile(jnp.arange(GRID_W, dtype=jnp.float32), rows)
    ang = jnp.concatenate([row[:, None] * freqs, col[:, None] * freqs], axis=-1)[None, :, None, :]
    cos, sin = jnp.cos(ang), jnp.sin(ang)
    xf = x.astype(jnp.float32)
    x1, x2 = xf[..., 0::2], xf[..., 1::2]
    return jnp.stack([x1 * cos - x2 * sin, x1 * sin + x2 * cos], axis=-1).reshape(x.shape).astype(x.dtype)

def rope_tail(x, rows):
    return jnp.concatenate([x[..., :B_NOPE], axial_rope(x[..., B_NOPE:], rows)], axis=-1)

def blocked_queries(fn, q):
    b, t = q.shape[:2]
    nb = t // Q_BLOCK
    qb = jnp.moveaxis(q.reshape(b, nb, Q_BLOCK, *q.shape[2:]), 1, 0)
    out = lax.map(fn, qb)
    return jnp.moveaxis(out, 0, 1).reshape(b, t, *out.shape[3:])

def diff_attention(q, k, v, lam):
    b, tk = q.shape[0], k.shape[1]
    scale = A_QK_DIM ** -0.5

    def block(qb):
        s = jnp.einsum('bqhd,bkhd->bhqk', qb, k, preferred_element_type=jnp.float32) * scale
        p = jax.nn.softmax(s, axis=-1).reshape(b, A_HEADS, 2, qb.shape[1], tk)
        w = p[:, :, 0] - lam * p[:, :, 1]
        return jnp.einsum('bhqk,bkhd->bqhd', w.astype(v.dtype), v)

    return blocked_queries(block, q)

def softmax_attention(q, k, v):
    scale = q.shape[-1] ** -0.5

    def block(qb):
        s = jnp.einsum('bqhd,bkhd->bhqk', qb, k, preferred_element_type=jnp.float32) * scale
        p = jax.nn.softmax(s, axis=-1)
        return jnp.einsum('bhqk,bkhd->bqhd', p.astype(v.dtype), v)

    return blocked_queries(block, q)

def mla_expand(ckv, kpe, lp):
    b, t = ckv.shape[:2]
    kv = (ckv @ lp['b_w_ukv']).reshape(b, t, B_HEADS, B_NOPE + B_V_DIM)
    k = jnp.concatenate([kv[..., :B_NOPE], jnp.broadcast_to(kpe[:, :, None, :], (b, t, B_HEADS, B_ROPE))], axis=-1)
    return rms_norm(k, lp['b_k_norm']), kv[..., B_NOPE:]

def centred_window_mean(x, w):
    b, t, g = x.shape
    left = w // 2
    right = w - 1 - left
    cs = jnp.concatenate([jnp.zeros((b, 1, g), jnp.float32), jnp.cumsum(x.astype(jnp.float32), axis=1)], axis=1)
    pos = jnp.arange(t)
    lo = jnp.clip(pos - left, 0, t)
    hi = jnp.clip(pos + right + 1, 0, t)
    s = jnp.take(cs, hi, axis=1) - jnp.take(cs, lo, axis=1)
    cnt = (hi - lo).astype(jnp.float32)[None, :, None]
    return (s / cnt).astype(x.dtype)

def mixer(m, lp, layer, ctx):
    b, t, _ = m.shape
    latent = ctx is not None
    a_q, a_k, a_v, b_q, b_kv, b_kpe, c_in, d_in, gate_logits = split_columns(m @ lp['w_in'], IN_SPLIT)

    qa = rms_norm(a_q.reshape(b, t, 2 * A_HEADS, A_QK_DIM), lp['a_q_norm'])
    ka = rms_norm(a_k.reshape(b, t, 2 * A_HEADS, A_QK_DIM), lp['a_k_norm'])
    va = a_v.reshape(b, t, A_HEADS, A_V_DIM)
    lam_init = 0.8 - 0.6 * math.exp(-0.3 * layer)
    lmb = lp['a_lambda'].astype(jnp.float32)
    lam = jnp.exp(jnp.sum(lmb[0] * lmb[1])) - jnp.exp(jnp.sum(lmb[2] * lmb[3])) + lam_init

    qb = (rms_norm(b_q, lp['b_q_lora_norm']) @ lp['b_w_uq']).reshape(b, t, B_HEADS, B_QK_DIM)
    qb = rms_norm(qb, lp['b_q_norm'])
    ckv = rms_norm(b_kv, lp['b_kv_lora_norm'])
    kb, vb = mla_expand(ckv, b_kpe, lp)

    if latent:
        rows = t // GRID_W
        qa = axial_rope(qa, rows)
        keys_a = jnp.concatenate([axial_rope(ka, rows), ctx[0]], axis=1)
        vals_a = jnp.concatenate([va, ctx[1]], axis=1)
        qb = rope_tail(qb, rows)
        kc, vc = mla_expand(ctx[2], ctx[3], lp)
        keys_b = jnp.concatenate([rope_tail(kb, rows), kc], axis=1)
        vals_b = jnp.concatenate([vb, vc], axis=1)
    else:
        keys_a, vals_a, keys_b, vals_b = ka, va, kb, vb

    oa = rms_norm(diff_attention(qa, keys_a, vals_a, lam), lp['a_sub_norm']) * (1.0 - lam_init)
    out_a = oa.reshape(b, t, A_HEADS * A_V_DIM) @ lp['a_w_o']
    ob = softmax_attention(qb, keys_b, vals_b)
    out_b = ob.reshape(b, t, B_HEADS * B_V_DIM) @ lp['b_w_o']

    glu = c_in[..., :C_CH] * jax.nn.sigmoid(c_in[..., C_CH:])
    conv = lax.conv_general_dilated(
        glu, lp['c_dw'][:, None, :], window_strides=(1,),
        padding=[(C_CONV_WIDTH // 2, C_CONV_WIDTH // 2)],
        dimension_numbers=('NWC', 'WIO', 'NWC'), feature_group_count=C_CH) + lp['c_dw_b']
    out_c = jax.nn.silu(layer_norm(conv, lp['c_ln_g'], lp['c_ln_b'])) @ lp['c_w_o']

    xg = d_in.reshape(b, t, len(POOL_WINDOWS), D_GROUP)
    pooled = jnp.stack([centred_window_mean(xg[:, :, i], w) for i, w in enumerate(POOL_WINDOWS)], axis=2)
    hd = jnp.einsum('btgc,gce->btge', pooled - xg, lp['d_w_group']).reshape(b, t, D_CH) * lp['d_scale']
    out_d = hd @ lp['d_w_o']

    gates = jax.nn.sigmoid(gate_logits.reshape(b, t, N_BRANCH, D_MODEL))
    merged = (gates[..., 0, :] * out_a + gates[..., 1, :] * out_b
              + gates[..., 2, :] * out_c + gates[..., 3, :] * out_d)
    y = merged @ lp['w_out']
    new_ctx = None if latent else (ka, va, ckv, b_kpe)
    return y, new_ctx

def swiglu(x, w1, w3, w2):
    return (jax.nn.silu(x @ w1) * (x @ w3)) @ w2

def moe_swiglu(x, router, w1, w3, w2):
    logits = (x @ router).astype(jnp.float32)
    top_val, top_idx = lax.top_k(logits, TOP_K)
    wts = jax.nn.softmax(top_val, axis=-1)
    comb = jnp.sum(jax.nn.one_hot(top_idx, N_EXPERTS, dtype=jnp.float32) * wts[..., None], axis=-2).astype(x.dtype)
    y = jnp.zeros_like(x)
    for e in range(N_EXPERTS):
        y = y + comb[..., e:e + 1] * swiglu(x, w1[e], w3[e], w2[e])
    return y

def trunk_layer(x, cvec, lp, layer, ctx):
    mod = (jax.nn.silu(cvec) @ lp['ada_w'] + lp['ada_b']).reshape(*cvec.shape[:-1], 1, 6, D_MODEL)
    sh1, sc1, g1, sh2, sc2, g2 = (mod[..., i, :] for i in range(6))
    y, new_ctx = mixer(rms_norm(x, lp['norm1_g']) * (1 + sc1) + sh1, lp, layer, ctx)
    x = x + g1 * y
    h = rms_norm(x, lp['norm2_g']) * (1 + sc2) + sh2
    if layer % 2 == 0:
        f = swiglu(h, lp['ffn_w1'], lp['ffn_w3'], lp['ffn_w2'])
    else:
        f = moe_swiglu(h, lp['moe_router'], lp['moe_w1'], lp['moe_w3'], lp['moe_w2'])
    return x + g2 * f, new_ctx

def setup_inputs(seed: int = 0) -> dict:
    key = jax.random.key(seed)
    ks = iter(jax.random.split(key, 64))

    def nrm(shape, scale):
        return scale * jax.random.normal(next(ks), shape, jnp.float32)

    def gain(shape, s=0.02):
        return 1.0 + s * jax.random.normal(next(ks), shape, jnp.float32)

    L = DEPTH
    return {
        'x_prompt': nrm((BATCH, SEQ, D_MODEL), 1.0),
        'x_sample': nrm((DEC_BATCH, DEC_SEQ, D_MODEL), 1.0),
        'cache_a_k': nrm((DEC_BATCH, DEPTH, PAST_LEN, 2 * A_HEADS, A_QK_DIM), 1.0),
        'cache_a_v': nrm((DEC_BATCH, DEPTH, PAST_LEN, A_HEADS, A_V_DIM), 1.0),
        'cache_b_ckv': nrm((DEC_BATCH, DEPTH, PAST_LEN, B_KV_LORA), 1.0),
        'cache_b_kpe': nrm((DEC_BATCH, DEPTH, PAST_LEN, B_ROPE), 1.0),
        'c': nrm((DEC_BATCH, D_MODEL), 1.0),
        'c_ctx': nrm((D_MODEL,), 1.0),
        'ada_w': nrm((L, D_MODEL, 6 * D_MODEL), 0.5 * D_MODEL ** -0.5),
        'ada_b': nrm((L, 6 * D_MODEL), 0.02),
        'norm1_g': gain((L, D_MODEL)),
        'norm2_g': gain((L, D_MODEL)),
        'w_in': nrm((L, D_MODEL, IN_DIM), D_MODEL ** -0.5),
        'a_q_norm': gain((L, A_QK_DIM)),
        'a_k_norm': gain((L, A_QK_DIM)),
        'a_lambda': nrm((L, 4, A_QK_DIM), 0.1),
        'a_sub_norm': gain((L, A_V_DIM)),
        'a_w_o': nrm((L, A_HEADS * A_V_DIM, D_MODEL), (A_HEADS * A_V_DIM) ** -0.5),
        'b_q_lora_norm': gain((L, B_Q_LORA)),
        'b_kv_lora_norm': gain((L, B_KV_LORA)),
        'b_w_uq': nrm((L, B_Q_LORA, B_HEADS * B_QK_DIM), B_Q_LORA ** -0.5),
        'b_w_ukv': nrm((L, B_KV_LORA, B_HEADS * (B_NOPE + B_V_DIM)), B_KV_LORA ** -0.5),
        'b_q_norm': gain((L, B_QK_DIM)),
        'b_k_norm': gain((L, B_QK_DIM)),
        'b_w_o': nrm((L, B_HEADS * B_V_DIM, D_MODEL), (B_HEADS * B_V_DIM) ** -0.5),
        'c_dw': nrm((L, C_CONV_WIDTH, C_CH), C_CONV_WIDTH ** -0.5),
        'c_dw_b': nrm((L, C_CH), 0.02),
        'c_ln_g': gain((L, C_CH)),
        'c_ln_b': nrm((L, C_CH), 0.02),
        'c_w_o': nrm((L, C_CH, D_MODEL), C_CH ** -0.5),
        'd_w_group': nrm((L, len(POOL_WINDOWS), D_GROUP, D_GROUP), D_GROUP ** -0.5),
        'd_scale': gain((L, D_CH), 0.1),
        'd_w_o': nrm((L, D_CH, D_MODEL), D_CH ** -0.5),
        'w_out': nrm((L, D_MODEL, D_MODEL), D_MODEL ** -0.5),
        'ffn_w1': nrm((N_DENSE, D_MODEL, FFN_DIM), D_MODEL ** -0.5),
        'ffn_w3': nrm((N_DENSE, D_MODEL, FFN_DIM), D_MODEL ** -0.5),
        'ffn_w2': nrm((N_DENSE, FFN_DIM, D_MODEL), FFN_DIM ** -0.5),
        'moe_router': nrm((N_MOE, D_MODEL, N_EXPERTS), D_MODEL ** -0.5),
        'moe_w1': nrm((N_MOE, N_EXPERTS, D_MODEL, EXPERT_DIM), D_MODEL ** -0.5),
        'moe_w3': nrm((N_MOE, N_EXPERTS, D_MODEL, EXPERT_DIM), D_MODEL ** -0.5),
        'moe_w2': nrm((N_MOE, N_EXPERTS, EXPERT_DIM, D_MODEL), EXPERT_DIM ** -0.5),
    }

def reference(x_prompt, x_sample, cache_a_k, cache_a_v, cache_b_ckv, cache_b_kpe, c, c_ctx,
              ada_w, ada_b, norm1_g, norm2_g, w_in,
              a_q_norm, a_k_norm, a_lambda, a_sub_norm, a_w_o,
              b_q_lora_norm, b_kv_lora_norm, b_w_uq, b_w_ukv, b_q_norm, b_k_norm, b_w_o,
              c_dw, c_dw_b, c_ln_g, c_ln_b, c_w_o,
              d_w_group, d_scale, d_w_o,
              w_out,
              ffn_w1, ffn_w3, ffn_w2,
              moe_router, moe_w1, moe_w3, moe_w2):
    y_prompt, y_sample = x_prompt, x_sample
    ak_list, av_list, ckv_list, kpe_list = [], [], [], []
    for l in range(DEPTH):
        lp = {
            'ada_w': ada_w[l], 'ada_b': ada_b[l], 'norm1_g': norm1_g[l], 'norm2_g': norm2_g[l],
            'w_in': w_in[l],
            'a_q_norm': a_q_norm[l], 'a_k_norm': a_k_norm[l], 'a_lambda': a_lambda[l],
            'a_sub_norm': a_sub_norm[l], 'a_w_o': a_w_o[l],
            'b_q_lora_norm': b_q_lora_norm[l], 'b_kv_lora_norm': b_kv_lora_norm[l],
            'b_w_uq': b_w_uq[l], 'b_w_ukv': b_w_ukv[l], 'b_q_norm': b_q_norm[l], 'b_k_norm': b_k_norm[l],
            'b_w_o': b_w_o[l],
            'c_dw': c_dw[l], 'c_dw_b': c_dw_b[l], 'c_ln_g': c_ln_g[l], 'c_ln_b': c_ln_b[l], 'c_w_o': c_w_o[l],
            'd_w_group': d_w_group[l], 'd_scale': d_scale[l], 'd_w_o': d_w_o[l],
            'w_out': w_out[l],
        }
        j = l // 2
        if l % 2 == 0:
            lp['ffn_w1'], lp['ffn_w3'], lp['ffn_w2'] = ffn_w1[j], ffn_w3[j], ffn_w2[j]
        else:
            lp['moe_router'], lp['moe_w1'], lp['moe_w3'], lp['moe_w2'] = moe_router[j], moe_w1[j], moe_w3[j], moe_w2[j]
        y_prompt, ctx_l = trunk_layer(y_prompt, c_ctx, lp, l, None)
        ak_list.append(ctx_l[0])
        av_list.append(ctx_l[1])
        ckv_list.append(ctx_l[2])
        kpe_list.append(ctx_l[3])
        y_sample, _ = trunk_layer(y_sample, c, lp, l,
                                  (cache_a_k[:, l], cache_a_v[:, l], cache_b_ckv[:, l], cache_b_kpe[:, l]))
    new_a_k = jnp.stack(ak_list, axis=1)
    new_a_v = jnp.stack(av_list, axis=1)
    new_b_ckv = jnp.stack(ckv_list, axis=1)
    new_b_kpe = jnp.stack(kpe_list, axis=1)
    return (y_prompt, y_sample, new_a_k, new_a_v, new_b_ckv, new_b_kpe)


_drawn_inputs = setup_inputs


def setup_inputs(seed=0):
    import zlib

    import numpy as np

    out = dict(_drawn_inputs(seed))
    spreads = {}
    factors = {'cache_b_kpe': 4.138,
     'norm1_g': 2.89,
     'norm2_g': 3.563,
     'a_q_norm': 8.0,
     'a_k_norm': 2.849,
     'a_lambda': 7.767,
     'a_sub_norm': 8.0,
     'b_q_lora_norm': 8.0,
     'b_kv_lora_norm': 2.907,
     'b_q_norm': 8.0,
     'b_k_norm': 8.0,
     'c_dw_b': 4.969,
     'c_ln_g': 5.803,
     'c_ln_b': 6.413,
     'cache_a_k': 8.0,
     'cache_a_v': 8.0}
    for name, (base, spread) in spreads.items():
        noise = np.random.default_rng([zlib.crc32(name.encode()), seed]).standard_normal(out[name].shape)
        drawn = base * np.exp(spread * noise) if base else spread * noise
        out[name] = jnp.asarray(drawn.astype(out[name].dtype))
    for name, factor in factors.items():
        out[name] = (out[name] * factor).astype(out[name].dtype)
    return out
```

```python
from contextlib import ExitStack

import numpy as np
import concourse.bass as bass
from concourse import mybir

F32 = mybir.dt.float32
F32R = mybir.dt.float32r
ALU = mybir.AluOpType
ACT = mybir.ActivationFunctionType
AX = mybir.AxisListType

P = 128
D = 1024
KT = D // P
L = 2
G = 2
AH, AQK, AV = 4, 64, 128
BH, BNOPE, BROPE, BV = 4, 64, 32, 64
BQK = BNOPE + BROPE
BQL, BKVL = 256, 128
CCH, TAPS = 256, 31
PAD = TAPS // 2
POOLS = (2, 4, 8, 16)
DG, DCH = 64, 256
FFN, NE, ED = 2816, 8, 3584
EPS = 1e-6
GRID_W, THETA = 64, 10000.0

CQ, CK, CV, CBQ, CKV, CPE, CC, CD = 0, 512, 1024, 1536, 1792, 1920, 1952, 2464
CGATE = 2720
IN_CHUNKS = [(0, 512), (512, 512), (1024, 512), (1536, 416), (1952, 512), (2464, 256)]
GATE_CHUNKS = [(CGATE + 512 * c, 512) for c in range(8)]
CHUNKS = IN_CHUNKS + GATE_CHUNKS

RAW, HI = 6, 3
TW = 2048

N_ADA = 24
N_IN = 2 * len(IN_CHUNKS)
N_GATE = 2 * len(GATE_CHUNKS)
N_BR = [2, 1, 1, 1]
N_OUT = 4
N_LAYER = N_ADA + N_IN + N_GATE + sum(N_BR) + N_OUT
FCH = [(512 * j, 512) for j in range(5)] + [(2560, 256)]
N_FFN_UP = 5 * 4 + 2
N_FFN_DN = FFN // 256
N_FFN = N_FFN_UP + N_FFN_DN
ECH = [(512 * j, 512) for j in range(ED // 512)]
N_EXP_UP = 4 * len(ECH)
N_EXP_DN = ED // 256
N_EXP = N_EXP_UP + N_EXP_DN


def t_layer(l):
    return l * (N_LAYER + N_FFN)


def t_in(l):
    return t_layer(l) + N_ADA


def t_gate(l):
    return t_in(l) + N_IN


def t_branch(l, b):
    return t_gate(l) + N_GATE + sum(N_BR[:b])


def t_out(l):
    return t_gate(l) + N_GATE + sum(N_BR)


def t_ffn(l):
    return t_layer(l) + N_LAYER


def tile_floats(t):
    for l in range(L):
        if t_in(l) <= t < t_in(l) + N_IN:
            return 4 * IN_CHUNKS[(t - t_in(l)) // 2][1]
    return TW


C_ID, C_POOL, C_RA, C_RB, C_SEL, C_SELG, C_SELB, C_TRI = 0, 128, 640, 768, 832, 834, 1090, 1138
C_N = 1262


def shape_tables():
    t = np.zeros((P, C_N), np.float32)
    t[:, C_ID:C_ID + P] = np.eye(P, dtype=np.float32)
    for i, w in enumerate(POOLS):
        left, right = w // 2, w - 1 - w // 2
        for q in range(P):
            lo, hi = max(q - left, 0), min(q + right + 1, P)
            t[lo:hi, C_POOL + i * P + q] = np.float32(1) / np.float32(hi - lo)
            t[q, C_POOL + i * P + q] -= np.float32(1)
    for base, dim in ((C_RA, AQK), (C_RB, BROPE)):
        nf = dim // 4
        freqs = np.float32(THETA) ** (-np.arange(nf, dtype=np.float32) / np.float32(nf))
        tok = np.arange(P)
        row, col = (tok // GRID_W).astype(np.float32), (tok % GRID_W).astype(np.float32)
        ang = np.concatenate([row[:, None] * freqs, col[:, None] * freqs], axis=1).astype(np.float32)
        cos, sin = np.cos(ang).astype(np.float32), np.sin(ang).astype(np.float32)
        t[:, base:base + dim] = np.repeat(cos, 2, axis=1)
        t[:, base + dim:base + 2 * dim:2] = -sin
        t[:, base + dim + 1:base + 2 * dim:2] = sin
    for g in range(G):
        for r in (g, g + 2):
            t[r, C_SEL + g] = 1
            for i in range(4):
                t[32 * i + r, C_SELG + g * P:C_SELG + (g + 1) * P] = 1
    for j in range(12):
        t[j, C_SELB + 4 * j:C_SELB + 4 * j + 2] = 1
    for e in range(NE):
        t[:, C_TRI + e * NE:C_TRI + e * NE + e] = 1
    return t


def trunk_kernel(nc, T, OUT):
    with ExitStack() as ctx:
        top = [-(-nc.sbuf_base // 32) * 32]

        def place(name, shape, dt=F32, at=None):
            size = 4 * int(np.prod(shape[1:]))
            off = top[0] if at is None else at
            if at is None:
                top[0] += -(-size // 32) * 32
            return nc.alloc_sbuf_tensor_at(name, shape, dt, offset=off)

        tab = place("tab", [P, C_N])
        colp = place("colp", [P, L, 98])
        sil = place("sil", [P, 2, 16])
        ada_hl = place("ada_hl", [P, 4 * KT + P], F32R)
        ada_h0 = place("ada_h0", [P, 4 * KT + P], F32R)
        gains = place("gains", [P, 1600])
        modcol = place("modcol", [P, 6, KT, G])
        scol = place("scol", [P, 2, KT, G])
        grow = place("grow", [P, 512])
        stat = place("stat", [P, 256])
        x = place("x", [P, G, D])
        hT_hi = place("hT_hi", [P, KT, G, P], F32R)
        hT_lo = place("hT_lo", [P, KT, G, P], F32R)
        raw_at = top[0]
        raw = place("raw", [P, RAW, TW])
        lo = place("lo", [P, RAW, TW], F32R, at=raw_at)
        hi = place("hi", [P, HI, TW], F32R)
        region = top[0]

        gates_at = top[0]
        gates = place("gates", [P, G, 4 * D])
        proj_at = top[0]
        proj = place("proj", [P, G, CGATE])
        rowp = place("rowp", [P, L, P], at=proj_at)
        brT_hi = place("brT_hi", [P, 4, G, P], F32R)
        brT_lo = place("brT_lo", [P, 4, G, P], F32R)
        u_at = top[0]
        tmp1 = place("tmp1", [P, 1024])
        tmp2 = place("tmp2", [P, 1024])
        prob = place("prob", [P, 2048], at=u_at)
        modrow = place("modrow", [P, 512], at=u_at)
        adab = place("adab", [12, 512], at=u_at + 2048)
        q_at = top[0]
        qT = place("qT", [P, 4, P])
        kT = place("kT", [P, 4, 2, P])
        wT = place("wT", [P, 4, 2, P])
        o_sb = place("o_sb", [P, 512])
        kc_at = top[0]
        k_c = place("k_c", [P, 512])
        v_c = place("v_c", [P, 512])
        top[0] = kc_at + 4608
        qk96 = place("qk96", [P, 12, BQK], at=kc_at)
        v_b = place("v_b", [P, 2, BH, BV])
        uq_w = place("uq_w", [P, 2, BH * BQK])
        ukv_w = place("ukv_w", [P, 512])
        dg_w = place("dg_w", [P, 2, DG])
        ckv_c = place("ckv_c", [P, BKVL])
        kpe_c = place("kpe_c", [P, BROPE])
        glu_p = place("glu_p", [P, 2, G, P + 2 * PAD], at=q_at)
        conv = place("conv", [P, 2, G, P], at=q_at + 4 * 2 * G * (P + 2 * PAD))
        lnz = place("lnz", [P, G, CCH], at=q_at + 8192)
        pdT = place("pdT", [P, G, 2, P], at=kc_at)
        hdT = place("hdT", [P, 2, G, P], at=kc_at + 2048)
        end_mix = top[0]

        top[0] = region
        xn = place("xn", [P, G, D])
        top[0] = region
        hidT_hi = place("hidT_hi", [P, ED // P, G, P], F32R)
        hidT_lo = place("hidT_lo", [P, ED // P, G, P], F32R)
        hfT = place("hfT", [P, G, KT, P])
        yacc = place("yacc", [P, G, D])
        silu_s = place("silu_s", [P, G, 512])
        hid = place("hid", [P, G, 512])
        router = place("router", [P, KT, NE])
        rtmp = place("rtmp", [P, G, 256])
        comb = place("comb", [P, G, NE])
        gbc = place("gbc", [P, G, D])
        assert max(top[0], end_mix) <= nc.sbuf_usable_end, (top[0], end_mix, nc.sbuf_usable_end)

        B = ctx.enter_context(nc.psum_tensor("B", [P, 4, 512], F32))
        X = ctx.enter_context(nc.psum_tensor("X", [P, 4, 512], F32))

        ident = tab[:, C_ID:C_ID + P]
        mg = [proj[:, g, 0:D] for g in range(G)]
        GAIN = {}
        at = 0
        for name, n in (("qk", 128), ("lam", 256), ("sub", 128), ("bql", 256), ("bkvl", 128),
                        ("bqk", 192), ("lng", 256), ("lnb", 256)):
            GAIN[name] = gains[:, at:at + n]
            at += n
        ssq = stat[:, 0:2]
        rstd = stat[:, 2:4]
        neg_half = stat[:, 4:20]
        nst16 = stat[:, 20:36]
        rst16 = stat[:, 36:52]
        mx = stat[:, 52:60]
        nmx = stat[:, 60:68]
        rsum = stat[:, 68:76]
        rinv = stat[:, 76:84]
        lam2 = stat[:, 84:86]
        lamx = stat[:, 86:88]
        neglam = stat[:, 88:89]
        zsum = stat[:, 92:94]
        bnst = stat[:, 96:108]
        mv = stat[:, 108:112]
        rln = stat[:, 112:114]

        S = {}
        for name in (
            "tab_in rows_in x_in router_in prm_in0 prm_in1 adab_in0 adab_in1 kv_in0 kv_in1 bw_in0 bw_in1 kv_stored ckv_stored y_stored "
            "raw_in0 raw_in1 raw_in2 raw_in3 raw_in4 raw_in5 hi_ready lo_ready tile_used "
            "act_order dve_order pool_order "
            "cols_psum cols_sb sil_th sil_sb ada_st ada_row ada_grow ada_cols mod_ready "
            "sumsq rstd_ready xn_ready xn_T hf_ready hT_hi_ready hT_lo_ready half_set "
            "proj_evac "
            "a_sq a_nst a_rstd a_qk a_roped a_T a_T_sb a_scores a_nmx a_exp a_w a_wT a_wT_sb a_o a_osq a_ost "
            "a_orstd a_on a_oT lam_p lam_e lam_ready "
            "b_zsq b_zrstd b_z b_zT b_zT_sb b_up b_up_sb b_kpe b_sq b_nst b_rstd b_qk b_T b_T_sb b_scores b_nmx "
            "b_exp b_p b_pT b_pT_sb b_o b_o_sb b_oT "
            "c_th c_glu c_T c_T_sb c_conv c_back c_mv c_rstd c_z c_zth c_act c_zT glu_zero "
            "d_pd d_pd_sb d_hd d_hd_sb "
            "br_hi br_lo br_used mg_ready mg_T gb_psum gb_sb x_ready "
            "silu_ready hid_ready hid_T hid_hi hid_lo dn_used r_psum r_sb r_diff r_exp comb_ready"
        ).split():
            S[name] = ctx.enter_context(nc.semaphore(name))
        RAW_IN = [S[f"raw_in{s}"] for s in range(RAW)]
        block = ctx.enter_context(nc.Block())

        def w_tile(w, k0, nk, c0, width):
            return w[k0 * P:(k0 + nk) * P, c0:c0 + width].rearrange("(k p) n -> p k n", p=P)

        def layer_tiles(l):
            for c in range(12):
                for half in range(2):
                    yield w_tile(T["ada_w"][l], 4 * half, 4, 512 * c, 512)
            for c0, width in CHUNKS:
                for half in range(2):
                    yield w_tile(T["w_in"][l], 4 * half, 4, c0, width)
            for b, w in enumerate(("a_w_o", "b_w_o", "c_w_o", "d_w_o")):
                for i in range(N_BR[b]):
                    yield w_tile(T[w][l], 2 * i, 2, 0, D)
            for i in range(N_OUT):
                yield w_tile(T["w_out"][l], 2 * i, 2, 0, D)

        def ffn_tiles():
            for c0, width in FCH:
                for w in ("ffn_w1", "ffn_w3"):
                    nk = TW // width
                    for i in range(KT // nk):
                        yield w_tile(T[w][0], nk * i, nk, c0, width)
            for i in range(N_FFN_DN):
                yield w_tile(T["ffn_w2"][0], 2 * i, 2, 0, D)

        def tile_view(buf, slot, ap):
            _, nk, width = ap.shape
            return buf[:, slot, 0:nk * width].rearrange("p (k n) -> p k n", n=width)

        @block.sync
        def _(sp):
            t = 0

            def load(ap, t, e=None):
                s = t % RAW
                if e is None:
                    if t >= RAW:
                        sp.wait_ge(S["tile_used"], t - RAW + 1)
                else:
                    sp.wait_ge(S["tile_used"], e * N_EXP + (t - RAW + 1))
                sp.dma_start(tile_view(raw, s, ap), ap).then_inc(RAW_IN[s], 16)

            for l in range(L):
                for ap in layer_tiles(l):
                    load(ap, t)
                    t += 1
                if l == 0:
                    for ap in ffn_tiles():
                        load(ap, t)
                        t += 1
            w1 = T["moe_w1"].rearrange("a e k n -> (a e k) n")
            w3 = T["moe_w3"].rearrange("a e k n -> (a e k) n")
            w2 = T["moe_w2"].rearrange("a e k n -> (a e k) n")
            with sp.Fori(0, NE) as e:
                tt = t
                for c0, width in ECH:
                    for w in (w1, w3):
                        for half in range(2):
                            rows = w[bass.ds(e * D + half * 512, 512), c0:c0 + width]
                            load(rows.rearrange("(k p) n -> p k n", p=P), tt, e)
                            tt += 1
                for i in range(N_EXP_DN):
                    rows = w2[bass.ds(e * ED + i * 256, 256), :]
                    load(rows.rearrange("(k p) n -> p k n", p=P), tt, e)
                    tt += 1

        @block.gpsimd
        def _(pool):
            order = [0]

            def chain(ins):
                order[0] += 1
                ins.then_inc(S["pool_order"], 1)
                pool.wait_ge(S["pool_order"], order[0])

            def row(ap):
                return ap.partition_broadcast(P)

            pool.dma_start(tab[:], T["tables"]).then_inc(S["tab_in"], 16)
            for l in range(L):
                items = [(0, 8, T["c_ctx"].rearrange("(r p) -> r p", p=P)),
                         (8, 8, T["c"][0].rearrange("(r p) -> r p", p=P)),
                         (16, 8, T["norm1_g"][l].rearrange("(r p) -> r p", p=P)),
                         (24, 8, T["norm2_g"][l].rearrange("(r p) -> r p", p=P)),
                         (32, 2, T["c_dw_b"][l].rearrange("(r p) -> r p", p=P)),
                         (34, 2, T["d_scale"][l].rearrange("(r p) -> r p", p=P)),
                         (36, 62, T["c_dw"][l].rearrange("k (r p) -> (k r) p", p=P))]
                for r0, n, ap in items:
                    pool.dma_start(rowp[r0:r0 + n, l, :], ap).then_inc(S["rows_in"], 16)
            pool.dma_start(x[:, 0, :], T["x_prompt"][0]).then_inc(S["x_in"], 16)
            pool.dma_start(x[:, 1, :], T["x_sample"][0]).then_inc(S["x_in"], 16)
            pool.memset(neg_half, -0.5).then_inc(S["half_set"], 1)
            pool.wait_ge(S["half_set"], 1)

            def load_layer(l):
                at = 0
                for name, n in (("a_q_norm", 64), ("a_k_norm", 64), ("a_lambda", 256), ("a_sub_norm", 128),
                                ("b_q_lora_norm", 256), ("b_kv_lora_norm", 128), ("b_q_norm", 96),
                                ("b_k_norm", 96), ("c_ln_g", 256), ("c_ln_b", 256)):
                    src = T[name][l]
                    if len(src.shape) == 2:
                        src = src.rearrange("a n -> (a n)")
                    pool.dma_start(gains[:, at:at + n], row(src)).then_inc(S[f"prm_in{l}"], 16)
                    at += n
                pool.dma_start(adab[:, :], T["ada_b"][l].rearrange("(r n) -> r n", n=512)).then_inc(
                    S[f"adab_in{l}"], 16)

            def load_b_weights(l):
                pool.dma_start(uq_w[:], T["b_w_uq"][l].rearrange("(k p) n -> p k n", p=P)).then_inc(S[f"bw_in{l}"], 16)
                pool.dma_start(ukv_w[:], T["b_w_ukv"][l]).then_inc(S[f"bw_in{l}"], 16)
                for i in range(4):
                    pool.dma_start(dg_w[64 * (i % 2):64 * (i % 2) + 64, i // 2, :],
                                   T["d_w_group"][l, i]).then_inc(S[f"bw_in{l}"], 16)
                pool.dma_start(ckv_c[:], T["cache_b_ckv"][0, l]).then_inc(S[f"bw_in{l}"], 16)
                pool.dma_start(kpe_c[:], T["cache_b_kpe"][0, l]).then_inc(S[f"bw_in{l}"], 16)
                pool.dma_start(k_c[:], T["cache_a_k"][0, l].rearrange("t h d -> t (h d)")).then_inc(S[f"kv_in{l}"], 16)
                pool.dma_start(v_c[:], T["cache_a_v"][0, l].rearrange("t h d -> t (h d)")).then_inc(S[f"kv_in{l}"], 16)

            def power(out, in_, width, inv_n):
                chain(pool.tensor_scalar(out, in_, inv_n, EPS, ALU.mult, ALU.add))
                return pool.tensor_tensor(out, out, neg_half[:, 0:width], ALU.pow)

            def norm(i):
                g = i % G
                pool.wait_ge(S["sumsq"], i + 1)
                power(rstd[:, g:g + 1], ssq[:, g:g + 1], 1, 1.0 / D).then_inc(S["rstd_ready"], 1)

            for l in range(L):
                if l:
                    pool.wait_ge(S["x_ready"], 4)
                load_layer(l)
                for g in range(G):
                    norm(4 * l + g)
                if True:
                    pool.wait_ge(S["hT_lo_ready"], 4 * l + 2)
                load_b_weights(l)
                for g in range(G):
                    u = l * G + g
                    pool.wait_ge(S["a_nst"], u + 1)
                    power(rst16, nst16, 16, 1.0 / AQK).then_inc(S["a_rstd"], 1)
                    if g == 0:
                        pool.wait_ge(S["proj_evac"], 28 * l + 6)
                        pool.dma_start(OUT["av"][0, l].rearrange("t h d -> t (h d)"),
                                       proj[:, 0, CV:CV + 512]).then_inc(S["kv_stored"], 16)
                        pool.wait_ge(S["a_qk"], u + 1)
                        pool.dma_start(OUT["ak"][0, l].rearrange("t h d -> t (h d)"),
                                       proj[:, 0, CK:CK + 512]).then_inc(S["kv_stored"], 16)
                    pool.wait_ge(S["a_ost"], u + 1)
                    power(rst16[:, 0:4], nst16[:, 0:4], 4, 1.0 / AV).then_inc(S["a_orstd"], 1)
                for g in range(G):
                    u = l * G + g
                    pool.wait_ge(S["b_zsq"], 2 * u + 2)
                    chain(pool.tensor_scalar(zsum[:, 0:1], zsum[:, 0:1], float(BKVL) / BQL, None, ALU.mult))
                    power(zsum, zsum, 2, 1.0 / BKVL).then_inc(S["b_zrstd"], 1)
                    if g == 0:
                        pool.wait_ge(S["proj_evac"], 28 * l + 8)
                        pool.dma_start(OUT["kpe"][0, l], proj[:, 0, CPE:CPE + BROPE]).then_inc(S["ckv_stored"], 16)
                        pool.wait_ge(S["b_z"], u + 1)
                        pool.dma_start(OUT["ckv"][0, l], proj[:, 0, CKV:CKV + BKVL]).then_inc(S["ckv_stored"], 16)
                    nh = 8 if g == 0 else 12
                    pool.wait_ge(S["b_nst"], u + 1)
                    power(rst16[:, 0:nh], nst16[:, 0:nh], nh, 1.0 / BQK).then_inc(S["b_rstd"], 1)
                pool.wait_ge(S["c_mv"], l + 1)
                for g in range(G):
                    ins = power(rln[:, g:g + 1], mv[:, 2 * g + 1:2 * g + 2], 1, 1.0)
                    if g == G - 1:
                        ins.then_inc(S["c_rstd"], 1)
                    else:
                        chain(ins)
                pool.wait_ge(S["ckv_stored"], 32 * (l + 1))
                for g in range(G):
                    norm(4 * l + 2 + g)
                if l == 1:
                    pool.dma_start(router[:], T["moe_router"][0].rearrange("(k p) e -> p k e", p=P)).then_inc(
                        S["router_in"], 16)
            pool.wait_ge(S["x_ready"], 8)
            pool.dma_start(OUT["y_prompt"][0], x[:, 0, :]).then_inc(S["y_stored"], 16)
            pool.dma_start(OUT["y_sample"][0], x[:, 1, :]).then_inc(S["y_stored"], 16)
            pool.wait_ge(S["kv_stored"], 32 * L)
            pool.wait_ge(S["ckv_stored"], 32 * L)
            pool.wait_ge(S["y_stored"], 32)

        @block.scalar
        def _(act):
            split_next = [0]
            order = [0]

            def chain(ins):
                order[0] += 1
                ins.then_inc(S["act_order"], 1)
                act.wait_ge(S["act_order"], order[0])

            def split_hi(t, e=None):
                s, h = t % RAW, t % HI
                if e is None:
                    act.wait_ge(RAW_IN[s], 16 * (t // RAW + 1))
                    if t >= HI:
                        act.wait_ge(S["tile_used"], t - HI + 1)
                else:
                    act.wait_ge(RAW_IN[s], e * (16 * N_EXP // RAW) + 16 * (t // RAW + 1))
                    act.wait_ge(S["tile_used"], e * N_EXP + (t - HI + 1))
                n = tile_floats(t)
                act.copy(hi[:, h, 0:n], raw[:, s, 0:n]).then_inc(S["hi_ready"], 1)

            def split_to(t):
                while split_next[0] < t:
                    split_hi(split_next[0])
                    split_next[0] += 1

            def norm_sums(i):
                g = i % G
                if i % 4 >= 2:
                    act.wait_ge(S["x_ready"], 4 * (i // 4) + 1 + g)
                elif i < 4:
                    act.wait_ge(S["x_in"], 32)
                else:
                    act.wait_ge(S["x_ready"], 4 * (i // 4) - 2 + 1 + g)
                act.activation(xn[:, g, :], x[:, g, :], ACT.Square,
                               accum_out=ssq[:, g:g + 1]).then_inc(S["sumsq"], 1)

            def norm_hi(i):
                g = i % G
                act.wait_ge(S["hf_ready"], i + 1)
                act.copy(hT_hi[:, :, g, :], hfT[:, g, :, :]).then_inc(S["hT_hi_ready"], 1)

            for l in range(L):
                t0 = t_layer(l)
                if l == 0:
                    act.wait_ge(S["cols_psum"], 2)
                    act.copy(colp[:, :, :], X[:, 0, 0:196].rearrange("p (l n) -> p l n", l=L)).then_inc(S["cols_sb"], 1)
                    act.wait_ge(S["cols_sb"], 1)
                    act.activation(sil[:, 0, :], colp[:, 0, 0:16], ACT.Tanh, scale=0.5).then_inc(S["sil_th"], 1)
                split_to(t0 + HI)
                for c in range(12):
                    n = 12 * l + c
                    act.wait_ge(S["tile_used"], t0 + 2 * c + 2)
                    v, half = c // 2, c % 2
                    if v in (2, 5):
                        r = 32 * ((v == 5) * 2 + half)
                        act.copy(grow[r:r + 4, :], B[0:4, c % 2, :]).then_inc(S["ada_row"], 1)
                    else:
                        if n:
                            act.wait_ge(S["ada_cols"], n)
                        act.copy(modrow[0:4, :], B[0:4, c % 2, :]).then_inc(S["ada_row"], 1)
                    split_to(min(t0 + 2 * c + 2 + HI + 1, t0 + N_ADA + HI))
                for g in range(G):
                    norm_sums(4 * l + g)
                for g in range(G):
                    norm_hi(4 * l + g)

                def evac_chunk(c):
                    c0, width = CHUNKS[c]
                    act.wait_ge(S["tile_used"], t_in(l) + 2 * c + 2)
                    for g in range(G):
                        bank = B[:, 2 * (c % 2) + g, 0:width]
                        if c < 6:
                            act.copy(proj[:, g, c0:c0 + width], bank).then_inc(S["proj_evac"], 1)
                        else:
                            gc = c0 - CGATE
                            act.activation(gates[:, g, gc:gc + 512], bank, ACT.Tanh,
                                           scale=0.5).then_inc(S["proj_evac"], 1)

                for c in range(6):
                    split_to(t_in(l) + 2 * c + 2 + HI)
                    evac_chunk(c)
                gate = [0]

                def fill(n):
                    for _ in range(n):
                        c = 6 + gate[0]
                        if gate[0] < 8:
                            split_to(t_in(l) + 2 * c + 2 + HI)
                            evac_chunk(c)
                            gate[0] += 1

                for g in range(G):
                    u = l * G + g
                    nk = 1 + g
                    act.activation(tmp1[:], proj[:, g, 0:1024], ACT.Square).then_inc(S["a_sq"], 1)
                    if g == 0:
                        act.wait_ge(S["lam_p"], l + 1)
                        act.activation(lamx, lam2, ACT.Exp).then_inc(S["lam_e"], 1)
                    fill(1)
                    act.wait_ge(S["a_T"], u + 1)
                    chain(act.copy(qT[:], X[:, 0, :].rearrange("p (h t) -> p h t", h=4)))
                    for j in range(nk):
                        ins = act.copy(kT[:, :, j, :], X[:, 1 + j, :].rearrange("p (h t) -> p h t", h=4))
                        if j == nk - 1:
                            ins.then_inc(S["a_T_sb"], 1)
                        else:
                            chain(ins)
                    fill(1)
                    act.wait_ge(S["a_nmx"], u + 1)
                    Xs = X[:, :, :].rearrange("p b (h k) -> p (b h) k", k=256)
                    pv = prob[:].rearrange("p (h k) -> p h k", k=256)
                    for h in range(8):
                        ins = act.activation(pv[:, h, 0:nk * P], Xs[:, h, 0:nk * P], ACT.Exp, bias=nmx[:, h:h + 1],
                                             scale=AQK ** -0.5, accum_out=rsum[:, h:h + 1])
                        if h == 7:
                            ins.then_inc(S["a_exp"], 1)
                        else:
                            chain(ins)
                    fill(1)
                    act.wait_ge(S["a_wT"], u + 1)
                    act.copy(wT[:, :, 0:nk, :],
                             X[:, 0:2, :].rearrange("p b (h j t) -> p (b h) j t", h=2, j=2)[:, :, 0:nk, :]).then_inc(
                        S["a_wT_sb"], 1)
                    fill(1)
                    act.wait_ge(S["a_o"], u + 1)
                    act.activation(tmp1[:, 0:512], X[:, 2, :], ACT.Square).then_inc(S["a_osq"], 1)
                    act.wait_ge(S["a_oT"], u + 1)
                    act.copy(brT_hi[:, :, g, :], X[:, 3, :].rearrange("p (h t) -> p h t", h=4)).then_inc(S["br_hi"], 1)
                split_to(t_branch(l, 0) + HI)
                for g in range(G):
                    u = l * G + g
                    nk = 1 + g
                    chain(act.activation(tmp1[:, 0:BQL], proj[:, g, CBQ:CBQ + BQL], ACT.Square,
                                         accum_out=zsum[:, 0:1]))
                    act.sem_inc(S["b_zsq"], 1)
                    act.activation(tmp1[:, BQL:BQL + BKVL], proj[:, g, CKV:CKV + BKVL], ACT.Square,
                                   accum_out=zsum[:, 1:2]).then_inc(S["b_zsq"], 1)
                    act.wait_ge(S["b_zT"], u + 1)
                    zT = wT[:].rearrange("p a b t -> p (a b) t")[:, 0:4, :]
                    act.copy(zT[:, 0:3 + g, :], X[:, 0, 0:(3 + g) * P].rearrange("p (j t) -> p j t", t=P)).then_inc(
                        S["b_zT_sb"], 1)
                    act.wait_ge(S["b_up"], u + 1)
                    chain(act.copy(qk96[:, 0:4, :], X[:, 1, 0:384].rearrange("p (h d) -> p h d", h=4)))
                    for j in range(nk):
                        kv = X[:, 2 + j, :].rearrange("p (h d) -> p h d", h=4)
                        chain(act.copy(qk96[:, 4 + 4 * j:8 + 4 * j, 0:BNOPE], kv[:, :, 0:BNOPE]))
                        chain(act.copy(v_b[:, j, :, :], kv[:, :, BNOPE:BNOPE + BV]))
                    act.wait_ge(S["b_kpe"], u + 1)
                    nh = 4 + 4 * nk
                    sq = tmp1[:].rearrange("p n -> p n")
                    act.activation(prob[:, 0:nh * BQK], qk96[:, 0:nh, :].rearrange("p h d -> p (h d)"),
                                   ACT.Square).then_inc(S["b_sq"], 1)
                    act.wait_ge(S["b_T"], u + 1)
                    chain(act.copy(qT[0:BQK, :, :], X[0:BQK, 0, :].rearrange("p (h t) -> p h t", h=4)))
                    for j in range(nk):
                        ins = act.copy(kT[0:BQK, :, j, :], X[0:BQK, 1 + j, :].rearrange("p (h t) -> p h t", h=4))
                        if j == nk - 1:
                            ins.then_inc(S["b_T_sb"], 1)
                        else:
                            chain(ins)
                    act.wait_ge(S["b_nmx"], u + 1)
                    Xs = X[:, 0:2, :].rearrange("p b (h k) -> p (b h) k", k=256)
                    pv = prob[:].rearrange("p (h k) -> p h k", k=256)
                    for h in range(BH):
                        ins = act.activation(pv[:, h, 0:nk * P], Xs[:, h, 0:nk * P], ACT.Exp, bias=nmx[:, h:h + 1],
                                             scale=BQK ** -0.5, accum_out=rsum[:, h:h + 1])
                        if h == BH - 1:
                            ins.then_inc(S["b_exp"], 1)
                        else:
                            chain(ins)
                    act.wait_ge(S["b_pT"], u + 1)
                    act.copy(wT[:, :, 0:nk, :],
                             X[:, 2:4, :].rearrange("p b (h j t) -> p (b h) j t", h=2, j=2)[:, :, 0:nk, :]).then_inc(
                        S["b_pT_sb"], 1)
                    act.wait_ge(S["b_o"], u + 1)
                    act.copy(o_sb[:, 0:256], X[:, 0, 0:256]).then_inc(S["b_o_sb"], 1)
                    act.wait_ge(S["b_oT"], u + 1)
                    if g == 0:
                        act.wait_ge(S["tile_used"], t_branch(l, 1))
                    act.copy(brT_hi[:, 0:2, g, :], X[:, 1, 0:256].rearrange("p (h t) -> p h t", h=2)).then_inc(
                        S["br_hi"], 1)
                split_to(t_branch(l, 1) + HI)
                for g in range(G):
                    act.activation(tmp2[:, g * 256:(g + 1) * 256], proj[:, g, CC + CCH:CC + 2 * CCH], ACT.Tanh,
                                   scale=0.5).then_inc(S["c_th"], 1)
                act.wait_ge(S["c_T"], l + 1)
                act.wait_ge(S["glu_zero"], l + 1)
                for g in range(G):
                    act.activation(glu_p[:, :, g, PAD:PAD + P],
                                   X[:, 0, g * 256:(g + 1) * 256].rearrange("p (c t) -> p c t", c=2), ACT.Copy,
                                   scale=0.5).then_inc(S["c_T_sb"], 1)
                act.wait_ge(S["c_z"], l + 1)
                act.activation(tmp2[:, 0:512], lnz[:].rearrange("p g n -> p (g n)"), ACT.Tanh,
                               scale=0.5).then_inc(S["c_zth"], 1)
                act.wait_ge(S["c_zT"], l + 1)
                act.wait_ge(S["tile_used"], t_branch(l, 2))
                for g in range(G):
                    act.activation(brT_hi[:, 0:2, g, :],
                                   X[:, 2 + g, 0:256].rearrange("p (h t) -> p h t", h=2), ACT.Copy,
                                   scale=0.5).then_inc(S["br_hi"], 1)
                split_to(t_branch(l, 2) + HI)
                act.wait_ge(S["d_pd"], l + 1)
                act.copy(pdT[:].rearrange("p g k t -> p (g k t)"), X[:, 3, :]).then_inc(S["d_pd_sb"], 1)
                act.wait_ge(S["d_hd"], l + 1)
                for k in range(2):
                    ins = act.activation(hdT[:, k, :, :],
                                         X[:, 0, :].rearrange("p (g k t) -> p k g t", g=G, k=2)[:, k],
                                         ACT.Copy, scale=colp[:, l, 34 + k:35 + k])
                    ins.then_inc(S["d_hd_sb"], 1)
                act.wait_ge(S["d_hd_sb"], 2 * l + 2)
                act.wait_ge(S["tile_used"], t_branch(l, 3))
                for g in range(G):
                    act.copy(brT_hi[:, 0:2, g, :], hdT[:, :, g, :]).then_inc(S["br_hi"], 1)
                split_to(t_branch(l, 3) + HI)
                for g in range(G):
                    act.wait_ge(S["mg_T"], 2 * l + g + 1)
                    act.activation(hT_hi[:, :, g, :],
                                   X[:, 2 * g:2 * g + 2, :].rearrange("p b (k t) -> p (b k) t", t=P), ACT.Copy,
                                   scale=0.5).then_inc(S["hT_hi_ready"], 1)
                split_to(t_out(l) + N_OUT)

                def gate_rows(which):
                    act.wait_ge(S["gb_psum"], 2 * l + which + 1)
                    for g in range(G):
                        act.copy(gbc[:, g, :], X[:, 2 * g:2 * g + 2, :].rearrange("p b n -> p (b n)")).then_inc(
                            S["gb_sb"], 1)

                gate_rows(0)
                split_to(t_ffn(l))
                for g in range(G):
                    norm_sums(4 * l + 2 + g)
                for g in range(G):
                    norm_hi(4 * l + 2 + g)

                def hid_hi(cnt, j, width):
                    act.wait_ge(S["hid_T"], cnt)
                    nb = width // P
                    for g in range(G):
                        act.copy(hidT_hi[:, 4 * j:4 * j + nb, g, :],
                                 X[:, g, 0:width].rearrange("p (k t) -> p k t", t=P)).then_inc(S["hid_hi"], 1)

                if l == 0:
                    tf = t_ffn(0)
                    split_to(tf + HI)
                    for j, (c0, width) in enumerate(FCH):
                        w1_end = tf + 4 * j + (2 if width == 512 else 1)
                        w3_end = tf + 4 * j + (4 if width == 512 else 2)
                        split_to(w1_end + HI)
                        act.wait_ge(S["tile_used"], w1_end)
                        if j:
                            act.wait_ge(S["hid_ready"], 2 * j)
                        for g in range(G):
                            act.activation(silu_s[:, g, 0:width], B[:, g, 0:width], ACT.Silu).then_inc(
                                S["silu_ready"], 1)
                        split_to(w3_end + HI)
                        hid_hi(j + 1, j, width)
                    split_to(tf + N_FFN)
                    gate_rows(1)
                else:
                    act.wait_ge(S["r_diff"], 2)
                    for g in range(G):
                        act.activation(rtmp[:, g, 80:81], rtmp[:, g, 81:82], ACT.Exp).then_inc(S["r_exp"], 1)
                    t0e = t_ffn(1)
                    nch = len(ECH)
                    with act.Fori(0, NE) as e:
                        nxt = [t0e]

                        def esplit(upto):
                            while nxt[0] < min(upto, t0e + N_EXP):
                                split_hi(nxt[0], e)
                                nxt[0] += 1

                        for j in range(nch):
                            esplit(t0e + 4 * j + 2 + HI)
                            act.wait_ge(S["tile_used"], e * N_EXP + (t0e + 4 * j + 2))
                            act.wait_ge(S["hid_ready"], e * (2 * nch) + 2 * (len(FCH) + j))
                            for g in range(G):
                                act.activation(silu_s[:, g, :], B[:, g, :], ACT.Silu).then_inc(S["silu_ready"], 1)
                            esplit(t0e + 4 * j + 4 + HI)
                            act.wait_ge(S["hid_T"], e * nch + (len(FCH) + j + 1))
                            for g in range(G):
                                act.copy(hidT_hi[:, 4 * j:4 * j + 4, g, :],
                                         X[:, g, :].rearrange("p (k t) -> p k t", t=P)).then_inc(S["hid_hi"], 1)
                        esplit(t0e + N_EXP)
                    gate_rows(1)

        @block.vector
        def _(dve):
            split_next = [0]
            order = [0]

            def chain(ins):
                order[0] += 1
                ins.then_inc(S["dve_order"], 1)
                dve.wait_ge(S["dve_order"], order[0])

            def split_lo(t, e=None):
                s, h = t % RAW, t % HI
                dve.wait_ge(S["hi_ready"], t + 1 if e is None else e * N_EXP + (t + 1))
                n = tile_floats(t)
                dve.tensor_tensor(lo[:, s, 0:n], raw[:, s, 0:n], hi[:, h, 0:n].bitcast(F32), ALU.subtract).then_inc(
                    S["lo_ready"], 1)

            def split_to(t):
                while split_next[0] < t:
                    split_lo(split_next[0])
                    split_next[0] += 1

            def bc(ap, n):
                return ap.unsqueeze(2).broadcast_to([P, ap.shape[1], n])

            def norm_scale(i):
                g = i % G
                dve.wait_ge(S["rstd_ready"], i + 1)
                dve.tensor_scalar(xn[:, g, :], x[:, g, :], rstd[:, g:g + 1], None, ALU.mult).then_inc(S["xn_ready"], 1)

            def norm_modulate(i):
                l, which, g = i // 4, i % 4 // 2, i % G
                dve.wait_ge(S["xn_T"], i + 1)
                dve.wait_ge(S["mod_ready"], l + 1)
                for k in range(KT):
                    ins = dve.tensor_scalar(hfT[:, g, k, :], X[:, 2 * g + k // 4, (k % 4) * P:(k % 4 + 1) * P],
                                            scol[:, which, k, g:g + 1], modcol[:, 3 * which, k, g:g + 1],
                                            ALU.mult, ALU.add)
                ins.then_inc(S["hf_ready"], 1)
                dve.wait_ge(S["hT_hi_ready"], 6 * l + 4 * which + g + 1)
                dve.tensor_tensor(hT_lo[:, :, g, :], hfT[:, g, :, :], hT_hi[:, :, g, :].bitcast(F32),
                                  ALU.subtract).then_inc(S["hT_lo_ready"], 1)

            for l in range(L):
                t0 = t_layer(l)
                if l == 0:
                    dve.memset(ada_hl[:].bitcast(F32), 0.0).then_inc(S["ada_st"], 1)
                    dve.memset(ada_h0[:].bitcast(F32), 0.0).then_inc(S["ada_st"], 1)
                    dve.wait_ge(S["ada_st"], 2)
                    dve.wait_ge(S["sil_th"], 1)
                    chain(dve.scalar_tensor_tensor(sil[:, 1, :], sil[:, 0, :], 1.0, colp[:, 0, 0:16], ALU.add, ALU.mult))
                    chain(dve.tensor_scalar(sil[:, 0, :], sil[:, 1, :], 0.5, None, ALU.mult))
                    src = sil[:, 0, :].rearrange("p (g k) -> p k g", g=G)
                    hl = ada_hl[:, 0:4 * KT].rearrange("p (k v) -> p k v", v=4)
                    h0 = ada_h0[:, 0:4 * KT].rearrange("p (k v) -> p k v", v=4)
                    chain(dve.tensor_copy(hl[:, :, 0:2], src))
                    dve.tensor_copy(h0[:, :, 0:2], src).then_inc(S["ada_st"], 1)
                    dve.tensor_tensor(hl[:, :, 2:4], src, hl[:, :, 0:2].bitcast(F32), ALU.subtract).then_inc(
                        S["ada_st"], 1)
                split_to(t0 + N_ADA)
                dve.wait_ge(S["ada_cols"], 12 * (l + 1))
                chain(dve.tensor_copy(modcol[:].rearrange("p v k g -> p (v k g)"), X[:, 0, 0:96]))
                for which in range(2):
                    gcol = colp[:, l, 16 + 8 * which:24 + 8 * which].unsqueeze(2).broadcast_to([P, KT, G])
                    ins = dve.scalar_tensor_tensor(scol[:, which, :, :], modcol[:, 3 * which + 1, :, :], 1.0, gcol,
                                                   ALU.add, ALU.mult)
                    if which:
                        ins.then_inc(S["mod_ready"], 1)
                    else:
                        chain(ins)
                for g in range(G):
                    norm_scale(4 * l + g)
                split_to(t_in(l) + HI)
                for g in range(G):
                    norm_modulate(4 * l + g)
                lam_init = 0.8 - 0.6 * float(np.exp(-0.3 * l))
                dve.wait_ge(S[f"prm_in{l}"], 160)
                lm = GAIN["lam"].rearrange("p (a b d) -> p a b d", a=2, b=2)
                split_to(t_in(l) + 2 * 6)
                chain(dve.tensor_tensor(tmp2[:, 0:128].rearrange("p (a d) -> p a d", a=2), lm[:, :, 0, :],
                                        lm[:, :, 1, :], ALU.mult))
                dve.tensor_reduce(lam2, tmp2[:, 0:128].rearrange("p (a d) -> p a d", a=2), AX.X, ALU.add).then_inc(
                    S["lam_p"], 1)
                chain(dve.tensor_scalar(GAIN["sub"], GAIN["sub"], 1.0 - lam_init, None, ALU.mult))
                dve.wait_ge(S["lam_e"], l + 1)
                chain(dve.tensor_tensor(neglam, lamx[:, 1:2], lamx[:, 0:1], ALU.subtract))
                dve.tensor_scalar(neglam, neglam, -lam_init, None, ALU.add).then_inc(S["lam_ready"], 1)
                dve.wait_ge(S["lam_ready"], l + 1)

                gate = [0]

                def fill(n):
                    for _ in range(n):
                        if gate[0] < 8:
                            split_to(t_in(l) + 2 * (6 + gate[0]) + 2 + HI)
                            gate[0] += 1

                for g in range(G):
                    u = l * G + g
                    nk = 1 + g
                    fill(1)
                    qk = proj[:, g, 0:1024].rearrange("p (h d) -> p h d", d=AQK)
                    t1 = tmp1[:].rearrange("p (h d) -> p h d", d=AQK)
                    t2 = tmp2[:].rearrange("p (h d) -> p h d", d=AQK)
                    dve.wait_ge(S["a_sq"], u + 1)
                    dve.tensor_reduce(nst16, t1, AX.X, ALU.add).then_inc(S["a_nst"], 1)
                    dve.wait_ge(S["a_rstd"], u + 1)
                    chain(dve.tensor_tensor(t2, qk, bc(rst16, AQK), ALU.mult))
                    gn = GAIN["qk"].rearrange("p (a d) -> p a d", a=2)
                    for a in range(2):
                        ins = dve.tensor_tensor(qk[:, 8 * a:8 * a + 8, :], t2[:, 8 * a:8 * a + 8, :],
                                                gn[:, a:a + 1, :].broadcast_to([P, 8, AQK]), ALU.mult)
                        if a == 0:
                            chain(ins)
                        else:
                            ins.then_inc(S["a_qk"], 1)
                            dve.wait_ge(S["a_qk"], u + 1)
                    if g == 1:
                        cos = tab[:, C_RA:C_RA + AQK].unsqueeze(1).broadcast_to([P, 16, AQK])
                        sin = tab[:, C_RA + AQK:C_RA + 2 * AQK].rearrange("p (f i) -> p f i", i=2)
                        chain(dve.tensor_tensor(t1, qk, cos, ALU.mult))
                        q4 = proj[:, g, 0:1024].rearrange("p (h f i) -> p h f i", f=32, i=2)
                        t4 = tmp2[:].rearrange("p (h f i) -> p h f i", f=32, i=2)
                        for i in range(2):
                            chain(dve.tensor_tensor(t4[:, :, :, i], q4[:, :, :, 1 - i],
                                                    sin[:, :, i].unsqueeze(1).broadcast_to([P, 16, 32]), ALU.mult))
                        dve.tensor_tensor(qk, t1, t2, ALU.add).then_inc(S["a_roped"], 1)
                    fill(1)
                    dve.wait_ge(S["a_scores"], u + 1)
                    Xs = X[:, :, :].rearrange("p b (h k) -> p (b h) k", k=256)
                    chain(dve.tensor_reduce(mx, Xs[:, :, 0:nk * P], AX.X, ALU.max))
                    dve.tensor_scalar(nmx, mx, -(AQK ** -0.5), None, ALU.mult).then_inc(S["a_nmx"], 1)
                    fill(1)
                    dve.wait_ge(S["a_exp"], u + 1)
                    chain(dve.reciprocal(rinv, rsum))
                    chain(dve.tensor_scalar(rinv[:, 4:8], rinv[:, 4:8], neglam, None, ALU.mult))
                    pv = prob[:].rearrange("p (h k) -> p h k", k=256)
                    chain(dve.tensor_tensor(pv[:, :, 0:nk * P], pv[:, :, 0:nk * P], bc(rinv, nk * P), ALU.mult))
                    dve.tensor_tensor(pv[:, 0:4, 0:nk * P], pv[:, 0:4, 0:nk * P], pv[:, 4:8, 0:nk * P],
                                      ALU.add).then_inc(S["a_w"], 1)
                    fill(1)
                    dve.wait_ge(S["a_osq"], u + 1)
                    dve.tensor_reduce(nst16[:, 0:4], tmp1[:, 0:512].rearrange("p (h d) -> p h d", d=AV), AX.X,
                                      ALU.add).then_inc(S["a_ost"], 1)
                    dve.wait_ge(S["a_orstd"], u + 1)
                    ov = o_sb[:].rearrange("p (h d) -> p h d", d=AV)
                    chain(dve.tensor_tensor(ov, X[:, 2, :].rearrange("p (h d) -> p h d", d=AV), bc(rst16[:, 0:4], AV),
                                            ALU.mult))
                    dve.tensor_tensor(ov, ov, GAIN["sub"].unsqueeze(1).broadcast_to([P, 4, AV]), ALU.mult).then_inc(
                        S["a_on"], 1)
                    dve.wait_ge(S["br_hi"], 8 * l + g + 1)
                    dve.tensor_tensor(brT_lo[:, :, g, :], X[:, 3, :].rearrange("p (h t) -> p h t", h=4),
                                      brT_hi[:, :, g, :].bitcast(F32), ALU.subtract).then_inc(S["br_lo"], 1)

                def branch_merge(b):
                    dve.wait_ge(S["tile_used"], t_branch(l, b) + N_BR[b])
                    if b == 0:
                        dve.wait_ge(S["proj_evac"], 28 * (l + 1))
                        dve.wait_ge(S["kv_stored"], 32 * (l + 1))
                    for g in range(G):
                        for half in range(2):
                            gt = gates[:, g, b * D + half * 512:b * D + half * 512 + 512]
                            dst = mg[g][:, half * 512:half * 512 + 512]
                            out = B[:, 2 * g + half, :]
                            if b == 0:
                                chain(dve.scalar_tensor_tensor(dst, gt, 1.0, out, ALU.add, ALU.mult))
                            else:
                                chain(dve.scalar_tensor_tensor(tmp1[:, 0:512], gt, 1.0, out, ALU.add, ALU.mult))
                                chain(dve.tensor_tensor(dst, dst, tmp1[:, 0:512], ALU.add))
                    dve.sem_inc(S["br_used"], 1)

                split_to(t_branch(l, 0) + N_BR[0])
                branch_merge(0)
                for g in range(G):
                    u = l * G + g
                    nk = 1 + g
                    dve.wait_ge(S["b_zrstd"], u + 1)
                    chain(dve.scalar_tensor_tensor(proj[:, g, CBQ:CBQ + BQL], proj[:, g, CBQ:CBQ + BQL], zsum[:, 0:1],
                                                   GAIN["bql"], ALU.mult, ALU.mult))
                    dve.scalar_tensor_tensor(proj[:, g, CKV:CKV + BKVL], proj[:, g, CKV:CKV + BKVL], zsum[:, 1:2],
                                             GAIN["bkvl"], ALU.mult, ALU.mult).then_inc(S["b_z"], 1)
                    dve.wait_ge(S["b_up"], u + 1)
                    if g == 0:
                        dve.wait_ge(S[f"bw_in{l}"], 128)
                    for j in range(nk):
                        kpe = proj[:, g, CPE:CPE + BROPE] if j == 0 else kpe_c[:]
                        ins = dve.tensor_copy(qk96[:, 4 + 4 * j:8 + 4 * j, BNOPE:BQK],
                                              kpe.unsqueeze(1).broadcast_to([P, BH, BROPE]))
                        if j == nk - 1:
                            ins.then_inc(S["b_kpe"], 1)
                        else:
                            chain(ins)
                    nh = 4 + 4 * nk
                    dve.wait_ge(S["b_sq"], u + 1)
                    dve.tensor_reduce(nst16[:, 0:nh], prob[:, 0:nh * BQK].rearrange("p (h d) -> p h d", d=BQK), AX.X,
                                      ALU.add).then_inc(S["b_nst"], 1)
                    dve.wait_ge(S["b_rstd"], u + 1)
                    chain(dve.tensor_tensor(qk96[:, 0:nh, :], qk96[:, 0:nh, :], bc(rst16[:, 0:nh], BQK), ALU.mult))
                    gn = GAIN["bqk"].rearrange("p (a d) -> p a d", a=2)
                    chain(dve.tensor_tensor(qk96[:, 0:4, :], qk96[:, 0:4, :], gn[:, 0:1, :].broadcast_to([P, 4, BQK]),
                                            ALU.mult))
                    ins = dve.tensor_tensor(qk96[:, 4:nh, :], qk96[:, 4:nh, :],
                                            gn[:, 1:2, :].broadcast_to([P, nh - 4, BQK]), ALU.mult)
                    if g == 0:
                        ins.then_inc(S["b_qk"], 1)
                    else:
                        chain(ins)
                        tail = qk96[:, 0:8, BNOPE:BQK]
                        cos = tab[:, C_RB:C_RB + BROPE].unsqueeze(1).broadcast_to([P, 8, BROPE])
                        sin = tab[:, C_RB + BROPE:C_RB + 2 * BROPE].rearrange("p (f i) -> p f i", i=2)
                        tc = prob[:, 1280:1536].rearrange("p (h d) -> p h d", d=BROPE)
                        ts = prob[:, 1536:1792].rearrange("p (h f i) -> p h f i", f=16, i=2)
                        t4 = tail.rearrange("p h (f i) -> p h f i", i=2)
                        chain(dve.tensor_tensor(tc, tail, cos, ALU.mult))
                        for i in range(2):
                            chain(dve.tensor_tensor(ts[:, :, :, i], t4[:, :, :, 1 - i],
                                                    sin[:, :, i].unsqueeze(1).broadcast_to([P, 8, 16]), ALU.mult))
                        dve.tensor_tensor(tail, tc, prob[:, 1536:1792].rearrange("p (h d) -> p h d", d=BROPE),
                                          ALU.add).then_inc(S["b_qk"], 1)
                    dve.wait_ge(S["b_scores"], u + 1)
                    Xs = X[:, 0:2, :].rearrange("p b (h k) -> p (b h) k", k=256)
                    chain(dve.tensor_reduce(mx[:, 0:4], Xs[:, :, 0:nk * P], AX.X, ALU.max))
                    dve.tensor_scalar(nmx[:, 0:4], mx[:, 0:4], -(BQK ** -0.5), None, ALU.mult).then_inc(S["b_nmx"], 1)
                    dve.wait_ge(S["b_exp"], u + 1)
                    chain(dve.reciprocal(rinv[:, 0:4], rsum[:, 0:4]))
                    pv = prob[:].rearrange("p (h k) -> p h k", k=256)
                    dve.tensor_tensor(pv[:, 0:4, 0:nk * P], pv[:, 0:4, 0:nk * P], bc(rinv[:, 0:4], nk * P),
                                      ALU.mult).then_inc(S["b_p"], 1)
                    dve.wait_ge(S["br_hi"], 8 * l + 2 + g + 1)
                    dve.tensor_tensor(brT_lo[:, 0:2, g, :], X[:, 1, 0:256].rearrange("p (h t) -> p h t", h=2),
                                      brT_hi[:, 0:2, g, :].bitcast(F32), ALU.subtract).then_inc(S["br_lo"], 1)
                split_to(t_branch(l, 1) + N_BR[1])
                dve.wait_ge(S["b_oT"], 2 * l + 2)
                dve.memset(glu_p[:], 0.0).then_inc(S["glu_zero"], 1)
                for g in range(G):
                    dve.wait_ge(S["c_th"], 2 * l + g + 1)
                    dve.scalar_tensor_tensor(tmp2[:, g * 256:(g + 1) * 256], tmp2[:, g * 256:(g + 1) * 256], 1.0,
                                             proj[:, g, CC:CC + CCH], ALU.add, ALU.mult).then_inc(S["c_glu"], 1)
                branch_merge(1)
                dve.wait_ge(S["c_T_sb"], 2 * (l + 1))
                for c in range(2):
                    chain(dve.tensor_scalar(conv[:, c, :, :], glu_p[:, c, :, 0:P], colp[:, l, 36 + c:37 + c],
                                            colp[:, l, 32 + c:33 + c], ALU.mult, ALU.add))
                for k in range(1, TAPS):
                    for c in range(2):
                        w = colp[:, l, 36 + 2 * k + c:37 + 2 * k + c]
                        ins = dve.scalar_tensor_tensor(conv[:, c, :, :], glu_p[:, c, :, k:k + P], w, conv[:, c, :, :],
                                                       ALU.mult, ALU.add)
                        if k == TAPS - 1 and c == 1:
                            ins.then_inc(S["c_conv"], 1)
                        else:
                            chain(ins)
                dve.wait_ge(S["c_back"], l + 1)
                for g in range(G):
                    chain(dve.bn_stats(bnst[:, 6 * g:6 * g + 6], X[:, 1, g * 256:(g + 1) * 256]))
                for g in range(G):
                    ins = dve.bn_aggr(mv[:, 2 * g:2 * g + 2], bnst[:, 6 * g:6 * g + 6])
                    if g:
                        ins.then_inc(S["c_mv"], 1)
                        dve.wait_ge(S["c_mv"], l + 1)
                    else:
                        chain(ins)
                dve.wait_ge(S["c_rstd"], l + 1)
                for g in range(G):
                    chain(dve.tensor_scalar(lnz[:, g, :], X[:, 1, g * 256:(g + 1) * 256], mv[:, 2 * g:2 * g + 1],
                                            rln[:, g:g + 1], ALU.subtract, ALU.mult))
                chain(dve.tensor_tensor(lnz[:], lnz[:], GAIN["lng"].unsqueeze(1).broadcast_to([P, G, CCH]), ALU.mult))
                dve.tensor_tensor(lnz[:], lnz[:], GAIN["lnb"].unsqueeze(1).broadcast_to([P, G, CCH]),
                                  ALU.add).then_inc(S["c_z"], 1)
                dve.wait_ge(S["c_zth"], l + 1)
                dve.scalar_tensor_tensor(lnz[:].rearrange("p g n -> p (g n)"), tmp2[:, 0:512], 1.0,
                                         lnz[:].rearrange("p g n -> p (g n)"), ALU.add, ALU.mult).then_inc(
                    S["c_act"], 1)
                for g in range(G):
                    dve.wait_ge(S["br_hi"], 8 * l + 4 + g + 1)
                    dve.scalar_tensor_tensor(brT_lo[:, 0:2, g, :],
                                             X[:, 2 + g, 0:256].rearrange("p (h t) -> p h t", h=2), 0.5,
                                             brT_hi[:, 0:2, g, :].bitcast(F32), ALU.mult, ALU.subtract).then_inc(
                        S["br_lo"], 1)
                split_to(t_branch(l, 2) + N_BR[2])
                branch_merge(2)
                for g in range(G):
                    dve.wait_ge(S["br_hi"], 8 * l + 6 + g + 1)
                    dve.tensor_tensor(brT_lo[:, 0:2, g, :], hdT[:, :, g, :], brT_hi[:, 0:2, g, :].bitcast(F32),
                                      ALU.subtract).then_inc(S["br_lo"], 1)
                split_to(t_branch(l, 3) + N_BR[3])
                branch_merge(3)
                dve.sem_inc(S["mg_ready"], 1)
                for g in range(G):
                    dve.wait_ge(S["hT_hi_ready"], 6 * l + 2 + g + 1)
                    dve.scalar_tensor_tensor(hT_lo[:, :, g, :],
                                             X[:, 2 * g:2 * g + 2, :].rearrange("p b (k t) -> p (b k) t", t=P), 0.5,
                                             hT_hi[:, :, g, :].bitcast(F32), ALU.mult, ALU.subtract).then_inc(
                        S["hT_lo_ready"], 1)
                split_to(t_out(l) + N_OUT)

                def residual(which):
                    for g in range(G):
                        dve.wait_ge(S["gb_sb"], 2 * (2 * l + which) + g + 1)
                        if which == 0:
                            dve.wait_ge(S["tile_used"], t_out(l) + N_OUT)
                        elif l == 0:
                            dve.wait_ge(S["tile_used"], t_ffn(0) + N_FFN)
                        src = B[:, 2 * g:2 * g + 2, :].rearrange("p b n -> p (b n)") if which == 0 or l == 0 \
                            else yacc[:, g, :]
                        chain(dve.tensor_tensor(gbc[:, g, :], gbc[:, g, :], src, ALU.mult))
                        dve.tensor_tensor(x[:, g, :], x[:, g, :], gbc[:, g, :], ALU.add).then_inc(S["x_ready"], 1)
                        dve.wait_ge(S["x_ready"], 4 * l + 2 * which + g + 1)

                residual(0)
                for g in range(G):
                    norm_scale(4 * l + 2 + g)
                split_to(t_ffn(l))
                for g in range(G):
                    norm_modulate(4 * l + 2 + g)

                if l == 0:
                    tf = t_ffn(0)
                    for j, (c0, width) in enumerate(FCH):
                        w3_end = tf + 4 * j + (4 if width == 512 else 2)
                        split_to(w3_end + HI - 1)
                        dve.wait_ge(S["tile_used"], w3_end)
                        for g in range(G):
                            dve.wait_ge(S["silu_ready"], 2 * j + g + 1)
                            dve.tensor_tensor(hid[:, g, 0:width], silu_s[:, g, 0:width], B[:, 2 + g, 0:width],
                                              ALU.mult).then_inc(S["hid_ready"], 1)
                        nb = width // P
                        for g in range(G):
                            dve.wait_ge(S["hid_hi"], 2 * j + g + 1)
                            dve.tensor_tensor(hidT_lo[:, 4 * j:4 * j + nb, g, :],
                                              X[:, g, 0:width].rearrange("p (k t) -> p k t", t=P),
                                              hidT_hi[:, 4 * j:4 * j + nb, g, :].bitcast(F32), ALU.subtract).then_inc(
                                S["hid_lo"], 1)
                    split_to(tf + N_FFN)
                    residual(1)
                else:
                    for g in range(G):
                        dve.wait_ge(S["r_psum"], g + 1)
                        lg = rtmp[:, g, 0:8]
                        chain(dve.tensor_copy(lg, X[:, g, 0:8]))
                        cmp = rtmp[:, g, 128:192].rearrange("p (e j) -> p e j", j=8)
                        cm2 = rtmp[:, g, 192:256].rearrange("p (e j) -> p e j", j=8)
                        lj = lg.unsqueeze(1).broadcast_to([P, 8, 8])
                        le = lg.unsqueeze(2).broadcast_to([P, 8, 8])
                        tri = tab[:, C_TRI:C_TRI + 64].rearrange("p (e j) -> p e j", j=8)
                        chain(dve.tensor_tensor(cmp, lj, le, ALU.is_gt))
                        chain(dve.tensor_tensor(cm2, lj, le, ALU.is_equal))
                        chain(dve.tensor_tensor(cm2, cm2, tri, ALU.mult))
                        chain(dve.tensor_tensor(cmp, cmp, cm2, ALU.add))
                        rank = rtmp[:, g, 8:16]
                        chain(dve.tensor_reduce(rank, cmp, AX.X, ALU.add))
                        first, second = rtmp[:, g, 16:24], rtmp[:, g, 24:32]
                        chain(dve.tensor_scalar(first, rank, 0.0, None, ALU.is_equal))
                        chain(dve.tensor_scalar(second, rank, 1.0, None, ALU.is_equal))
                        chain(dve.tensor_tensor(rtmp[:, g, 32:40], first, lg, ALU.mult))
                        chain(dve.tensor_tensor(rtmp[:, g, 40:48], second, lg, ALU.mult))
                        chain(dve.tensor_tensor(rtmp[:, g, 32:40], rtmp[:, g, 40:48], rtmp[:, g, 32:40], ALU.subtract))
                        dve.tensor_reduce(rtmp[:, g, 81:82], rtmp[:, g, 32:40], AX.X, ALU.add).then_inc(S["r_diff"], 1)
                    for g in range(G):
                        dve.wait_ge(S["r_exp"], g + 1)
                        ex, w1, w2 = rtmp[:, g, 80:81], rtmp[:, g, 82:83], rtmp[:, g, 83:84]
                        chain(dve.tensor_scalar(w1, ex, 1.0, None, ALU.add))
                        chain(dve.reciprocal(w1, w1))
                        chain(dve.tensor_tensor(w2, ex, w1, ALU.mult))
                        first, second = rtmp[:, g, 16:24], rtmp[:, g, 24:32]
                        chain(dve.tensor_scalar(first, first, w1, None, ALU.mult))
                        dve.scalar_tensor_tensor(comb[:, g, :], second, w2, first, ALU.mult, ALU.add).then_inc(
                            S["comb_ready"], 1)
                    chain(dve.memset(yacc[:], 0.0))
                    dve.wait_ge(S["comb_ready"], 2)
                    t0e = t_ffn(1)
                    nch = len(ECH)
                    with dve.Fori(0, NE) as e:
                        nxt = [t0e]

                        def esplit(upto):
                            while nxt[0] < min(upto, t0e + N_EXP):
                                split_lo(nxt[0], e)
                                nxt[0] += 1

                        for j in range(nch):
                            esplit(t0e + 4 * j + 4 + HI - 1)
                            dve.wait_ge(S["tile_used"], e * N_EXP + (t0e + 4 * j + 4))
                            for g in range(G):
                                dve.wait_ge(S["silu_ready"], e * 2 * nch + (2 * (len(FCH) + j) + g + 1))
                                dve.tensor_tensor(hid[:, g, :], silu_s[:, g, :], B[:, 2 + g, :], ALU.mult).then_inc(
                                    S["hid_ready"], 1)
                            for g in range(G):
                                dve.wait_ge(S["hid_hi"], e * 2 * nch + (2 * (len(FCH) + j) + g + 1))
                                dve.tensor_tensor(hidT_lo[:, 4 * j:4 * j + 4, g, :],
                                                  X[:, g, :].rearrange("p (k t) -> p k t", t=P),
                                                  hidT_hi[:, 4 * j:4 * j + 4, g, :].bitcast(F32),
                                                  ALU.subtract).then_inc(S["hid_lo"], 1)
                        esplit(t0e + N_EXP)
                        dve.wait_ge(S["tile_used"], e * N_EXP + (t0e + N_EXP))
                        for g in range(G):
                            dve.scalar_tensor_tensor(yacc[:, g, :], B[:, 2 * g:2 * g + 2, :].rearrange("p b n -> p (b n)"),
                                                     comb[:, g, bass.ds(e, 1)], yacc[:, g, :], ALU.mult,
                                                     ALU.add).then_inc(S["dn_used"], 1)
                        dve.wait_ge(S["dn_used"], e * 2 + 2)
                    residual(1)

        @block.tensor
        def _(pe):
            def tile_done(ins):
                ins.then_inc(S["tile_used"], 1)

            def wait_tile(t, e=None):
                pe.wait_ge(S["lo_ready"], t + 1 if e is None else e * N_EXP + (t + 1))

            def parts(t, nk, width):
                h = hi[:, t % HI, 0:nk * width].rearrange("p (k n) -> p k n", n=width)
                lw = lo[:, t % RAW, 0:nk * width].rearrange("p (k n) -> p k n", n=width)
                return h, lw

            def product(out, s_hi, s_lo, w_hi, w_lo, start, stop):
                pe.matmul(out, s_hi, w_hi, start=start, stop=False)
                pe.matmul(out, s_hi, w_lo, start=False, stop=False)
                return pe.matmul(out, s_lo, w_hi, start=False, stop=stop)

            def rows_tile(t, a_hi, a_lo, banks, k0, first, last, e=None, width=512, nk=4, k_all=KT):
                wait_tile(t, e)
                wh, wl = parts(t, nk, width)
                for g in range(G):
                    for k in range(nk):
                        ins = product(banks[g][:, 0:width], a_hi[:, k0 + k, g, :], a_lo[:, k0 + k, g, :], wh[:, k, :],
                                      wl[:, k, :], first and k == 0, last and k == nk - 1)
                tile_done(ins)
                return ins

            def full_tile(t, a_hi, a_lo, k0, first, last, e=None):
                wait_tile(t, e)
                wh, wl = parts(t, 2, D)
                for g in range(G):
                    for half in range(2):
                        for k in range(2):
                            cs = slice(512 * half, 512 * half + 512)
                            ins = product(B[:, 2 * g + half, :], a_hi[:, k0 + k, g, :], a_lo[:, k0 + k, g, :],
                                          wh[:, k, cs], wl[:, k, cs], first and k == 0, last and k == 1)
                tile_done(ins)

            def norm_T(i):
                g = i % G
                pe.wait_ge(S["xn_ready"], i + 1)
                for k in range(KT):
                    ins = pe.transpose(X[:, 2 * g + k // 4, (k % 4) * P:(k % 4 + 1) * P], xn[:, g, k * P:(k + 1) * P],
                                       ident)
                ins.then_inc(S["xn_T"], 1)

            for l in range(L):
                t0 = t_layer(l)
                if l == 0:
                    pe.wait_ge(S["tab_in"], 16)
                    pe.wait_ge(S["rows_in"], 14 * 16)
                    for j in range(L):
                        pe.transpose(X[:, 0, 98 * j:98 * j + 98], rowp[0:98, j, :], ident[0:98, 0:98]).then_inc(
                            S["cols_psum"], 1)
                    pe.wait_ge(S["ada_st"], 4)
                pe.wait_ge(S[f"adab_in{l}"], 16)
                if l == 0:
                    pe.wait_ge(S["cols_sb"], 1)

                def mod_cols(c):
                    v, half = c // 2, c % 2
                    pe.wait_ge(S["ada_row"], 12 * l + c + 1)
                    if v in (2, 5):
                        pe.sem_inc(S["ada_cols"], 1)
                        return
                    for q in range(4):
                        n = (v * KT + half * 4 + q) * G
                        ins = pe.matmul(X[:, 0, n:n + 2], modrow[0:4, q * P:(q + 1) * P], tab[0:4, C_SEL:C_SEL + 2],
                                        start=True, stop=True)
                    ins.then_inc(S["ada_cols"], 1)

                if l == 1:
                    pe.wait_ge(S["x_ready"], 4)
                for c in range(12):
                    bank = B[:, c % 2, :]
                    if c >= 2:
                        pe.wait_ge(S["ada_row"], 12 * l + c - 1)
                    pe.matmul(bank, tab[0:12, C_SELB + 4 * c:C_SELB + 4 * c + P],
                              adab[:, :], start=True, stop=False)
                    for half in range(2):
                        t = t0 + 2 * c + half
                        wait_tile(t)
                        wh, wl = parts(t, 4, 512)
                        for k in range(4):
                            kk = 4 * (4 * half + k)
                            pe.matmul(bank, ada_hl[:, kk:kk + P], wh[:, k, :], start=False, stop=False)
                            ins = pe.matmul(bank, ada_h0[:, kk:kk + P], wl[:, k, :], start=False,
                                            stop=(half == 1 and k == 3))
                        tile_done(ins)
                    if c >= 1:
                        mod_cols(c - 1)
                mod_cols(11)
                pe.wait_ge(S["mod_ready"], l + 1)
                for g in range(G):
                    norm_T(4 * l + g)
                pe.wait_ge(S["hT_lo_ready"], 6 * l + 2)

                def chunk(c):
                    c0, width = CHUNKS[c]
                    banks = [B[:, 2 * (c % 2) + g, :] for g in range(G)]
                    n = 14 * l + c
                    if c >= 2:
                        pe.wait_ge(S["proj_evac"], 2 * (n - 1))
                    for half in range(2):
                        rows_tile(t_in(l) + 2 * c + half, hT_hi, hT_lo, banks, 4 * half, half == 0, half == 1,
                                  width=width)

                for c in range(6):
                    chunk(c)
                gate = [0]

                def fill(n):
                    for _ in range(n):
                        if gate[0] < 8:
                            chunk(6 + gate[0])
                            gate[0] += 1

                def branch_product(b):
                    pe.wait_ge(S["br_lo"], 8 * l + 2 * b + 2)
                    if b == 0:
                        pe.wait_ge(S["proj_evac"], 28 * (l + 1))
                    else:
                        pe.wait_ge(S["br_used"], 4 * l + b)
                    for i in range(N_BR[b]):
                        full_tile(t_branch(l, b) + i, brT_hi, brT_lo, 2 * i, i == 0, i == N_BR[b] - 1)

                for g in range(G):
                    u = l * G + g
                    nk = 1 + g
                    fill(1)
                    pe.wait_ge(S["a_qk"], u + 1)
                    if g == 1:
                        pe.wait_ge(S["a_roped"], l + 1)
                        pe.wait_ge(S[f"kv_in{l}"], 32)
                        pe.wait_ge(S["br_lo"], 8 * l + 1)
                    for j in range(2 + g):
                        for hp in range(4):
                            src = proj[:, g, 512 * j + hp * P:512 * j + (hp + 1) * P] if j < 2 \
                                else k_c[:, hp * P:(hp + 1) * P]
                            ins = pe.transpose(X[:, j, hp * P:(hp + 1) * P], src, ident)
                    ins.then_inc(S["a_T"], 1)
                    fill(1)
                    pe.wait_ge(S["a_T_sb"], u + 1)
                    for h in range(8):
                        hp, i = h // 2, h % 2
                        r = slice(64 * i, 64 * i + 64)
                        ins = pe.matmul(X[:, 2 * i + hp // 2, (hp % 2) * 256:(hp % 2) * 256 + nk * P], qT[r, hp, :],
                                        kT[r, hp, 0:nk, :].rearrange("p j t -> p (j t)"), start=True, stop=True)
                    ins.then_inc(S["a_scores"], 1)
                    fill(1)
                    pe.wait_ge(S["a_w"], u + 1)
                    for h in range(4):
                        for j in range(nk):
                            at = ((h % 2) * 2 + j) * P
                            ins = pe.transpose(X[:, h // 2, at:at + P], prob[:, h * 256 + j * P:h * 256 + (j + 1) * P],
                                               ident)
                    ins.then_inc(S["a_wT"], 1)
                    fill(1)
                    pe.wait_ge(S["a_wT_sb"], u + 1)
                    for h in range(4):
                        for j in range(nk):
                            v = proj[:, g, CV + h * AV:CV + (h + 1) * AV] if j == 0 else v_c[:, h * AV:(h + 1) * AV]
                            ins = pe.matmul(X[:, 2, h * AV:(h + 1) * AV], wT[:, h, j, :], v, start=(j == 0),
                                            stop=(j == nk - 1))
                    ins.then_inc(S["a_o"], 1)
                    pe.wait_ge(S["a_on"], u + 1)
                    for h in range(4):
                        ins = pe.transpose(X[:, 3, h * P:(h + 1) * P], o_sb[:, h * P:(h + 1) * P], ident)
                    ins.then_inc(S["a_oT"], 1)
                branch_product(0)
                pe.wait_ge(S[f"bw_in{l}"], 128)
                zT = wT[:].rearrange("p a b t -> p (a b) t")
                for g in range(G):
                    u = l * G + g
                    nk = 1 + g
                    pe.wait_ge(S["b_z"], u + 1)
                    srcs = [proj[:, g, CBQ:CBQ + P], proj[:, g, CBQ + P:CBQ + 2 * P], proj[:, g, CKV:CKV + P]]
                    if g == 1:
                        srcs.append(ckv_c[:])
                        pe.wait_ge(S["br_lo"], 8 * l + 3)
                    for j, src in enumerate(srcs):
                        ins = pe.transpose(X[:, 0, j * P:(j + 1) * P], src, ident)
                    ins.then_inc(S["b_zT"], 1)
                    pe.wait_ge(S["b_zT_sb"], u + 1)
                    for k in range(2):
                        pe.matmul(X[:, 1, 0:384], zT[:, k, :], uq_w[:, k, :], start=(k == 0), stop=(k == 1))
                    for j in range(nk):
                        ins = pe.matmul(X[:, 2 + j, :], zT[:, 2 + j, :], ukv_w[:], start=True, stop=True)
                    ins.then_inc(S["b_up"], 1)
                    pe.wait_ge(S["b_qk"], u + 1)
                    for j in range(1 + nk):
                        for h in range(4):
                            ins = pe.transpose(X[0:BQK, j, h * P:(h + 1) * P], qk96[:, 4 * j + h, :], ident)
                    ins.then_inc(S["b_T"], 1)
                    pe.wait_ge(S["b_T_sb"], u + 1)
                    for h in range(4):
                        ins = pe.matmul(X[:, h // 2, (h % 2) * 256:(h % 2) * 256 + nk * P], qT[0:BQK, h, :],
                                        kT[0:BQK, h, 0:nk, :].rearrange("p j t -> p (j t)"), start=True, stop=True)
                    ins.then_inc(S["b_scores"], 1)
                    pe.wait_ge(S["b_p"], u + 1)
                    for h in range(4):
                        for j in range(nk):
                            at = ((h % 2) * 2 + j) * P
                            ins = pe.transpose(X[:, 2 + h // 2, at:at + P],
                                               prob[:, h * 256 + j * P:h * 256 + (j + 1) * P], ident)
                    ins.then_inc(S["b_pT"], 1)
                    pe.wait_ge(S["b_pT_sb"], u + 1)
                    for h in range(4):
                        for j in range(nk):
                            ins = pe.matmul(X[:, 0, h * BV:(h + 1) * BV], wT[:, h, j, :], v_b[:, j, h, :],
                                            start=(j == 0), stop=(j == nk - 1))
                    ins.then_inc(S["b_o"], 1)
                    pe.wait_ge(S["b_o_sb"], u + 1)
                    for h in range(2):
                        ins = pe.transpose(X[:, 1, h * P:(h + 1) * P], o_sb[:, h * P:(h + 1) * P], ident)
                    ins.then_inc(S["b_oT"], 1)
                branch_product(1)
                pe.wait_ge(S["c_glu"], 2 * (l + 1))
                for g in range(G):
                    for c in range(2):
                        at = g * 256 + c * P
                        ins = pe.transpose(X[:, 0, at:at + P], tmp2[:, at:at + P], ident)
                ins.then_inc(S["c_T"], 1)
                pe.wait_ge(S["c_conv"], l + 1)
                for g in range(G):
                    for c in range(2):
                        at = g * 256 + c * P
                        ins = pe.transpose(X[:, 1, at:at + P], conv[:, c, g, :], ident)
                ins.then_inc(S["c_back"], 1)
                pe.wait_ge(S["c_act"], l + 1)
                for g in range(G):
                    for c in range(2):
                        ins = pe.transpose(X[:, 2 + g, c * P:(c + 1) * P], lnz[:, g, c * P:(c + 1) * P], ident)
                ins.then_inc(S["c_zT"], 1)
                branch_product(2)
                for g in range(G):
                    for i in range(4):
                        r = slice(64 * (i % 2), 64 * (i % 2) + 64)
                        at = g * 256 + (i // 2) * P
                        ins = pe.matmul(X[r, 3, at:at + P], proj[:, g, CD + i * DG:CD + (i + 1) * DG],
                                        tab[:, C_POOL + i * P:C_POOL + (i + 1) * P], start=True, stop=True)
                ins.then_inc(S["d_pd"], 1)
                pe.wait_ge(S["d_pd_sb"], l + 1)
                for g in range(G):
                    for i in range(4):
                        r = slice(64 * (i % 2), 64 * (i % 2) + 64)
                        at = g * 256 + (i // 2) * P
                        ins = pe.matmul(X[r, 0, at:at + P], dg_w[r, i // 2, :], pdT[r, g, i // 2, :], start=True,
                                        stop=True)
                ins.then_inc(S["d_hd"], 1)
                branch_product(3)
                pe.wait_ge(S["mg_ready"], l + 1)
                for g in range(G):
                    for k in range(KT):
                        ins = pe.transpose(X[:, 2 * g + k // 4, (k % 4) * P:(k % 4 + 1) * P],
                                           mg[g][:, k * P:(k + 1) * P], ident)
                    ins.then_inc(S["mg_T"], 1)
                pe.wait_ge(S["hT_lo_ready"], 6 * l + 4)
                for i in range(N_OUT):
                    full_tile(t_out(l) + i, hT_hi, hT_lo, 2 * i, i == 0, i == N_OUT - 1)

                def gate_rows(which):
                    for g in range(G):
                        for half in range(2):
                            r = 32 * (2 * which + half)
                            ins = pe.matmul(X[:, 2 * g + half, :], tab[r:r + 4, C_SELG + g * P:C_SELG + (g + 1) * P],
                                            grow[r:r + 4, :], start=True, stop=True)
                    ins.then_inc(S["gb_psum"], 1)

                gate_rows(0)
                pe.wait_ge(S["gb_sb"], 4 * l + 2)
                for g in range(G):
                    norm_T(4 * l + 2 + g)
                pe.wait_ge(S["hT_lo_ready"], 6 * l + 6)

                if l == 0:
                    tf = t_ffn(0)
                    for j, (c0, width) in enumerate(FCH):
                        nk = TW // width
                        n_t = KT // nk
                        for w in range(2):
                            if j:
                                if w == 0:
                                    pe.wait_ge(S["silu_ready"], 2 * j)
                                else:
                                    pe.wait_ge(S["hid_ready"], 2 * j)
                            for i in range(n_t):
                                rows_tile(tf + 4 * j + w * n_t + i, hT_hi, hT_lo, [B[:, 2 * w, :], B[:, 2 * w + 1, :]],
                                          nk * i, i == 0, i == n_t - 1, width=width, nk=nk)
                        pe.wait_ge(S["hid_ready"], 2 * j + 2)
                        if j:
                            pe.wait_ge(S["hid_lo"], 2 * j)
                        for g in range(G):
                            for k in range(width // P):
                                ins = pe.transpose(X[:, g, k * P:(k + 1) * P], hid[:, g, k * P:(k + 1) * P], ident)
                        ins.then_inc(S["hid_T"], 1)
                    pe.wait_ge(S["hid_lo"], 2 * len(FCH))
                    for i in range(N_FFN_DN):
                        full_tile(tf + N_FFN_UP + i, hidT_hi, hidT_lo, 2 * i, i == 0, i == N_FFN_DN - 1)
                    gate_rows(1)
                else:
                    pe.wait_ge(S["router_in"], 16)
                    for g in range(G):
                        for k in range(KT):
                            ins = pe.matmul(X[:, g, 0:8], hfT[:, g, k, :], router[:, k, :], start=(k == 0),
                                            stop=(k == KT - 1))
                        ins.then_inc(S["r_psum"], 1)
                    pe.wait_ge(S["r_diff"], 2)
                    t0e = t_ffn(1)
                    nch, nf = len(ECH), len(FCH)
                    with pe.Fori(0, NE) as e:
                        for j in range(nch):
                            for w in range(2):
                                if w == 0:
                                    pe.wait_ge(S["silu_ready"], e * 2 * nch + 2 * (nf + j))
                                    if j == 0:
                                        pe.wait_ge(S["dn_used"], e * 2)
                                else:
                                    pe.wait_ge(S["hid_ready"], e * 2 * nch + 2 * (nf + j))
                                for i in range(2):
                                    rows_tile(t0e + 4 * j + 2 * w + i, hT_hi, hT_lo,
                                              [B[:, 2 * w, :], B[:, 2 * w + 1, :]], 4 * i, i == 0, i == 1, e=e)
                            pe.wait_ge(S["hid_ready"], e * 2 * nch + 2 * (nf + j + 1))
                            pe.wait_ge(S["hid_lo"], e * 2 * nch + 2 * (nf + j))
                            for g in range(G):
                                for k in range(4):
                                    ins = pe.transpose(X[:, g, k * P:(k + 1) * P], hid[:, g, k * P:(k + 1) * P], ident)
                            ins.then_inc(S["hid_T"], 1)
                        pe.wait_ge(S["hid_lo"], e * 2 * nch + 2 * (nf + nch))
                        for i in range(N_EXP_DN):
                            full_tile(t0e + N_EXP_UP + i, hidT_hi, hidT_lo, 2 * i, i == 0, i == N_EXP_DN - 1, e=e)
                    gate_rows(1)


_INS = ['x_prompt', 'x_sample', 'cache_a_k', 'cache_a_v', 'cache_b_ckv', 'cache_b_kpe', 'c', 'c_ctx', 'ada_w', 'ada_b',
        'norm1_g', 'norm2_g', 'w_in', 'a_q_norm', 'a_k_norm', 'a_lambda', 'a_sub_norm', 'a_w_o', 'b_q_lora_norm',
        'b_kv_lora_norm', 'b_w_uq', 'b_w_ukv', 'b_q_norm', 'b_k_norm', 'b_w_o', 'c_dw', 'c_dw_b', 'c_ln_g', 'c_ln_b',
        'c_w_o', 'd_w_group', 'd_scale', 'd_w_o', 'w_out', 'ffn_w1', 'ffn_w3', 'ffn_w2', 'moe_router', 'moe_w1',
        'moe_w3', 'moe_w2']
_OUTS = [("y_prompt", (1, 128, 1024)), ("y_sample", (1, 128, 1024)), ("ak", (1, 2, 128, 8, 64)),
         ("av", (1, 2, 128, 4, 128)), ("ckv", (1, 2, 128, 128)), ("kpe", (1, 2, 128, 32))]


def kernel(**inputs):
    import concourse.bacc as _bacc
    from concourse.bass_utils import run_bass_kernel_spmd as _run

    nc = _bacc.Bacc("TRN2", target_bir_lowering=False, num_devices=1)
    arrays, args, outs = {}, {}, {}
    for name in _INS:
        a = np.ascontiguousarray(inputs[name])
        arrays[f"in_{name}"] = a
        args[name] = nc.dram_tensor(f"in_{name}", a.shape, F32, kind="ExternalInput").ap()
    arrays["in_tables"] = shape_tables()
    args["tables"] = nc.dram_tensor("in_tables", (P, C_N), F32, kind="ExternalInput").ap()
    for name, shape in _OUTS:
        outs[name] = nc.dram_tensor(f"out_{name}", shape, F32, kind="ExternalOutput").ap()
    trunk_kernel(nc, args, outs)
    r = _run(nc, [arrays], core_ids=[0])
    return tuple(r.results[0][f"out_{name}"] for name, _ in _OUTS)
```

```python
from contextlib import ExitStack

import numpy as np
import concourse.bass as bass
from concourse import mybir

F32 = mybir.dt.float32
F32R = mybir.dt.float32r
ALU = mybir.AluOpType
ACT = mybir.ActivationFunctionType
AX = mybir.AxisListType

P = 128
D = 1024
KT = D // P
L = 2
G = 2
AH, AQK, AV = 4, 64, 128
BH, BNOPE, BROPE, BV = 4, 64, 32, 64
BQK = BNOPE + BROPE
BQL, BKVL = 256, 128
CCH, TAPS = 256, 31
PAD = TAPS // 2
POOLS = (2, 4, 8, 16)
DG, DCH = 64, 256
FFN, NE, ED = 2816, 8, 3584
EPS = 1e-6
GRID_W, THETA = 64, 10000.0

CQ, CK, CV, CBQ, CKV, CPE, CC, CD = 0, 512, 1024, 1536, 1792, 1920, 1952, 2464
CGATE = 2720
IN_CHUNKS = [(0, 512), (512, 512), (1024, 512), (1536, 416), (1952, 512), (2464, 256)]
GATE_CHUNKS = [(CGATE + 512 * c, 512) for c in range(8)]
CHUNKS = IN_CHUNKS + GATE_CHUNKS

RAW, HI = 6, 3
TW = 2048

N_ADA = 24
N_IN = 2 * len(IN_CHUNKS)
N_GATE = 2 * len(GATE_CHUNKS)
N_BR = [2, 1, 1, 1]
N_OUT = 4
N_LAYER = N_ADA + N_IN + N_GATE + sum(N_BR) + N_OUT
FCH = [(512 * j, 512) for j in range(5)] + [(2560, 256)]
N_FFN_UP = 5 * 4 + 2
N_FFN_DN = FFN // 256
N_FFN = N_FFN_UP + N_FFN_DN
ECH = [(512 * j, 512) for j in range(ED // 512)]
JOBS = NE + 3
N_EXP_UP = 4 * len(ECH)
N_EXP_DN = ED // 256
N_EXP = N_EXP_UP + N_EXP_DN


def t_layer(l):
    return l * (N_LAYER + N_FFN)


def t_in(l):
    return t_layer(l) + N_ADA


def t_gate(l):
    return t_in(l) + N_IN


def t_branch(l, b):
    return t_gate(l) + N_GATE + sum(N_BR[:b])


def t_out(l):
    return t_gate(l) + N_GATE + sum(N_BR)


def t_ffn(l):
    return t_layer(l) + N_LAYER


def tile_floats(t):
    for l in range(L):
        if t_in(l) <= t < t_in(l) + N_IN:
            return 4 * IN_CHUNKS[(t - t_in(l)) // 2][1]
    return TW


C_ID, C_POOL, C_RA, C_RB, C_SEL, C_SELG, C_SELB, C_TRI = 0, 128, 640, 768, 832, 834, 1090, 1138
C_N = 1262
C_IOTA, C_BEFORE, C_ALL = C_N, C_N + P, C_N + 2 * P


def shape_tables():
    t = np.zeros((P, C_ALL), np.float32)
    t[:, C_ID:C_ID + P] = np.eye(P, dtype=np.float32)
    for i, w in enumerate(POOLS):
        left, right = w // 2, w - 1 - w // 2
        for q in range(P):
            lo, hi = max(q - left, 0), min(q + right + 1, P)
            t[lo:hi, C_POOL + i * P + q] = np.float32(1) / np.float32(hi - lo)
            t[q, C_POOL + i * P + q] -= np.float32(1)
    for base, dim in ((C_RA, AQK), (C_RB, BROPE)):
        nf = dim // 4
        freqs = np.float32(THETA) ** (-np.arange(nf, dtype=np.float32) / np.float32(nf))
        tok = np.arange(P)
        row, col = (tok // GRID_W).astype(np.float32), (tok % GRID_W).astype(np.float32)
        ang = np.concatenate([row[:, None] * freqs, col[:, None] * freqs], axis=1).astype(np.float32)
        cos, sin = np.cos(ang).astype(np.float32), np.sin(ang).astype(np.float32)
        t[:, base:base + dim] = np.repeat(cos, 2, axis=1)
        t[:, base + dim:base + 2 * dim:2] = -sin
        t[:, base + dim + 1:base + 2 * dim:2] = sin
    for g in range(G):
        for r in (g, g + 2):
            t[r, C_SEL + g] = 1
            for i in range(4):
                t[32 * i + r, C_SELG + g * P:C_SELG + (g + 1) * P] = 1
    for j in range(12):
        t[j, C_SELB + 4 * j:C_SELB + 4 * j + 2] = 1
    for e in range(NE):
        t[:, C_TRI + e * NE:C_TRI + e * NE + e] = 1
    t[:, C_IOTA:C_IOTA + P] = np.arange(P)
    t[:, C_BEFORE:C_BEFORE + P] = np.triu(np.ones((P, P)), 1)
    return t


def trunk_kernel(nc, T, OUT):
    with ExitStack() as ctx:
        top = [-(-nc.sbuf_base // 32) * 32]

        def place(name, shape, dt=F32, at=None):
            size = 4 * int(np.prod(shape[1:]))
            off = top[0] if at is None else at
            if at is None:
                top[0] += -(-size // 32) * 32
            return nc.alloc_sbuf_tensor_at(name, shape, dt, offset=off)

        tab = place("tab", [P, C_N])
        colp = place("colp", [P, L, 98])
        sil = place("sil", [P, 2, 16])
        ada_hl = place("ada_hl", [P, 4 * KT + P], F32R)
        ada_h0 = place("ada_h0", [P, 4 * KT + P], F32R)
        gains = place("gains", [P, 1600])
        modcol = place("modcol", [P, 6, KT, G])
        scol = place("scol", [P, 2, KT, G])
        grow = place("grow", [P, 512])
        stat = place("stat", [P, 256])
        x = place("x", [P, G, D])
        hT_hi = place("hT_hi", [P, KT, G, P], F32R)
        hT_lo = place("hT_lo", [P, KT, G, P], F32R)
        raw_at = top[0]
        raw = place("raw", [P, RAW, TW])
        lo = place("lo", [P, RAW, TW], F32R, at=raw_at)
        hi = place("hi", [P, HI, TW], F32R)
        region = top[0]

        gates_at = top[0]
        gates = place("gates", [P, G, 4 * D])
        proj_at = top[0]
        proj = place("proj", [P, G, CGATE])
        rowp = place("rowp", [P, L, P], at=proj_at)
        brT_hi = place("brT_hi", [P, 4, G, P], F32R)
        brT_lo = place("brT_lo", [P, 4, G, P], F32R)
        u_at = top[0]
        tmp1 = place("tmp1", [P, 1024])
        tmp2 = place("tmp2", [P, 1024])
        prob = place("prob", [P, 2048], at=u_at)
        modrow = place("modrow", [P, 512], at=u_at)
        adab = place("adab", [12, 512], at=u_at + 2048)
        q_at = top[0]
        qT = place("qT", [P, 4, P])
        kT = place("kT", [P, 4, 2, P])
        wT = place("wT", [P, 4, 2, P])
        o_sb = place("o_sb", [P, 512])
        kc_at = top[0]
        k_c = place("k_c", [P, 512])
        v_c = place("v_c", [P, 512])
        top[0] = kc_at + 4608
        qk96 = place("qk96", [P, 12, BQK], at=kc_at)
        v_b = place("v_b", [P, 2, BH, BV])
        uq_w = place("uq_w", [P, 2, BH * BQK])
        ukv_w = place("ukv_w", [P, 512])
        dg_w = place("dg_w", [P, 2, DG])
        ckv_c = place("ckv_c", [P, BKVL])
        kpe_c = place("kpe_c", [P, BROPE])
        glu_p = place("glu_p", [P, 2, G, P + 2 * PAD], at=q_at)
        conv = place("conv", [P, 2, G, P], at=q_at + 4 * 2 * G * (P + 2 * PAD))
        lnz = place("lnz", [P, G, CCH], at=q_at + 8192)
        pdT = place("pdT", [P, G, 2, P], at=kc_at)
        hdT = place("hdT", [P, 2, G, P], at=kc_at + 2048)
        end_mix = top[0]

        top[0] = region
        xn = place("xn", [P, G, D])
        top[0] = region
        hidT_hi = place("hidT_hi", [P, FFN // P, G, P], F32R)
        hidT_lo = place("hidT_lo", [P, FFN // P, G, P], F32R)
        hfT = place("hfT", [P, G, KT, P])
        hfT_at = top[0]
        silu_s = place("silu_s", [P, G, 512])
        hid = place("hid", [P, G, 512])
        gbc = place("gbc", [P, G, D])
        top[0] = region
        hidE_hi = place("hidE_hi", [P, ED // P, P], F32R)
        hidE_lo = place("hidE_lo", [P, ED // P, P], F32R)
        xg_hi = place("xg_hi", [P, KT, P], F32R)
        xg_lo = place("xg_lo", [P, KT, P], F32R)
        pick = place("pick", [P, G, P], F32R)
        pickT = place("pickT", [P, G, P], F32R)
        assert top[0] <= hfT_at
        top[0] = hfT_at + 4 * (2 * G * 512 + G * D)
        silu_e = place("silu_e", [P, 2, 512], at=hfT_at)
        hid_e = place("hid_e", [P, 2, 512], at=hfT_at + 4096)
        yacc = place("yacc", [P, G, D])
        ye_hi = place("ye_hi", [P, D], F32R)
        ye_lo = place("ye_lo", [P, D], F32R)
        etab = place("etab", [P, 2 * P])
        router = place("router", [P, KT, NE])
        rtmp = place("rtmp", [P, G, 320])
        job_pos = place("job_pos", [P, G, JOBS + 1])
        job_comb = place("job_comb", [P, G, JOBS + 1])
        job_int = place("job_int", [P, 4], mybir.dt.int32)
        ones = place("ones", [P, P])
        assert max(top[0], end_mix) <= nc.sbuf_usable_end, (top[0], end_mix, nc.sbuf_usable_end)

        B = ctx.enter_context(nc.psum_tensor("B", [P, 4, 512], F32))
        X = ctx.enter_context(nc.psum_tensor("X", [P, 4, 512], F32))

        ident = tab[:, C_ID:C_ID + P]
        mg = [proj[:, g, 0:D] for g in range(G)]
        GAIN = {}
        at = 0
        for name, n in (("qk", 128), ("lam", 256), ("sub", 128), ("bql", 256), ("bkvl", 128),
                        ("bqk", 192), ("lng", 256), ("lnb", 256)):
            GAIN[name] = gains[:, at:at + n]
            at += n
        ssq = stat[:, 0:2]
        rstd = stat[:, 2:4]
        neg_half = stat[:, 4:20]
        nst16 = stat[:, 20:36]
        rst16 = stat[:, 36:52]
        mx = stat[:, 52:60]
        nmx = stat[:, 60:68]
        rsum = stat[:, 68:76]
        rinv = stat[:, 76:84]
        lam2 = stat[:, 84:86]
        lamx = stat[:, 86:88]
        neglam = stat[:, 88:89]
        zsum = stat[:, 92:94]
        bnst = stat[:, 96:108]
        mv = stat[:, 108:112]
        rln = stat[:, 112:114]

        S = {}
        for name in (
            "tab_in rows_in x_in router_in prm_in0 prm_in1 adab_in0 adab_in1 kv_in0 kv_in1 bw_in0 bw_in1 kv_stored ckv_stored y_stored "
            "raw_in0 raw_in1 raw_in2 raw_in3 raw_in4 raw_in5 hi_ready lo_ready tile_used "
            "act_order dve_order pool_order "
            "cols_psum cols_sb sil_th sil_sb ada_st ada_row ada_grow ada_cols mod_ready "
            "sumsq rstd_ready xn_ready xn_T hf_ready hT_hi_ready hT_lo_ready half_set "
            "proj_evac "
            "a_sq a_nst a_rstd a_qk a_roped a_T a_T_sb a_scores a_nmx a_exp a_w a_wT a_wT_sb a_o a_osq a_ost "
            "a_orstd a_on a_oT lam_p lam_e lam_ready "
            "b_zsq b_zrstd b_z b_zT b_zT_sb b_up b_up_sb b_kpe b_sq b_nst b_rstd b_qk b_T b_T_sb b_scores b_nmx "
            "b_exp b_p b_pT b_pT_sb b_o b_o_sb b_oT "
            "c_th c_glu c_T c_T_sb c_conv c_back c_mv c_rstd c_z c_zth c_act c_zT glu_zero "
            "d_pd d_pd_sb d_hd d_hd_sb "
            "br_hi br_lo br_used mg_ready mg_T gb_psum gb_sb x_ready "
            "silu_ready hid_ready hid_T hid_hi hid_lo r_psum r_diff r_exp r_mask r_pos jobs_ready "
            "h_tok h_tok_hi h_tok_lo pick_ready pickT_psum pickT_sb xg_psum xg_ready e_silu e_hid e_hidT e_hid_hi e_hid_lo ye_hi_ready ye_lo_ready ys_psum ys_used"
        ).split():
            S[name] = ctx.enter_context(nc.semaphore(name))
        RAW_IN = [S[f"raw_in{s}"] for s in range(RAW)]
        block = ctx.enter_context(nc.Block())

        def w_tile(w, k0, nk, c0, width):
            return w[k0 * P:(k0 + nk) * P, c0:c0 + width].rearrange("(k p) n -> p k n", p=P)

        def layer_tiles(l):
            for c in range(12):
                for half in range(2):
                    yield w_tile(T["ada_w"][l], 4 * half, 4, 512 * c, 512)
            for c0, width in CHUNKS:
                for half in range(2):
                    yield w_tile(T["w_in"][l], 4 * half, 4, c0, width)
            for b, w in enumerate(("a_w_o", "b_w_o", "c_w_o", "d_w_o")):
                for i in range(N_BR[b]):
                    yield w_tile(T[w][l], 2 * i, 2, 0, D)
            for i in range(N_OUT):
                yield w_tile(T["w_out"][l], 2 * i, 2, 0, D)

        def ffn_tiles():
            for c0, width in FCH:
                for w in ("ffn_w1", "ffn_w3"):
                    nk = TW // width
                    for i in range(KT // nk):
                        yield w_tile(T[w][0], nk * i, nk, c0, width)
            for i in range(N_FFN_DN):
                yield w_tile(T["ffn_w2"][0], 2 * i, 2, 0, D)

        def tile_view(buf, slot, ap):
            _, nk, width = ap.shape
            return buf[:, slot, 0:nk * width].rearrange("p (k n) -> p k n", n=width)

        @block.sync
        def _(sp):
            t = 0

            def load(ap, t, e=None):
                s = t % RAW
                if e is None:
                    if t >= RAW:
                        sp.wait_ge(S["tile_used"], t - RAW + 1)
                else:
                    sp.wait_ge(S["tile_used"], e * N_EXP + (t - RAW + 1))
                sp.dma_start(tile_view(raw, s, ap), ap).then_inc(RAW_IN[s], 16)

            for l in range(L):
                for ap in layer_tiles(l):
                    load(ap, t)
                    t += 1
                if l == 0:
                    for ap in ffn_tiles():
                        load(ap, t)
                        t += 1
            w1 = T["moe_w1"].rearrange("a e k n -> (a e k) n")
            w3 = T["moe_w3"].rearrange("a e k n -> (a e k) n")
            w2 = T["moe_w2"].rearrange("a e k n -> (a e k) n")

            def load_expert(job, expert):
                tt = t
                for c0, width in ECH:
                    for w in (w1, w3):
                        for half in range(2):
                            rows = w[bass.ds(expert * D + half * 512, 512), c0:c0 + width]
                            load(rows.rearrange("(k p) n -> p k n", p=P), tt, job)
                            tt += 1
                for i in range(N_EXP_DN):
                    rows = w2[bass.ds(expert * ED + i * 256, 256), :]
                    load(rows.rearrange("(k p) n -> p k n", p=P), tt, job)
                    tt += 1

            with sp.Fori(0, NE) as e:
                load_expert(e, e)
            sp.wait_ge(S["jobs_ready"], 1)
            n_jobs = sp.value_load(job_int[0:1, 0:1], min_val=NE, max_val=JOBS)
            for k in range(JOBS - NE):
                with sp.If(n_jobs > NE + k):
                    load_expert(NE + k, sp.value_load(job_int[0:1, 1 + k:2 + k], min_val=0, max_val=NE - 1))

        @block.gpsimd
        def _(pool):
            order = [0]

            def chain(ins):
                order[0] += 1
                ins.then_inc(S["pool_order"], 1)
                pool.wait_ge(S["pool_order"], order[0])

            def row(ap):
                return ap.partition_broadcast(P)

            pool.dma_start(tab[:], T["tables"][:, 0:C_N]).then_inc(S["tab_in"], 16)
            for l in range(L):
                items = [(0, 8, T["c_ctx"].rearrange("(r p) -> r p", p=P)),
                         (8, 8, T["c"][0].rearrange("(r p) -> r p", p=P)),
                         (16, 8, T["norm1_g"][l].rearrange("(r p) -> r p", p=P)),
                         (24, 8, T["norm2_g"][l].rearrange("(r p) -> r p", p=P)),
                         (32, 2, T["c_dw_b"][l].rearrange("(r p) -> r p", p=P)),
                         (34, 2, T["d_scale"][l].rearrange("(r p) -> r p", p=P)),
                         (36, 62, T["c_dw"][l].rearrange("k (r p) -> (k r) p", p=P))]
                for r0, n, ap in items:
                    pool.dma_start(rowp[r0:r0 + n, l, :], ap).then_inc(S["rows_in"], 16)
            pool.dma_start(x[:, 0, :], T["x_prompt"][0]).then_inc(S["x_in"], 16)
            pool.dma_start(x[:, 1, :], T["x_sample"][0]).then_inc(S["x_in"], 16)
            pool.memset(neg_half, -0.5).then_inc(S["half_set"], 1)
            pool.wait_ge(S["half_set"], 1)

            def load_layer(l):
                at = 0
                for name, n in (("a_q_norm", 64), ("a_k_norm", 64), ("a_lambda", 256), ("a_sub_norm", 128),
                                ("b_q_lora_norm", 256), ("b_kv_lora_norm", 128), ("b_q_norm", 96),
                                ("b_k_norm", 96), ("c_ln_g", 256), ("c_ln_b", 256)):
                    src = T[name][l]
                    if len(src.shape) == 2:
                        src = src.rearrange("a n -> (a n)")
                    pool.dma_start(gains[:, at:at + n], row(src)).then_inc(S[f"prm_in{l}"], 16)
                    at += n
                pool.dma_start(adab[:, :], T["ada_b"][l].rearrange("(r n) -> r n", n=512)).then_inc(
                    S[f"adab_in{l}"], 16)

            def load_b_weights(l):
                pool.dma_start(uq_w[:], T["b_w_uq"][l].rearrange("(k p) n -> p k n", p=P)).then_inc(S[f"bw_in{l}"], 16)
                pool.dma_start(ukv_w[:], T["b_w_ukv"][l]).then_inc(S[f"bw_in{l}"], 16)
                for i in range(4):
                    pool.dma_start(dg_w[64 * (i % 2):64 * (i % 2) + 64, i // 2, :],
                                   T["d_w_group"][l, i]).then_inc(S[f"bw_in{l}"], 16)
                pool.dma_start(ckv_c[:], T["cache_b_ckv"][0, l]).then_inc(S[f"bw_in{l}"], 16)
                pool.dma_start(kpe_c[:], T["cache_b_kpe"][0, l]).then_inc(S[f"bw_in{l}"], 16)
                pool.dma_start(k_c[:], T["cache_a_k"][0, l].rearrange("t h d -> t (h d)")).then_inc(S[f"kv_in{l}"], 16)
                pool.dma_start(v_c[:], T["cache_a_v"][0, l].rearrange("t h d -> t (h d)")).then_inc(S[f"kv_in{l}"], 16)

            def power(out, in_, width, inv_n):
                chain(pool.tensor_scalar(out, in_, inv_n, EPS, ALU.mult, ALU.add))
                return pool.tensor_tensor(out, out, neg_half[:, 0:width], ALU.pow)

            def norm(i):
                g = i % G
                pool.wait_ge(S["sumsq"], i + 1)
                power(rstd[:, g:g + 1], ssq[:, g:g + 1], 1, 1.0 / D).then_inc(S["rstd_ready"], 1)

            for l in range(L):
                if l:
                    pool.wait_ge(S["x_ready"], 4)
                load_layer(l)
                for g in range(G):
                    norm(4 * l + g)
                if True:
                    pool.wait_ge(S["hT_lo_ready"], 4 * l + 2)
                load_b_weights(l)
                for g in range(G):
                    u = l * G + g
                    pool.wait_ge(S["a_nst"], u + 1)
                    power(rst16, nst16, 16, 1.0 / AQK).then_inc(S["a_rstd"], 1)
                    if g == 0:
                        pool.wait_ge(S["proj_evac"], 28 * l + 6)
                        pool.dma_start(OUT["av"][0, l].rearrange("t h d -> t (h d)"),
                                       proj[:, 0, CV:CV + 512]).then_inc(S["kv_stored"], 16)
                        pool.wait_ge(S["a_qk"], u + 1)
                        pool.dma_start(OUT["ak"][0, l].rearrange("t h d -> t (h d)"),
                                       proj[:, 0, CK:CK + 512]).then_inc(S["kv_stored"], 16)
                    pool.wait_ge(S["a_ost"], u + 1)
                    power(rst16[:, 0:4], nst16[:, 0:4], 4, 1.0 / AV).then_inc(S["a_orstd"], 1)
                for g in range(G):
                    u = l * G + g
                    pool.wait_ge(S["b_zsq"], 2 * u + 2)
                    chain(pool.tensor_scalar(zsum[:, 0:1], zsum[:, 0:1], float(BKVL) / BQL, None, ALU.mult))
                    power(zsum, zsum, 2, 1.0 / BKVL).then_inc(S["b_zrstd"], 1)
                    if g == 0:
                        pool.wait_ge(S["proj_evac"], 28 * l + 8)
                        pool.dma_start(OUT["kpe"][0, l], proj[:, 0, CPE:CPE + BROPE]).then_inc(S["ckv_stored"], 16)
                        pool.wait_ge(S["b_z"], u + 1)
                        pool.dma_start(OUT["ckv"][0, l], proj[:, 0, CKV:CKV + BKVL]).then_inc(S["ckv_stored"], 16)
                    nh = 8 if g == 0 else 12
                    pool.wait_ge(S["b_nst"], u + 1)
                    power(rst16[:, 0:nh], nst16[:, 0:nh], nh, 1.0 / BQK).then_inc(S["b_rstd"], 1)
                pool.wait_ge(S["c_mv"], l + 1)
                for g in range(G):
                    ins = power(rln[:, g:g + 1], mv[:, 2 * g + 1:2 * g + 2], 1, 1.0)
                    if g == G - 1:
                        ins.then_inc(S["c_rstd"], 1)
                    else:
                        chain(ins)
                pool.wait_ge(S["ckv_stored"], 32 * (l + 1))
                for g in range(G):
                    norm(4 * l + 2 + g)
                if l == 1:
                    pool.dma_start(router[:], T["moe_router"][0].rearrange("(k p) e -> p k e", p=P)).then_inc(
                        S["router_in"], 16)
                    pool.dma_start(etab[:], T["tables"][:, C_IOTA:C_ALL]).then_inc(S["router_in"], 16)
            pool.wait_ge(S["x_ready"], 8)
            pool.dma_start(OUT["y_prompt"][0], x[:, 0, :]).then_inc(S["y_stored"], 16)
            pool.dma_start(OUT["y_sample"][0], x[:, 1, :]).then_inc(S["y_stored"], 16)
            pool.wait_ge(S["kv_stored"], 32 * L)
            pool.wait_ge(S["ckv_stored"], 32 * L)
            pool.wait_ge(S["y_stored"], 32)

        @block.scalar
        def _(act):
            split_next = [0]
            order = [0]

            def chain(ins):
                order[0] += 1
                ins.then_inc(S["act_order"], 1)
                act.wait_ge(S["act_order"], order[0])

            def split_hi(t, e=None):
                s, h = t % RAW, t % HI
                if e is None:
                    act.wait_ge(RAW_IN[s], 16 * (t // RAW + 1))
                    if t >= HI:
                        act.wait_ge(S["tile_used"], t - HI + 1)
                else:
                    act.wait_ge(RAW_IN[s], e * (16 * N_EXP // RAW) + 16 * (t // RAW + 1))
                    act.wait_ge(S["tile_used"], e * N_EXP + (t - HI + 1))
                n = tile_floats(t)
                act.copy(hi[:, h, 0:n], raw[:, s, 0:n]).then_inc(S["hi_ready"], 1)

            def split_to(t):
                while split_next[0] < t:
                    split_hi(split_next[0])
                    split_next[0] += 1

            def norm_sums(i):
                g = i % G
                if i % 4 >= 2:
                    act.wait_ge(S["x_ready"], 4 * (i // 4) + 1 + g)
                elif i < 4:
                    act.wait_ge(S["x_in"], 32)
                else:
                    act.wait_ge(S["x_ready"], 4 * (i // 4) - 2 + 1 + g)
                act.activation(xn[:, g, :], x[:, g, :], ACT.Square,
                               accum_out=ssq[:, g:g + 1]).then_inc(S["sumsq"], 1)

            def norm_hi(i):
                g = i % G
                act.wait_ge(S["hf_ready"], i + 1)
                act.copy(hT_hi[:, :, g, :], hfT[:, g, :, :]).then_inc(S["hT_hi_ready"], 1)

            for l in range(L):
                t0 = t_layer(l)
                if l == 0:
                    act.wait_ge(S["cols_psum"], 2)
                    act.copy(colp[:, :, :], X[:, 0, 0:196].rearrange("p (l n) -> p l n", l=L)).then_inc(S["cols_sb"], 1)
                    act.wait_ge(S["cols_sb"], 1)
                    act.activation(sil[:, 0, :], colp[:, 0, 0:16], ACT.Tanh, scale=0.5).then_inc(S["sil_th"], 1)
                split_to(t0 + HI)
                for c in range(12):
                    n = 12 * l + c
                    act.wait_ge(S["tile_used"], t0 + 2 * c + 2)
                    v, half = c // 2, c % 2
                    if v in (2, 5):
                        r = 32 * ((v == 5) * 2 + half)
                        act.copy(grow[r:r + 4, :], B[0:4, c % 2, :]).then_inc(S["ada_row"], 1)
                    else:
                        if n:
                            act.wait_ge(S["ada_cols"], n)
                        act.copy(modrow[0:4, :], B[0:4, c % 2, :]).then_inc(S["ada_row"], 1)
                    split_to(min(t0 + 2 * c + 2 + HI + 1, t0 + N_ADA + HI))
                for g in range(G):
                    norm_sums(4 * l + g)
                for g in range(G):
                    norm_hi(4 * l + g)

                def evac_chunk(c):
                    c0, width = CHUNKS[c]
                    act.wait_ge(S["tile_used"], t_in(l) + 2 * c + 2)
                    for g in range(G):
                        bank = B[:, 2 * (c % 2) + g, 0:width]
                        if c < 6:
                            act.copy(proj[:, g, c0:c0 + width], bank).then_inc(S["proj_evac"], 1)
                        else:
                            gc = c0 - CGATE
                            act.activation(gates[:, g, gc:gc + 512], bank, ACT.Tanh,
                                           scale=0.5).then_inc(S["proj_evac"], 1)

                for c in range(6):
                    split_to(t_in(l) + 2 * c + 2 + HI)
                    evac_chunk(c)
                gate = [0]

                def fill(n):
                    for _ in range(n):
                        c = 6 + gate[0]
                        if gate[0] < 8:
                            split_to(t_in(l) + 2 * c + 2 + HI)
                            evac_chunk(c)
                            gate[0] += 1

                for g in range(G):
                    u = l * G + g
                    nk = 1 + g
                    act.activation(tmp1[:], proj[:, g, 0:1024], ACT.Square).then_inc(S["a_sq"], 1)
                    if g == 0:
                        act.wait_ge(S["lam_p"], l + 1)
                        act.activation(lamx, lam2, ACT.Exp).then_inc(S["lam_e"], 1)
                    fill(1)
                    act.wait_ge(S["a_T"], u + 1)
                    chain(act.copy(qT[:], X[:, 0, :].rearrange("p (h t) -> p h t", h=4)))
                    for j in range(nk):
                        ins = act.copy(kT[:, :, j, :], X[:, 1 + j, :].rearrange("p (h t) -> p h t", h=4))
                        if j == nk - 1:
                            ins.then_inc(S["a_T_sb"], 1)
                        else:
                            chain(ins)
                    fill(1)
                    act.wait_ge(S["a_nmx"], u + 1)
                    Xs = X[:, :, :].rearrange("p b (h k) -> p (b h) k", k=256)
                    pv = prob[:].rearrange("p (h k) -> p h k", k=256)
                    for h in range(8):
                        ins = act.activation(pv[:, h, 0:nk * P], Xs[:, h, 0:nk * P], ACT.Exp, bias=nmx[:, h:h + 1],
                                             scale=AQK ** -0.5, accum_out=rsum[:, h:h + 1])
                        if h == 7:
                            ins.then_inc(S["a_exp"], 1)
                        else:
                            chain(ins)
                    fill(1)
                    act.wait_ge(S["a_wT"], u + 1)
                    act.copy(wT[:, :, 0:nk, :],
                             X[:, 0:2, :].rearrange("p b (h j t) -> p (b h) j t", h=2, j=2)[:, :, 0:nk, :]).then_inc(
                        S["a_wT_sb"], 1)
                    fill(1)
                    act.wait_ge(S["a_o"], u + 1)
                    act.activation(tmp1[:, 0:512], X[:, 2, :], ACT.Square).then_inc(S["a_osq"], 1)
                    act.wait_ge(S["a_oT"], u + 1)
                    act.copy(brT_hi[:, :, g, :], X[:, 3, :].rearrange("p (h t) -> p h t", h=4)).then_inc(S["br_hi"], 1)
                split_to(t_branch(l, 0) + HI)
                for g in range(G):
                    u = l * G + g
                    nk = 1 + g
                    chain(act.activation(tmp1[:, 0:BQL], proj[:, g, CBQ:CBQ + BQL], ACT.Square,
                                         accum_out=zsum[:, 0:1]))
                    act.sem_inc(S["b_zsq"], 1)
                    act.activation(tmp1[:, BQL:BQL + BKVL], proj[:, g, CKV:CKV + BKVL], ACT.Square,
                                   accum_out=zsum[:, 1:2]).then_inc(S["b_zsq"], 1)
                    act.wait_ge(S["b_zT"], u + 1)
                    zT = wT[:].rearrange("p a b t -> p (a b) t")[:, 0:4, :]
                    act.copy(zT[:, 0:3 + g, :], X[:, 0, 0:(3 + g) * P].rearrange("p (j t) -> p j t", t=P)).then_inc(
                        S["b_zT_sb"], 1)
                    act.wait_ge(S["b_up"], u + 1)
                    chain(act.copy(qk96[:, 0:4, :], X[:, 1, 0:384].rearrange("p (h d) -> p h d", h=4)))
                    for j in range(nk):
                        kv = X[:, 2 + j, :].rearrange("p (h d) -> p h d", h=4)
                        chain(act.copy(qk96[:, 4 + 4 * j:8 + 4 * j, 0:BNOPE], kv[:, :, 0:BNOPE]))
                        chain(act.copy(v_b[:, j, :, :], kv[:, :, BNOPE:BNOPE + BV]))
                    act.wait_ge(S["b_kpe"], u + 1)
                    nh = 4 + 4 * nk
                    sq = tmp1[:].rearrange("p n -> p n")
                    act.activation(prob[:, 0:nh * BQK], qk96[:, 0:nh, :].rearrange("p h d -> p (h d)"),
                                   ACT.Square).then_inc(S["b_sq"], 1)
                    act.wait_ge(S["b_T"], u + 1)
                    chain(act.copy(qT[0:BQK, :, :], X[0:BQK, 0, :].rearrange("p (h t) -> p h t", h=4)))
                    for j in range(nk):
                        ins = act.copy(kT[0:BQK, :, j, :], X[0:BQK, 1 + j, :].rearrange("p (h t) -> p h t", h=4))
                        if j == nk - 1:
                            ins.then_inc(S["b_T_sb"], 1)
                        else:
                            chain(ins)
                    act.wait_ge(S["b_nmx"], u + 1)
                    Xs = X[:, 0:2, :].rearrange("p b (h k) -> p (b h) k", k=256)
                    pv = prob[:].rearrange("p (h k) -> p h k", k=256)
                    for h in range(BH):
                        ins = act.activation(pv[:, h, 0:nk * P], Xs[:, h, 0:nk * P], ACT.Exp, bias=nmx[:, h:h + 1],
                                             scale=BQK ** -0.5, accum_out=rsum[:, h:h + 1])
                        if h == BH - 1:
                            ins.then_inc(S["b_exp"], 1)
                        else:
                            chain(ins)
                    act.wait_ge(S["b_pT"], u + 1)
                    act.copy(wT[:, :, 0:nk, :],
                             X[:, 2:4, :].rearrange("p b (h j t) -> p (b h) j t", h=2, j=2)[:, :, 0:nk, :]).then_inc(
                        S["b_pT_sb"], 1)
                    act.wait_ge(S["b_o"], u + 1)
                    act.copy(o_sb[:, 0:256], X[:, 0, 0:256]).then_inc(S["b_o_sb"], 1)
                    act.wait_ge(S["b_oT"], u + 1)
                    if g == 0:
                        act.wait_ge(S["tile_used"], t_branch(l, 1))
                    act.copy(brT_hi[:, 0:2, g, :], X[:, 1, 0:256].rearrange("p (h t) -> p h t", h=2)).then_inc(
                        S["br_hi"], 1)
                split_to(t_branch(l, 1) + HI)
                for g in range(G):
                    act.activation(tmp2[:, g * 256:(g + 1) * 256], proj[:, g, CC + CCH:CC + 2 * CCH], ACT.Tanh,
                                   scale=0.5).then_inc(S["c_th"], 1)
                act.wait_ge(S["c_T"], l + 1)
                act.wait_ge(S["glu_zero"], l + 1)
                for g in range(G):
                    act.activation(glu_p[:, :, g, PAD:PAD + P],
                                   X[:, 0, g * 256:(g + 1) * 256].rearrange("p (c t) -> p c t", c=2), ACT.Copy,
                                   scale=0.5).then_inc(S["c_T_sb"], 1)
                act.wait_ge(S["c_z"], l + 1)
                act.activation(tmp2[:, 0:512], lnz[:].rearrange("p g n -> p (g n)"), ACT.Tanh,
                               scale=0.5).then_inc(S["c_zth"], 1)
                act.wait_ge(S["c_zT"], l + 1)
                act.wait_ge(S["tile_used"], t_branch(l, 2))
                for g in range(G):
                    act.activation(brT_hi[:, 0:2, g, :],
                                   X[:, 2 + g, 0:256].rearrange("p (h t) -> p h t", h=2), ACT.Copy,
                                   scale=0.5).then_inc(S["br_hi"], 1)
                split_to(t_branch(l, 2) + HI)
                act.wait_ge(S["d_pd"], l + 1)
                act.copy(pdT[:].rearrange("p g k t -> p (g k t)"), X[:, 3, :]).then_inc(S["d_pd_sb"], 1)
                act.wait_ge(S["d_hd"], l + 1)
                for k in range(2):
                    ins = act.activation(hdT[:, k, :, :],
                                         X[:, 0, :].rearrange("p (g k t) -> p k g t", g=G, k=2)[:, k],
                                         ACT.Copy, scale=colp[:, l, 34 + k:35 + k])
                    ins.then_inc(S["d_hd_sb"], 1)
                act.wait_ge(S["d_hd_sb"], 2 * l + 2)
                act.wait_ge(S["tile_used"], t_branch(l, 3))
                for g in range(G):
                    act.copy(brT_hi[:, 0:2, g, :], hdT[:, :, g, :]).then_inc(S["br_hi"], 1)
                split_to(t_branch(l, 3) + HI)
                for g in range(G):
                    act.wait_ge(S["mg_T"], 2 * l + g + 1)
                    act.activation(hT_hi[:, :, g, :],
                                   X[:, 2 * g:2 * g + 2, :].rearrange("p b (k t) -> p (b k) t", t=P), ACT.Copy,
                                   scale=0.5).then_inc(S["hT_hi_ready"], 1)
                split_to(t_out(l) + N_OUT)

                def gate_rows(which):
                    act.wait_ge(S["gb_psum"], 2 * l + which + 1)
                    for g in range(G):
                        act.copy(gbc[:, g, :], X[:, 2 * g:2 * g + 2, :].rearrange("p b n -> p (b n)")).then_inc(
                            S["gb_sb"], 1)

                gate_rows(0)
                split_to(t_ffn(l))
                for g in range(G):
                    norm_sums(4 * l + 2 + g)
                for g in range(G):
                    norm_hi(4 * l + 2 + g)

                def hid_hi(cnt, j, width):
                    act.wait_ge(S["hid_T"], cnt)
                    nb = width // P
                    for g in range(G):
                        act.copy(hidT_hi[:, 4 * j:4 * j + nb, g, :],
                                 X[:, g, 0:width].rearrange("p (k t) -> p k t", t=P)).then_inc(S["hid_hi"], 1)

                if l == 0:
                    tf = t_ffn(0)
                    split_to(tf + HI)
                    for j, (c0, width) in enumerate(FCH):
                        w1_end = tf + 4 * j + (2 if width == 512 else 1)
                        w3_end = tf + 4 * j + (4 if width == 512 else 2)
                        split_to(w1_end + HI)
                        act.wait_ge(S["tile_used"], w1_end)
                        if j:
                            act.wait_ge(S["hid_ready"], 2 * j)
                        for g in range(G):
                            act.activation(silu_s[:, g, 0:width], B[:, g, 0:width], ACT.Silu).then_inc(
                                S["silu_ready"], 1)
                        split_to(w3_end + HI)
                        hid_hi(j + 1, j, width)
                    split_to(tf + N_FFN)
                    gate_rows(1)
                else:
                    act.wait_ge(S["r_diff"], 2)
                    for g in range(G):
                        act.activation(rtmp[:, g, 80:81], rtmp[:, g, 81:82], ACT.Exp).then_inc(S["r_exp"], 1)
                    for g in range(G):
                        act.wait_ge(S["h_tok"], g + 1)
                        act.copy(hT_hi[:, :, g, :],
                                 X[:, 2 * g:2 * g + 2, :].rearrange("p b (k t) -> p (b k) t", t=P)).then_inc(
                            S["h_tok_hi"], 1)

                    def gathered_hi(count):
                        act.wait_ge(S["xg_psum"], count)
                        act.copy(xg_hi[:], B[:, 0:2, :].rearrange("p b (k t) -> p (b k) t", t=P)).then_inc(
                            S["xg_ready"], 1)

                    gathered_hi(2)
                    act.wait_ge(S["h_tok_lo"], 2)
                    t0e = t_ffn(1)
                    nch = len(ECH)
                    act.wait_ge(S["jobs_ready"], 1)
                    n_jobs = act.value_load(job_int[0:1, 0:1], min_val=NE, max_val=JOBS)
                    with act.Fori(0, n_jobs) as e:
                        nxt = [t0e]

                        def esplit(upto):
                            while nxt[0] < min(upto, t0e + N_EXP):
                                split_hi(nxt[0], e)
                                nxt[0] += 1

                        def hid_hi_e(j):
                            act.wait_ge(S["e_hidT"], e * nch + (j + 1))
                            act.copy(hidE_hi[:, 4 * j:4 * j + 4, :],
                                     X[:, j % 2, :].rearrange("p (k t) -> p k t", t=P)).then_inc(S["e_hid_hi"], 1)

                        esplit(t0e + HI)
                        act.wait_ge(S["tile_used"], e * N_EXP + t0e)
                        act.copy(ye_hi[:], X[:, 2:4, :].rearrange("p b n -> p (b n)")).then_inc(S["ye_hi_ready"], 1)
                        for j in range(nch):
                            esplit(t0e + 4 * j + 2 + HI)
                            act.wait_ge(S["tile_used"], e * N_EXP + (t0e + 4 * j + 2))
                            if j >= 2:
                                act.wait_ge(S["e_hid"], e * nch + (j - 1))
                            act.activation(silu_e[:, j % 2, :], B[:, 2 * (j % 2), :], ACT.Silu).then_inc(S["e_silu"], 1)
                            if j:
                                hid_hi_e(j - 1)
                            esplit(t0e + 4 * j + 4 + HI)
                            if j == 2:
                                act.wait_ge(S["pickT_psum"], e + 1)
                                act.copy(pickT[:], X[:, 2, 0:256].rearrange("p (g t) -> p g t", g=G)).then_inc(
                                    S["pickT_sb"], 1)
                        hid_hi_e(nch - 1)
                        gathered_hi(e * 2 + 4)
                        esplit(t0e + N_EXP)
                    act.wait_ge(S["tile_used"], n_jobs * N_EXP + t0e)
                    act.copy(ye_hi[:], X[:, 2:4, :].rearrange("p b n -> p (b n)")).then_inc(S["ye_hi_ready"], 1)
                    gate_rows(1)

        @block.vector
        def _(dve):
            split_next = [0]
            order = [0]

            def chain(ins):
                order[0] += 1
                ins.then_inc(S["dve_order"], 1)
                dve.wait_ge(S["dve_order"], order[0])

            def split_lo(t, e=None):
                s, h = t % RAW, t % HI
                dve.wait_ge(S["hi_ready"], t + 1 if e is None else e * N_EXP + (t + 1))
                n = tile_floats(t)
                dve.tensor_tensor(lo[:, s, 0:n], raw[:, s, 0:n], hi[:, h, 0:n].bitcast(F32), ALU.subtract).then_inc(
                    S["lo_ready"], 1)

            def split_to(t):
                while split_next[0] < t:
                    split_lo(split_next[0])
                    split_next[0] += 1

            def bc(ap, n):
                return ap.unsqueeze(2).broadcast_to([P, ap.shape[1], n])

            def norm_scale(i):
                g = i % G
                dve.wait_ge(S["rstd_ready"], i + 1)
                dve.tensor_scalar(xn[:, g, :], x[:, g, :], rstd[:, g:g + 1], None, ALU.mult).then_inc(S["xn_ready"], 1)

            def norm_modulate(i):
                l, which, g = i // 4, i % 4 // 2, i % G
                dve.wait_ge(S["xn_T"], i + 1)
                dve.wait_ge(S["mod_ready"], l + 1)
                for k in range(KT):
                    ins = dve.tensor_scalar(hfT[:, g, k, :], X[:, 2 * g + k // 4, (k % 4) * P:(k % 4 + 1) * P],
                                            scol[:, which, k, g:g + 1], modcol[:, 3 * which, k, g:g + 1],
                                            ALU.mult, ALU.add)
                ins.then_inc(S["hf_ready"], 1)
                dve.wait_ge(S["hT_hi_ready"], 6 * l + 4 * which + g + 1)
                dve.tensor_tensor(hT_lo[:, :, g, :], hfT[:, g, :, :], hT_hi[:, :, g, :].bitcast(F32),
                                  ALU.subtract).then_inc(S["hT_lo_ready"], 1)

            for l in range(L):
                t0 = t_layer(l)
                if l == 0:
                    dve.memset(ada_hl[:].bitcast(F32), 0.0).then_inc(S["ada_st"], 1)
                    dve.memset(ada_h0[:].bitcast(F32), 0.0).then_inc(S["ada_st"], 1)
                    dve.wait_ge(S["ada_st"], 2)
                    dve.wait_ge(S["sil_th"], 1)
                    chain(dve.scalar_tensor_tensor(sil[:, 1, :], sil[:, 0, :], 1.0, colp[:, 0, 0:16], ALU.add, ALU.mult))
                    chain(dve.tensor_scalar(sil[:, 0, :], sil[:, 1, :], 0.5, None, ALU.mult))
                    src = sil[:, 0, :].rearrange("p (g k) -> p k g", g=G)
                    hl = ada_hl[:, 0:4 * KT].rearrange("p (k v) -> p k v", v=4)
                    h0 = ada_h0[:, 0:4 * KT].rearrange("p (k v) -> p k v", v=4)
                    chain(dve.tensor_copy(hl[:, :, 0:2], src))
                    dve.tensor_copy(h0[:, :, 0:2], src).then_inc(S["ada_st"], 1)
                    dve.tensor_tensor(hl[:, :, 2:4], src, hl[:, :, 0:2].bitcast(F32), ALU.subtract).then_inc(
                        S["ada_st"], 1)
                split_to(t0 + N_ADA)
                dve.wait_ge(S["ada_cols"], 12 * (l + 1))
                chain(dve.tensor_copy(modcol[:].rearrange("p v k g -> p (v k g)"), X[:, 0, 0:96]))
                for which in range(2):
                    gcol = colp[:, l, 16 + 8 * which:24 + 8 * which].unsqueeze(2).broadcast_to([P, KT, G])
                    ins = dve.scalar_tensor_tensor(scol[:, which, :, :], modcol[:, 3 * which + 1, :, :], 1.0, gcol,
                                                   ALU.add, ALU.mult)
                    if which:
                        ins.then_inc(S["mod_ready"], 1)
                    else:
                        chain(ins)
                for g in range(G):
                    norm_scale(4 * l + g)
                split_to(t_in(l) + HI)
                for g in range(G):
                    norm_modulate(4 * l + g)
                lam_init = 0.8 - 0.6 * float(np.exp(-0.3 * l))
                dve.wait_ge(S[f"prm_in{l}"], 160)
                lm = GAIN["lam"].rearrange("p (a b d) -> p a b d", a=2, b=2)
                split_to(t_in(l) + 2 * 6)
                chain(dve.tensor_tensor(tmp2[:, 0:128].rearrange("p (a d) -> p a d", a=2), lm[:, :, 0, :],
                                        lm[:, :, 1, :], ALU.mult))
                dve.tensor_reduce(lam2, tmp2[:, 0:128].rearrange("p (a d) -> p a d", a=2), AX.X, ALU.add).then_inc(
                    S["lam_p"], 1)
                chain(dve.tensor_scalar(GAIN["sub"], GAIN["sub"], 1.0 - lam_init, None, ALU.mult))
                dve.wait_ge(S["lam_e"], l + 1)
                chain(dve.tensor_tensor(neglam, lamx[:, 1:2], lamx[:, 0:1], ALU.subtract))
                dve.tensor_scalar(neglam, neglam, -lam_init, None, ALU.add).then_inc(S["lam_ready"], 1)
                dve.wait_ge(S["lam_ready"], l + 1)

                gate = [0]

                def fill(n):
                    for _ in range(n):
                        if gate[0] < 8:
                            split_to(t_in(l) + 2 * (6 + gate[0]) + 2 + HI)
                            gate[0] += 1

                for g in range(G):
                    u = l * G + g
                    nk = 1 + g
                    fill(1)
                    qk = proj[:, g, 0:1024].rearrange("p (h d) -> p h d", d=AQK)
                    t1 = tmp1[:].rearrange("p (h d) -> p h d", d=AQK)
                    t2 = tmp2[:].rearrange("p (h d) -> p h d", d=AQK)
                    dve.wait_ge(S["a_sq"], u + 1)
                    dve.tensor_reduce(nst16, t1, AX.X, ALU.add).then_inc(S["a_nst"], 1)
                    dve.wait_ge(S["a_rstd"], u + 1)
                    chain(dve.tensor_tensor(t2, qk, bc(rst16, AQK), ALU.mult))
                    gn = GAIN["qk"].rearrange("p (a d) -> p a d", a=2)
                    for a in range(2):
                        ins = dve.tensor_tensor(qk[:, 8 * a:8 * a + 8, :], t2[:, 8 * a:8 * a + 8, :],
                                                gn[:, a:a + 1, :].broadcast_to([P, 8, AQK]), ALU.mult)
                        if a == 0:
                            chain(ins)
                        else:
                            ins.then_inc(S["a_qk"], 1)
                            dve.wait_ge(S["a_qk"], u + 1)
                    if g == 1:
                        cos = tab[:, C_RA:C_RA + AQK].unsqueeze(1).broadcast_to([P, 16, AQK])
                        sin = tab[:, C_RA + AQK:C_RA + 2 * AQK].rearrange("p (f i) -> p f i", i=2)
                        chain(dve.tensor_tensor(t1, qk, cos, ALU.mult))
                        q4 = proj[:, g, 0:1024].rearrange("p (h f i) -> p h f i", f=32, i=2)
                        t4 = tmp2[:].rearrange("p (h f i) -> p h f i", f=32, i=2)
                        for i in range(2):
                            chain(dve.tensor_tensor(t4[:, :, :, i], q4[:, :, :, 1 - i],
                                                    sin[:, :, i].unsqueeze(1).broadcast_to([P, 16, 32]), ALU.mult))
                        dve.tensor_tensor(qk, t1, t2, ALU.add).then_inc(S["a_roped"], 1)
                    fill(1)
                    dve.wait_ge(S["a_scores"], u + 1)
                    Xs = X[:, :, :].rearrange("p b (h k) -> p (b h) k", k=256)
                    chain(dve.tensor_reduce(mx, Xs[:, :, 0:nk * P], AX.X, ALU.max))
                    dve.tensor_scalar(nmx, mx, -(AQK ** -0.5), None, ALU.mult).then_inc(S["a_nmx"], 1)
                    fill(1)
                    dve.wait_ge(S["a_exp"], u + 1)
                    chain(dve.reciprocal(rinv, rsum))
                    chain(dve.tensor_scalar(rinv[:, 4:8], rinv[:, 4:8], neglam, None, ALU.mult))
                    pv = prob[:].rearrange("p (h k) -> p h k", k=256)
                    chain(dve.tensor_tensor(pv[:, :, 0:nk * P], pv[:, :, 0:nk * P], bc(rinv, nk * P), ALU.mult))
                    dve.tensor_tensor(pv[:, 0:4, 0:nk * P], pv[:, 0:4, 0:nk * P], pv[:, 4:8, 0:nk * P],
                                      ALU.add).then_inc(S["a_w"], 1)
                    fill(1)
                    dve.wait_ge(S["a_osq"], u + 1)
                    dve.tensor_reduce(nst16[:, 0:4], tmp1[:, 0:512].rearrange("p (h d) -> p h d", d=AV), AX.X,
                                      ALU.add).then_inc(S["a_ost"], 1)
                    dve.wait_ge(S["a_orstd"], u + 1)
                    ov = o_sb[:].rearrange("p (h d) -> p h d", d=AV)
                    chain(dve.tensor_tensor(ov, X[:, 2, :].rearrange("p (h d) -> p h d", d=AV), bc(rst16[:, 0:4], AV),
                                            ALU.mult))
                    dve.tensor_tensor(ov, ov, GAIN["sub"].unsqueeze(1).broadcast_to([P, 4, AV]), ALU.mult).then_inc(
                        S["a_on"], 1)
                    dve.wait_ge(S["br_hi"], 8 * l + g + 1)
                    dve.tensor_tensor(brT_lo[:, :, g, :], X[:, 3, :].rearrange("p (h t) -> p h t", h=4),
                                      brT_hi[:, :, g, :].bitcast(F32), ALU.subtract).then_inc(S["br_lo"], 1)

                def branch_merge(b):
                    dve.wait_ge(S["tile_used"], t_branch(l, b) + N_BR[b])
                    if b == 0:
                        dve.wait_ge(S["proj_evac"], 28 * (l + 1))
                        dve.wait_ge(S["kv_stored"], 32 * (l + 1))
                    for g in range(G):
                        for half in range(2):
                            gt = gates[:, g, b * D + half * 512:b * D + half * 512 + 512]
                            dst = mg[g][:, half * 512:half * 512 + 512]
                            out = B[:, 2 * g + half, :]
                            if b == 0:
                                chain(dve.scalar_tensor_tensor(dst, gt, 1.0, out, ALU.add, ALU.mult))
                            else:
                                chain(dve.scalar_tensor_tensor(tmp1[:, 0:512], gt, 1.0, out, ALU.add, ALU.mult))
                                chain(dve.tensor_tensor(dst, dst, tmp1[:, 0:512], ALU.add))
                    dve.sem_inc(S["br_used"], 1)

                split_to(t_branch(l, 0) + N_BR[0])
                branch_merge(0)
                for g in range(G):
                    u = l * G + g
                    nk = 1 + g
                    dve.wait_ge(S["b_zrstd"], u + 1)
                    chain(dve.scalar_tensor_tensor(proj[:, g, CBQ:CBQ + BQL], proj[:, g, CBQ:CBQ + BQL], zsum[:, 0:1],
                                                   GAIN["bql"], ALU.mult, ALU.mult))
                    dve.scalar_tensor_tensor(proj[:, g, CKV:CKV + BKVL], proj[:, g, CKV:CKV + BKVL], zsum[:, 1:2],
                                             GAIN["bkvl"], ALU.mult, ALU.mult).then_inc(S["b_z"], 1)
                    dve.wait_ge(S["b_up"], u + 1)
                    if g == 0:
                        dve.wait_ge(S[f"bw_in{l}"], 128)
                    for j in range(nk):
                        kpe = proj[:, g, CPE:CPE + BROPE] if j == 0 else kpe_c[:]
                        ins = dve.tensor_copy(qk96[:, 4 + 4 * j:8 + 4 * j, BNOPE:BQK],
                                              kpe.unsqueeze(1).broadcast_to([P, BH, BROPE]))
                        if j == nk - 1:
                            ins.then_inc(S["b_kpe"], 1)
                        else:
                            chain(ins)
                    nh = 4 + 4 * nk
                    dve.wait_ge(S["b_sq"], u + 1)
                    dve.tensor_reduce(nst16[:, 0:nh], prob[:, 0:nh * BQK].rearrange("p (h d) -> p h d", d=BQK), AX.X,
                                      ALU.add).then_inc(S["b_nst"], 1)
                    dve.wait_ge(S["b_rstd"], u + 1)
                    chain(dve.tensor_tensor(qk96[:, 0:nh, :], qk96[:, 0:nh, :], bc(rst16[:, 0:nh], BQK), ALU.mult))
                    gn = GAIN["bqk"].rearrange("p (a d) -> p a d", a=2)
                    chain(dve.tensor_tensor(qk96[:, 0:4, :], qk96[:, 0:4, :], gn[:, 0:1, :].broadcast_to([P, 4, BQK]),
                                            ALU.mult))
                    ins = dve.tensor_tensor(qk96[:, 4:nh, :], qk96[:, 4:nh, :],
                                            gn[:, 1:2, :].broadcast_to([P, nh - 4, BQK]), ALU.mult)
                    if g == 0:
                        ins.then_inc(S["b_qk"], 1)
                    else:
                        chain(ins)
                        tail = qk96[:, 0:8, BNOPE:BQK]
                        cos = tab[:, C_RB:C_RB + BROPE].unsqueeze(1).broadcast_to([P, 8, BROPE])
                        sin = tab[:, C_RB + BROPE:C_RB + 2 * BROPE].rearrange("p (f i) -> p f i", i=2)
                        tc = prob[:, 1280:1536].rearrange("p (h d) -> p h d", d=BROPE)
                        ts = prob[:, 1536:1792].rearrange("p (h f i) -> p h f i", f=16, i=2)
                        t4 = tail.rearrange("p h (f i) -> p h f i", i=2)
                        chain(dve.tensor_tensor(tc, tail, cos, ALU.mult))
                        for i in range(2):
                            chain(dve.tensor_tensor(ts[:, :, :, i], t4[:, :, :, 1 - i],
                                                    sin[:, :, i].unsqueeze(1).broadcast_to([P, 8, 16]), ALU.mult))
                        dve.tensor_tensor(tail, tc, prob[:, 1536:1792].rearrange("p (h d) -> p h d", d=BROPE),
                                          ALU.add).then_inc(S["b_qk"], 1)
                    dve.wait_ge(S["b_scores"], u + 1)
                    Xs = X[:, 0:2, :].rearrange("p b (h k) -> p (b h) k", k=256)
                    chain(dve.tensor_reduce(mx[:, 0:4], Xs[:, :, 0:nk * P], AX.X, ALU.max))
                    dve.tensor_scalar(nmx[:, 0:4], mx[:, 0:4], -(BQK ** -0.5), None, ALU.mult).then_inc(S["b_nmx"], 1)
                    dve.wait_ge(S["b_exp"], u + 1)
                    chain(dve.reciprocal(rinv[:, 0:4], rsum[:, 0:4]))
                    pv = prob[:].rearrange("p (h k) -> p h k", k=256)
                    dve.tensor_tensor(pv[:, 0:4, 0:nk * P], pv[:, 0:4, 0:nk * P], bc(rinv[:, 0:4], nk * P),
                                      ALU.mult).then_inc(S["b_p"], 1)
                    dve.wait_ge(S["br_hi"], 8 * l + 2 + g + 1)
                    dve.tensor_tensor(brT_lo[:, 0:2, g, :], X[:, 1, 0:256].rearrange("p (h t) -> p h t", h=2),
                                      brT_hi[:, 0:2, g, :].bitcast(F32), ALU.subtract).then_inc(S["br_lo"], 1)
                split_to(t_branch(l, 1) + N_BR[1])
                dve.wait_ge(S["b_oT"], 2 * l + 2)
                dve.memset(glu_p[:], 0.0).then_inc(S["glu_zero"], 1)
                for g in range(G):
                    dve.wait_ge(S["c_th"], 2 * l + g + 1)
                    dve.scalar_tensor_tensor(tmp2[:, g * 256:(g + 1) * 256], tmp2[:, g * 256:(g + 1) * 256], 1.0,
                                             proj[:, g, CC:CC + CCH], ALU.add, ALU.mult).then_inc(S["c_glu"], 1)
                branch_merge(1)
                dve.wait_ge(S["c_T_sb"], 2 * (l + 1))
                for c in range(2):
                    chain(dve.tensor_scalar(conv[:, c, :, :], glu_p[:, c, :, 0:P], colp[:, l, 36 + c:37 + c],
                                            colp[:, l, 32 + c:33 + c], ALU.mult, ALU.add))
                for k in range(1, TAPS):
                    for c in range(2):
                        w = colp[:, l, 36 + 2 * k + c:37 + 2 * k + c]
                        ins = dve.scalar_tensor_tensor(conv[:, c, :, :], glu_p[:, c, :, k:k + P], w, conv[:, c, :, :],
                                                       ALU.mult, ALU.add)
                        if k == TAPS - 1 and c == 1:
                            ins.then_inc(S["c_conv"], 1)
                        else:
                            chain(ins)
                dve.wait_ge(S["c_back"], l + 1)
                for g in range(G):
                    chain(dve.bn_stats(bnst[:, 6 * g:6 * g + 6], X[:, 1, g * 256:(g + 1) * 256]))
                for g in range(G):
                    ins = dve.bn_aggr(mv[:, 2 * g:2 * g + 2], bnst[:, 6 * g:6 * g + 6])
                    if g:
                        ins.then_inc(S["c_mv"], 1)
                        dve.wait_ge(S["c_mv"], l + 1)
                    else:
                        chain(ins)
                dve.wait_ge(S["c_rstd"], l + 1)
                for g in range(G):
                    chain(dve.tensor_scalar(lnz[:, g, :], X[:, 1, g * 256:(g + 1) * 256], mv[:, 2 * g:2 * g + 1],
                                            rln[:, g:g + 1], ALU.subtract, ALU.mult))
                chain(dve.tensor_tensor(lnz[:], lnz[:], GAIN["lng"].unsqueeze(1).broadcast_to([P, G, CCH]), ALU.mult))
                dve.tensor_tensor(lnz[:], lnz[:], GAIN["lnb"].unsqueeze(1).broadcast_to([P, G, CCH]),
                                  ALU.add).then_inc(S["c_z"], 1)
                dve.wait_ge(S["c_zth"], l + 1)
                dve.scalar_tensor_tensor(lnz[:].rearrange("p g n -> p (g n)"), tmp2[:, 0:512], 1.0,
                                         lnz[:].rearrange("p g n -> p (g n)"), ALU.add, ALU.mult).then_inc(
                    S["c_act"], 1)
                for g in range(G):
                    dve.wait_ge(S["br_hi"], 8 * l + 4 + g + 1)
                    dve.scalar_tensor_tensor(brT_lo[:, 0:2, g, :],
                                             X[:, 2 + g, 0:256].rearrange("p (h t) -> p h t", h=2), 0.5,
                                             brT_hi[:, 0:2, g, :].bitcast(F32), ALU.mult, ALU.subtract).then_inc(
                        S["br_lo"], 1)
                split_to(t_branch(l, 2) + N_BR[2])
                branch_merge(2)
                for g in range(G):
                    dve.wait_ge(S["br_hi"], 8 * l + 6 + g + 1)
                    dve.tensor_tensor(brT_lo[:, 0:2, g, :], hdT[:, :, g, :], brT_hi[:, 0:2, g, :].bitcast(F32),
                                      ALU.subtract).then_inc(S["br_lo"], 1)
                split_to(t_branch(l, 3) + N_BR[3])
                branch_merge(3)
                dve.sem_inc(S["mg_ready"], 1)
                for g in range(G):
                    dve.wait_ge(S["hT_hi_ready"], 6 * l + 2 + g + 1)
                    dve.scalar_tensor_tensor(hT_lo[:, :, g, :],
                                             X[:, 2 * g:2 * g + 2, :].rearrange("p b (k t) -> p (b k) t", t=P), 0.5,
                                             hT_hi[:, :, g, :].bitcast(F32), ALU.mult, ALU.subtract).then_inc(
                        S["hT_lo_ready"], 1)
                split_to(t_out(l) + N_OUT)

                def residual(which):
                    for g in range(G):
                        dve.wait_ge(S["gb_sb"], 2 * (2 * l + which) + g + 1)
                        if which == 0:
                            dve.wait_ge(S["tile_used"], t_out(l) + N_OUT)
                        elif l == 0:
                            dve.wait_ge(S["tile_used"], t_ffn(0) + N_FFN)
                        src = B[:, 2 * g:2 * g + 2, :].rearrange("p b n -> p (b n)") if which == 0 or l == 0 \
                            else yacc[:, g, :]
                        chain(dve.tensor_tensor(gbc[:, g, :], gbc[:, g, :], src, ALU.mult))
                        dve.tensor_tensor(x[:, g, :], x[:, g, :], gbc[:, g, :], ALU.add).then_inc(S["x_ready"], 1)
                        dve.wait_ge(S["x_ready"], 4 * l + 2 * which + g + 1)

                residual(0)
                for g in range(G):
                    norm_scale(4 * l + 2 + g)
                split_to(t_ffn(l))
                for g in range(G):
                    norm_modulate(4 * l + 2 + g)

                if l == 0:
                    tf = t_ffn(0)
                    for j, (c0, width) in enumerate(FCH):
                        w3_end = tf + 4 * j + (4 if width == 512 else 2)
                        split_to(w3_end + HI - 1)
                        dve.wait_ge(S["tile_used"], w3_end)
                        for g in range(G):
                            dve.wait_ge(S["silu_ready"], 2 * j + g + 1)
                            dve.tensor_tensor(hid[:, g, 0:width], silu_s[:, g, 0:width], B[:, 2 + g, 0:width],
                                              ALU.mult).then_inc(S["hid_ready"], 1)
                        nb = width // P
                        for g in range(G):
                            dve.wait_ge(S["hid_hi"], 2 * j + g + 1)
                            dve.tensor_tensor(hidT_lo[:, 4 * j:4 * j + nb, g, :],
                                              X[:, g, 0:width].rearrange("p (k t) -> p k t", t=P),
                                              hidT_hi[:, 4 * j:4 * j + nb, g, :].bitcast(F32), ALU.subtract).then_inc(
                                S["hid_lo"], 1)
                    split_to(tf + N_FFN)
                    residual(1)
                else:
                    dve.memset(ones[:], 1.0).then_inc(S["r_mask"], 1)
                    for g in range(G):
                        dve.wait_ge(S["r_psum"], g + 1)
                        lg = rtmp[:, g, 0:8]
                        chain(dve.tensor_copy(lg, X[:, g, 0:8]))
                        cmp = rtmp[:, g, 128:192].rearrange("p (e j) -> p e j", j=8)
                        cm2 = rtmp[:, g, 192:256].rearrange("p (e j) -> p e j", j=8)
                        lj = lg.unsqueeze(1).broadcast_to([P, 8, 8])
                        le = lg.unsqueeze(2).broadcast_to([P, 8, 8])
                        tri = tab[:, C_TRI:C_TRI + 64].rearrange("p (e j) -> p e j", j=8)
                        chain(dve.tensor_tensor(cmp, lj, le, ALU.is_gt))
                        chain(dve.tensor_tensor(cm2, lj, le, ALU.is_equal))
                        chain(dve.tensor_tensor(cm2, cm2, tri, ALU.mult))
                        chain(dve.tensor_tensor(cmp, cmp, cm2, ALU.add))
                        rank = rtmp[:, g, 8:16]
                        chain(dve.tensor_reduce(rank, cmp, AX.X, ALU.add))
                        first, second = rtmp[:, g, 16:24], rtmp[:, g, 24:32]
                        chain(dve.tensor_scalar(first, rank, 0.0, None, ALU.is_equal))
                        chain(dve.tensor_scalar(second, rank, 1.0, None, ALU.is_equal))
                        chain(dve.tensor_tensor(rtmp[:, g, 32:40], first, lg, ALU.mult))
                        chain(dve.tensor_tensor(rtmp[:, g, 40:48], second, lg, ALU.mult))
                        chain(dve.tensor_tensor(rtmp[:, g, 32:40], rtmp[:, g, 40:48], rtmp[:, g, 32:40], ALU.subtract))
                        dve.tensor_tensor(rtmp[:, g, 48:56], first, second, ALU.add).then_inc(S["r_mask"], 1)
                        dve.tensor_reduce(rtmp[:, g, 81:82], rtmp[:, g, 32:40], AX.X, ALU.add).then_inc(S["r_diff"], 1)
                    for g in range(G):
                        dve.wait_ge(S["r_exp"], g + 1)
                        ex, w1, w2 = rtmp[:, g, 80:81], rtmp[:, g, 82:83], rtmp[:, g, 83:84]
                        chain(dve.tensor_scalar(w1, ex, 1.0, None, ALU.add))
                        chain(dve.reciprocal(w1, w1))
                        chain(dve.tensor_tensor(w2, ex, w1, ALU.mult))
                        first, second = rtmp[:, g, 16:24], rtmp[:, g, 24:32]
                        chain(dve.tensor_scalar(first, first, w1, None, ALU.mult))
                        chain(dve.scalar_tensor_tensor(rtmp[:, g, 88:96], second, w2, first, ALU.mult, ALU.add))
                    dve.wait_ge(S["router_in"], 32)
                    for g in range(G):
                        m, pc = rtmp[:, g, 48:56], rtmp[:, g, 56:64]
                        dve.wait_ge(S["r_pos"], 1)
                        chain(dve.tensor_tensor(pc, X[:, g, 16:24], m, ALU.mult))
                        chain(dve.tensor_tensor(pc, pc, m, ALU.add))
                        chain(dve.tensor_scalar(job_pos[:, g, 0:NE], pc, 1.0, None, ALU.subtract))
                        chain(dve.tensor_scalar(pc, pc, 129.0, None, ALU.subtract))
                        chain(dve.memset(job_pos[:, g, JOBS:JOBS + 1], -1.0))
                        chain(dve.memset(job_comb[:, g, 0:1], 0.0))
                        chain(dve.tensor_copy(job_comb[:, g, 1:1 + NE], rtmp[:, g, 88:96]))
                    over, orank, sel = rtmp[:, 0, 96:104], rtmp[:, 0, 104:112], rtmp[:, 1, 96:104]
                    cmp = rtmp[:, 0, 128:192].rearrange("p (e j) -> p e j", j=8)
                    tri = tab[:, C_TRI:C_TRI + 64].rearrange("p (e j) -> p e j", j=8)
                    some = rtmp[:, 1, 104:105]
                    chain(dve.tensor_scalar(over, X[:, 2, 16:24], float(P), None, ALU.is_gt))
                    chain(dve.tensor_tensor(cmp, over.unsqueeze(1).broadcast_to([P, 8, 8]), tri, ALU.mult))
                    chain(dve.tensor_reduce(orank, cmp, AX.X, ALU.add))
                    fint = rtmp[:, 1, 105:109]
                    chain(dve.tensor_reduce(fint[:, 0:1], over, AX.X, ALU.add))
                    chain(dve.tensor_scalar(fint[:, 0:1], fint[:, 0:1], float(NE), None, ALU.add))
                    for k in range(JOBS - NE):
                        chain(dve.scalar_tensor_tensor(sel, orank, float(k), over, ALU.is_equal, ALU.mult))
                        chain(dve.tensor_reduce(some, sel, AX.X, ALU.add))
                        prod = rtmp[:, 0, 112:120]
                        for g in range(G):
                            pc, cb = rtmp[:, g, 56:64], rtmp[:, g, 88:96]
                            jp = job_pos[:, g, NE + k:NE + k + 1]
                            chain(dve.tensor_tensor(prod, sel, pc, ALU.mult))
                            chain(dve.tensor_reduce(jp, prod, AX.X, ALU.add))
                            chain(dve.tensor_scalar(jp, jp, some, 1.0, ALU.add, ALU.subtract))
                            chain(dve.tensor_tensor(prod, sel, cb, ALU.mult))
                            chain(dve.tensor_reduce(job_comb[:, g, 1 + NE + k:2 + NE + k], prod, AX.X, ALU.add))
                        chain(dve.tensor_tensor(prod, sel, etab[:, 0:NE], ALU.mult))
                        chain(dve.tensor_reduce(fint[:, 1 + k:2 + k], prod, AX.X, ALU.add))
                    dve.tensor_copy(job_int[:], fint).then_inc(S["jobs_ready"], 1)

                    def pick_job(e):
                        for g in range(G):
                            dve.tensor_scalar(pick[:, g, :], etab[:, 0:P], job_pos[:, g, bass.ds(e, 1)], None,
                                              ALU.is_equal).then_inc(S["pick_ready"], 1)

                    def gathered_lo(count):
                        dve.wait_ge(S["xg_psum"], count)
                        dve.tensor_copy(xg_lo[:], B[:, 2:4, :].rearrange("p b (k t) -> p (b k) t", t=P)).then_inc(
                            S["xg_ready"], 1)

                    pick_job(0)
                    for g in range(G):
                        dve.wait_ge(S["h_tok_hi"], g + 1)
                        dve.tensor_tensor(hT_lo[:, :, g, :],
                                          X[:, 2 * g:2 * g + 2, :].rearrange("p b (k t) -> p (b k) t", t=P),
                                          hT_hi[:, :, g, :].bitcast(F32), ALU.subtract).then_inc(S["h_tok_lo"], 1)
                    dve.memset(pickT[:].bitcast(F32), 0.0).then_inc(S["ys_used"], 1)
                    dve.memset(yacc[:], 0.0).then_inc(S["ys_used"], 1)
                    gathered_lo(1)
                    t0e = t_ffn(1)
                    nch = len(ECH)
                    dve.wait_ge(S["jobs_ready"], 1)
                    n_jobs = dve.value_load(job_int[0:1, 0:1], min_val=NE, max_val=JOBS)

                    def output_lo(e):
                        dve.wait_ge(S["ye_hi_ready"], e + 1)
                        dve.tensor_tensor(ye_lo[:], X[:, 2:4, :].rearrange("p b n -> p (b n)"), ye_hi[:].bitcast(F32),
                                          ALU.subtract).then_inc(S["ye_lo_ready"], 1)

                    def accumulate(e):
                        for g in range(G):
                            dve.wait_ge(S["ys_psum"], e * 2 + (g + 1))
                            bank = X[:, 2:4, :] if g == 0 else X[:, 0:2, :]
                            dve.scalar_tensor_tensor(yacc[:, g, :], bank.rearrange("p b n -> p (b n)"),
                                                     job_comb[:, g, bass.ds(e, 1)], yacc[:, g, :], ALU.mult,
                                                     ALU.add).then_inc(S["ys_used"], 1)

                    with dve.Fori(0, n_jobs) as e:
                        nxt = [t0e]

                        def esplit(upto):
                            while nxt[0] < min(upto, t0e + N_EXP):
                                split_lo(nxt[0], e)
                                nxt[0] += 1

                        def hid_lo_e(j):
                            dve.wait_ge(S["e_hid_hi"], e * nch + (j + 1))
                            dve.tensor_tensor(hidE_lo[:, 4 * j:4 * j + 4, :],
                                              X[:, j % 2, :].rearrange("p (k t) -> p k t", t=P),
                                              hidE_hi[:, 4 * j:4 * j + 4, :].bitcast(F32), ALU.subtract).then_inc(
                                S["e_hid_lo"], 1)

                        esplit(t0e + HI)
                        output_lo(e)
                        for j in range(nch):
                            esplit(t0e + 4 * j + 2 + HI - 1)
                            if j:
                                hid_lo_e(j - 1)
                            esplit(t0e + 4 * j + 4 + HI - 1)
                            dve.wait_ge(S["tile_used"], e * N_EXP + (t0e + 4 * j + 4))
                            dve.wait_ge(S["e_silu"], e * nch + (j + 1))
                            if j >= 2:
                                dve.wait_ge(S["e_hidT"], e * nch + (j - 1))
                            dve.tensor_tensor(hid_e[:, j % 2, :], silu_e[:, j % 2, :], B[:, 2 * (j % 2) + 1, :],
                                              ALU.mult).then_inc(S["e_hid"], 1)
                            if j == 0:
                                accumulate(e)
                            if j == 3:
                                dve.wait_ge(S["pickT_psum"], e + 1)
                                pick_job(e + 1)
                        hid_lo_e(nch - 1)
                        gathered_lo(e * 2 + 3)
                        esplit(t0e + N_EXP)
                    output_lo(n_jobs)
                    accumulate(n_jobs)
                    dve.wait_ge(S["ys_used"], n_jobs * 2 + 4)
                    residual(1)

        @block.tensor
        def _(pe):
            def tile_done(ins):
                ins.then_inc(S["tile_used"], 1)

            def wait_tile(t, e=None):
                pe.wait_ge(S["lo_ready"], t + 1 if e is None else e * N_EXP + (t + 1))

            def parts(t, nk, width):
                h = hi[:, t % HI, 0:nk * width].rearrange("p (k n) -> p k n", n=width)
                lw = lo[:, t % RAW, 0:nk * width].rearrange("p (k n) -> p k n", n=width)
                return h, lw

            def product(out, s_hi, s_lo, w_hi, w_lo, start, stop):
                pe.matmul(out, s_hi, w_hi, start=start, stop=False)
                pe.matmul(out, s_hi, w_lo, start=False, stop=False)
                return pe.matmul(out, s_lo, w_hi, start=False, stop=stop)

            def rows_tile(t, a_hi, a_lo, banks, k0, first, last, e=None, width=512, nk=4, k_all=KT):
                wait_tile(t, e)
                wh, wl = parts(t, nk, width)
                for g in range(G):
                    for k in range(nk):
                        ins = product(banks[g][:, 0:width], a_hi[:, k0 + k, g, :], a_lo[:, k0 + k, g, :], wh[:, k, :],
                                      wl[:, k, :], first and k == 0, last and k == nk - 1)
                tile_done(ins)
                return ins

            def full_tile(t, a_hi, a_lo, k0, first, last, e=None):
                wait_tile(t, e)
                wh, wl = parts(t, 2, D)
                for g in range(G):
                    for half in range(2):
                        for k in range(2):
                            cs = slice(512 * half, 512 * half + 512)
                            ins = product(B[:, 2 * g + half, :], a_hi[:, k0 + k, g, :], a_lo[:, k0 + k, g, :],
                                          wh[:, k, cs], wl[:, k, cs], first and k == 0, last and k == 1)
                tile_done(ins)

            def norm_T(i):
                g = i % G
                pe.wait_ge(S["xn_ready"], i + 1)
                for k in range(KT):
                    ins = pe.transpose(X[:, 2 * g + k // 4, (k % 4) * P:(k % 4 + 1) * P], xn[:, g, k * P:(k + 1) * P],
                                       ident)
                ins.then_inc(S["xn_T"], 1)

            for l in range(L):
                t0 = t_layer(l)
                if l == 0:
                    pe.wait_ge(S["tab_in"], 16)
                    pe.wait_ge(S["rows_in"], 14 * 16)
                    for j in range(L):
                        pe.transpose(X[:, 0, 98 * j:98 * j + 98], rowp[0:98, j, :], ident[0:98, 0:98]).then_inc(
                            S["cols_psum"], 1)
                    pe.wait_ge(S["ada_st"], 4)
                pe.wait_ge(S[f"adab_in{l}"], 16)
                if l == 0:
                    pe.wait_ge(S["cols_sb"], 1)

                def mod_cols(c):
                    v, half = c // 2, c % 2
                    pe.wait_ge(S["ada_row"], 12 * l + c + 1)
                    if v in (2, 5):
                        pe.sem_inc(S["ada_cols"], 1)
                        return
                    for q in range(4):
                        n = (v * KT + half * 4 + q) * G
                        ins = pe.matmul(X[:, 0, n:n + 2], modrow[0:4, q * P:(q + 1) * P], tab[0:4, C_SEL:C_SEL + 2],
                                        start=True, stop=True)
                    ins.then_inc(S["ada_cols"], 1)

                if l == 1:
                    pe.wait_ge(S["x_ready"], 4)
                for c in range(12):
                    bank = B[:, c % 2, :]
                    if c >= 2:
                        pe.wait_ge(S["ada_row"], 12 * l + c - 1)
                    pe.matmul(bank, tab[0:12, C_SELB + 4 * c:C_SELB + 4 * c + P],
                              adab[:, :], start=True, stop=False)
                    for half in range(2):
                        t = t0 + 2 * c + half
                        wait_tile(t)
                        wh, wl = parts(t, 4, 512)
                        for k in range(4):
                            kk = 4 * (4 * half + k)
                            pe.matmul(bank, ada_hl[:, kk:kk + P], wh[:, k, :], start=False, stop=False)
                            ins = pe.matmul(bank, ada_h0[:, kk:kk + P], wl[:, k, :], start=False,
                                            stop=(half == 1 and k == 3))
                        tile_done(ins)
                    if c >= 1:
                        mod_cols(c - 1)
                mod_cols(11)
                pe.wait_ge(S["mod_ready"], l + 1)
                for g in range(G):
                    norm_T(4 * l + g)
                pe.wait_ge(S["hT_lo_ready"], 6 * l + 2)

                def chunk(c):
                    c0, width = CHUNKS[c]
                    banks = [B[:, 2 * (c % 2) + g, :] for g in range(G)]
                    n = 14 * l + c
                    if c >= 2:
                        pe.wait_ge(S["proj_evac"], 2 * (n - 1))
                    for half in range(2):
                        rows_tile(t_in(l) + 2 * c + half, hT_hi, hT_lo, banks, 4 * half, half == 0, half == 1,
                                  width=width)

                for c in range(6):
                    chunk(c)
                gate = [0]

                def fill(n):
                    for _ in range(n):
                        if gate[0] < 8:
                            chunk(6 + gate[0])
                            gate[0] += 1

                def branch_product(b):
                    pe.wait_ge(S["br_lo"], 8 * l + 2 * b + 2)
                    if b == 0:
                        pe.wait_ge(S["proj_evac"], 28 * (l + 1))
                    else:
                        pe.wait_ge(S["br_used"], 4 * l + b)
                    for i in range(N_BR[b]):
                        full_tile(t_branch(l, b) + i, brT_hi, brT_lo, 2 * i, i == 0, i == N_BR[b] - 1)

                for g in range(G):
                    u = l * G + g
                    nk = 1 + g
                    fill(1)
                    pe.wait_ge(S["a_qk"], u + 1)
                    if g == 1:
                        pe.wait_ge(S["a_roped"], l + 1)
                        pe.wait_ge(S[f"kv_in{l}"], 32)
                        pe.wait_ge(S["br_lo"], 8 * l + 1)
                    for j in range(2 + g):
                        for hp in range(4):
                            src = proj[:, g, 512 * j + hp * P:512 * j + (hp + 1) * P] if j < 2 \
                                else k_c[:, hp * P:(hp + 1) * P]
                            ins = pe.transpose(X[:, j, hp * P:(hp + 1) * P], src, ident)
                    ins.then_inc(S["a_T"], 1)
                    fill(1)
                    pe.wait_ge(S["a_T_sb"], u + 1)
                    for h in range(8):
                        hp, i = h // 2, h % 2
                        r = slice(64 * i, 64 * i + 64)
                        ins = pe.matmul(X[:, 2 * i + hp // 2, (hp % 2) * 256:(hp % 2) * 256 + nk * P], qT[r, hp, :],
                                        kT[r, hp, 0:nk, :].rearrange("p j t -> p (j t)"), start=True, stop=True)
                    ins.then_inc(S["a_scores"], 1)
                    fill(1)
                    pe.wait_ge(S["a_w"], u + 1)
                    for h in range(4):
                        for j in range(nk):
                            at = ((h % 2) * 2 + j) * P
                            ins = pe.transpose(X[:, h // 2, at:at + P], prob[:, h * 256 + j * P:h * 256 + (j + 1) * P],
                                               ident)
                    ins.then_inc(S["a_wT"], 1)
                    fill(1)
                    pe.wait_ge(S["a_wT_sb"], u + 1)
                    for h in range(4):
                        for j in range(nk):
                            v = proj[:, g, CV + h * AV:CV + (h + 1) * AV] if j == 0 else v_c[:, h * AV:(h + 1) * AV]
                            ins = pe.matmul(X[:, 2, h * AV:(h + 1) * AV], wT[:, h, j, :], v, start=(j == 0),
                                            stop=(j == nk - 1))
                    ins.then_inc(S["a_o"], 1)
                    pe.wait_ge(S["a_on"], u + 1)
                    for h in range(4):
                        ins = pe.transpose(X[:, 3, h * P:(h + 1) * P], o_sb[:, h * P:(h + 1) * P], ident)
                    ins.then_inc(S["a_oT"], 1)
                branch_product(0)
                pe.wait_ge(S[f"bw_in{l}"], 128)
                zT = wT[:].rearrange("p a b t -> p (a b) t")
                for g in range(G):
                    u = l * G + g
                    nk = 1 + g
                    pe.wait_ge(S["b_z"], u + 1)
                    srcs = [proj[:, g, CBQ:CBQ + P], proj[:, g, CBQ + P:CBQ + 2 * P], proj[:, g, CKV:CKV + P]]
                    if g == 1:
                        srcs.append(ckv_c[:])
                        pe.wait_ge(S["br_lo"], 8 * l + 3)
                    for j, src in enumerate(srcs):
                        ins = pe.transpose(X[:, 0, j * P:(j + 1) * P], src, ident)
                    ins.then_inc(S["b_zT"], 1)
                    pe.wait_ge(S["b_zT_sb"], u + 1)
                    for k in range(2):
                        pe.matmul(X[:, 1, 0:384], zT[:, k, :], uq_w[:, k, :], start=(k == 0), stop=(k == 1))
                    for j in range(nk):
                        ins = pe.matmul(X[:, 2 + j, :], zT[:, 2 + j, :], ukv_w[:], start=True, stop=True)
                    ins.then_inc(S["b_up"], 1)
                    pe.wait_ge(S["b_qk"], u + 1)
                    for j in range(1 + nk):
                        for h in range(4):
                            ins = pe.transpose(X[0:BQK, j, h * P:(h + 1) * P], qk96[:, 4 * j + h, :], ident)
                    ins.then_inc(S["b_T"], 1)
                    pe.wait_ge(S["b_T_sb"], u + 1)
                    for h in range(4):
                        ins = pe.matmul(X[:, h // 2, (h % 2) * 256:(h % 2) * 256 + nk * P], qT[0:BQK, h, :],
                                        kT[0:BQK, h, 0:nk, :].rearrange("p j t -> p (j t)"), start=True, stop=True)
                    ins.then_inc(S["b_scores"], 1)
                    pe.wait_ge(S["b_p"], u + 1)
                    for h in range(4):
                        for j in range(nk):
                            at = ((h % 2) * 2 + j) * P
                            ins = pe.transpose(X[:, 2 + h // 2, at:at + P],
                                               prob[:, h * 256 + j * P:h * 256 + (j + 1) * P], ident)
                    ins.then_inc(S["b_pT"], 1)
                    pe.wait_ge(S["b_pT_sb"], u + 1)
                    for h in range(4):
                        for j in range(nk):
                            ins = pe.matmul(X[:, 0, h * BV:(h + 1) * BV], wT[:, h, j, :], v_b[:, j, h, :],
                                            start=(j == 0), stop=(j == nk - 1))
                    ins.then_inc(S["b_o"], 1)
                    pe.wait_ge(S["b_o_sb"], u + 1)
                    for h in range(2):
                        ins = pe.transpose(X[:, 1, h * P:(h + 1) * P], o_sb[:, h * P:(h + 1) * P], ident)
                    ins.then_inc(S["b_oT"], 1)
                branch_product(1)
                pe.wait_ge(S["c_glu"], 2 * (l + 1))
                for g in range(G):
                    for c in range(2):
                        at = g * 256 + c * P
                        ins = pe.transpose(X[:, 0, at:at + P], tmp2[:, at:at + P], ident)
                ins.then_inc(S["c_T"], 1)
                pe.wait_ge(S["c_conv"], l + 1)
                for g in range(G):
                    for c in range(2):
                        at = g * 256 + c * P
                        ins = pe.transpose(X[:, 1, at:at + P], conv[:, c, g, :], ident)
                ins.then_inc(S["c_back"], 1)
                pe.wait_ge(S["c_act"], l + 1)
                for g in range(G):
                    for c in range(2):
                        ins = pe.transpose(X[:, 2 + g, c * P:(c + 1) * P], lnz[:, g, c * P:(c + 1) * P], ident)
                ins.then_inc(S["c_zT"], 1)
                branch_product(2)
                for g in range(G):
                    for i in range(4):
                        r = slice(64 * (i % 2), 64 * (i % 2) + 64)
                        at = g * 256 + (i // 2) * P
                        ins = pe.matmul(X[r, 3, at:at + P], proj[:, g, CD + i * DG:CD + (i + 1) * DG],
                                        tab[:, C_POOL + i * P:C_POOL + (i + 1) * P], start=True, stop=True)
                ins.then_inc(S["d_pd"], 1)
                pe.wait_ge(S["d_pd_sb"], l + 1)
                for g in range(G):
                    for i in range(4):
                        r = slice(64 * (i % 2), 64 * (i % 2) + 64)
                        at = g * 256 + (i // 2) * P
                        ins = pe.matmul(X[r, 0, at:at + P], dg_w[r, i // 2, :], pdT[r, g, i // 2, :], start=True,
                                        stop=True)
                ins.then_inc(S["d_hd"], 1)
                branch_product(3)
                pe.wait_ge(S["mg_ready"], l + 1)
                for g in range(G):
                    for k in range(KT):
                        ins = pe.transpose(X[:, 2 * g + k // 4, (k % 4) * P:(k % 4 + 1) * P],
                                           mg[g][:, k * P:(k + 1) * P], ident)
                    ins.then_inc(S["mg_T"], 1)
                pe.wait_ge(S["hT_lo_ready"], 6 * l + 4)
                for i in range(N_OUT):
                    full_tile(t_out(l) + i, hT_hi, hT_lo, 2 * i, i == 0, i == N_OUT - 1)

                def gate_rows(which):
                    for g in range(G):
                        for half in range(2):
                            r = 32 * (2 * which + half)
                            ins = pe.matmul(X[:, 2 * g + half, :], tab[r:r + 4, C_SELG + g * P:C_SELG + (g + 1) * P],
                                            grow[r:r + 4, :], start=True, stop=True)
                    ins.then_inc(S["gb_psum"], 1)

                gate_rows(0)
                pe.wait_ge(S["gb_sb"], 4 * l + 2)
                for g in range(G):
                    norm_T(4 * l + 2 + g)
                pe.wait_ge(S["hT_lo_ready"], 6 * l + 6)

                if l == 0:
                    tf = t_ffn(0)
                    for j, (c0, width) in enumerate(FCH):
                        nk = TW // width
                        n_t = KT // nk
                        for w in range(2):
                            if j:
                                if w == 0:
                                    pe.wait_ge(S["silu_ready"], 2 * j)
                                else:
                                    pe.wait_ge(S["hid_ready"], 2 * j)
                            for i in range(n_t):
                                rows_tile(tf + 4 * j + w * n_t + i, hT_hi, hT_lo, [B[:, 2 * w, :], B[:, 2 * w + 1, :]],
                                          nk * i, i == 0, i == n_t - 1, width=width, nk=nk)
                        pe.wait_ge(S["hid_ready"], 2 * j + 2)
                        if j:
                            pe.wait_ge(S["hid_lo"], 2 * j)
                        for g in range(G):
                            for k in range(width // P):
                                ins = pe.transpose(X[:, g, k * P:(k + 1) * P], hid[:, g, k * P:(k + 1) * P], ident)
                        ins.then_inc(S["hid_T"], 1)
                    pe.wait_ge(S["hid_lo"], 2 * len(FCH))
                    for i in range(N_FFN_DN):
                        full_tile(tf + N_FFN_UP + i, hidT_hi, hidT_lo, 2 * i, i == 0, i == N_FFN_DN - 1)
                    gate_rows(1)
                else:
                    pe.wait_ge(S["router_in"], 32)
                    for g in range(G):
                        for k in range(KT):
                            ins = pe.matmul(X[:, g, 0:8], hfT[:, g, k, :], router[:, k, :], start=(k == 0),
                                            stop=(k == KT - 1))
                        ins.then_inc(S["r_psum"], 1)
                    pe.wait_ge(S["r_mask"], 3)
                    pe.wait_ge(S["r_diff"], 2)
                    before = etab[:, P:2 * P]
                    m = [rtmp[:, g, 48:56] for g in range(G)]
                    pe.matmul(X[:, 0, 16:24], before, m[0], start=True, stop=True)
                    pe.matmul(X[:, 1, 16:24], before, m[1], start=True, stop=False)
                    pe.matmul(X[:, 1, 16:24], ones[:], m[0], start=False, stop=True)
                    pe.matmul(X[:, 2, 16:24], ones[:], m[0], start=True, stop=False)
                    pe.matmul(X[:, 2, 16:24], ones[:], m[1], start=False, stop=True).then_inc(S["r_pos"], 1)
                    pe.wait_ge(S["jobs_ready"], 1)
                    for g in range(G):
                        for k in range(KT):
                            ins = pe.transpose(X[:, 2 * g + k // 4, (k % 4) * P:(k % 4 + 1) * P], hfT[:, g, k, :],
                                               ident)
                        ins.then_inc(S["h_tok"], 1)

                    def gather(part):
                        src, b0 = (hT_lo, 2) if part == 0 else (hT_hi, 0)
                        for k in range(KT):
                            for g in range(G):
                                ins = pe.matmul(B[:, b0 + k // 4, (k % 4) * P:(k % 4 + 1) * P], src[:, k, g, :],
                                                pick[:, g, :], start=(g == 0), stop=(g == G - 1))
                        ins.then_inc(S["xg_psum"], 1)

                    pe.wait_ge(S["pick_ready"], 2)
                    pe.wait_ge(S["h_tok_lo"], 2)
                    gather(0)
                    gather(1)
                    t0e = t_ffn(1)
                    nch = len(ECH)
                    n_jobs = pe.value_load(job_int[0:1, 0:1], min_val=NE, max_val=JOBS)

                    def scatter(e):
                        pe.wait_ge(S["ye_lo_ready"], e + 1)
                        for g in range(G):
                            b0 = 2 if g == 0 else 0
                            for half in range(2):
                                cs = slice(512 * half, 512 * half + 512)
                                pe.matmul(X[:, b0 + half, :], pickT[:, g, :], ye_hi[:, cs], start=True, stop=False)
                                ins = pe.matmul(X[:, b0 + half, :], pickT[:, g, :], ye_lo[:, cs], start=False,
                                                stop=True)
                            ins.then_inc(S["ys_psum"], 1)

                    with pe.Fori(0, n_jobs) as e:
                        def up(j, w):
                            for i in range(2):
                                t = t0e + 4 * j + 2 * w + i
                                wait_tile(t, e)
                                wh, wl = parts(t, 4, 512)
                                for k in range(4):
                                    ins = product(B[:, 2 * (j % 2) + w, :], xg_hi[:, 4 * i + k, :],
                                                  xg_lo[:, 4 * i + k, :], wh[:, k, :], wl[:, k, :],
                                                  i == 0 and k == 0, i == 1 and k == 3)
                                tile_done(ins)

                        def turn(j):
                            pe.wait_ge(S["e_hid"], e * nch + (j + 1))
                            if j >= 2:
                                pe.wait_ge(S["e_hid_lo"], e * nch + (j - 1))
                            for k in range(4):
                                ins = pe.transpose(X[:, j % 2, k * P:(k + 1) * P], hid_e[:, j % 2, k * P:(k + 1) * P],
                                                   ident)
                            ins.then_inc(S["e_hidT"], 1)

                        pe.wait_ge(S["xg_ready"], e * 2 + 2)
                        for j in range(nch):
                            if j >= 2:
                                pe.wait_ge(S["e_hid"], e * nch + (j - 1))
                            up(j, 0)
                            if j == 1:
                                pe.wait_ge(S["ys_used"], e * 2 + 4)
                            if j:
                                turn(j - 1)
                            up(j, 1)
                            if j == 0:
                                scatter(e)
                            if j == 1:
                                for g in range(G):
                                    ins = pe.transpose(X[:, 2, g * P:(g + 1) * P], pick[:, g, :].bitcast(F32), ident)
                                ins.then_inc(S["pickT_psum"], 1)
                        pe.wait_ge(S["pick_ready"], e * 2 + 4)
                        gather(0)
                        turn(nch - 1)
                        gather(1)
                        pe.wait_ge(S["pickT_sb"], e + 1)
                        for i in range(N_EXP_DN):
                            if i % 2 == 0:
                                pe.wait_ge(S["e_hid_lo"], e * nch + (i // 2 + 1))
                            t = t0e + N_EXP_UP + i
                            wait_tile(t, e)
                            wh, wl = parts(t, 2, D)
                            for half in range(2):
                                for k in range(2):
                                    cs = slice(512 * half, 512 * half + 512)
                                    ins = product(X[:, 2 + half, :], hidE_hi[:, 2 * i + k, :], hidE_lo[:, 2 * i + k, :],
                                                  wh[:, k, cs], wl[:, k, cs], i == 0 and k == 0,
                                                  i == N_EXP_DN - 1 and k == 1)
                            tile_done(ins)
                    scatter(n_jobs)
                    pe.wait_ge(S["ys_used"], n_jobs * 2 + 4)
                    gate_rows(1)


_INS = ['x_prompt', 'x_sample', 'cache_a_k', 'cache_a_v', 'cache_b_ckv', 'cache_b_kpe', 'c', 'c_ctx', 'ada_w', 'ada_b',
        'norm1_g', 'norm2_g', 'w_in', 'a_q_norm', 'a_k_norm', 'a_lambda', 'a_sub_norm', 'a_w_o', 'b_q_lora_norm',
        'b_kv_lora_norm', 'b_w_uq', 'b_w_ukv', 'b_q_norm', 'b_k_norm', 'b_w_o', 'c_dw', 'c_dw_b', 'c_ln_g', 'c_ln_b',
        'c_w_o', 'd_w_group', 'd_scale', 'd_w_o', 'w_out', 'ffn_w1', 'ffn_w3', 'ffn_w2', 'moe_router', 'moe_w1',
        'moe_w3', 'moe_w2']
_OUTS = [("y_prompt", (1, 128, 1024)), ("y_sample", (1, 128, 1024)), ("ak", (1, 2, 128, 8, 64)),
         ("av", (1, 2, 128, 4, 128)), ("ckv", (1, 2, 128, 128)), ("kpe", (1, 2, 128, 32))]


def kernel(**inputs):
    import concourse.bacc as _bacc
    from concourse.bass_utils import run_bass_kernel_spmd as _run

    nc = _bacc.Bacc("TRN2", target_bir_lowering=False, num_devices=1)
    arrays, args, outs = {}, {}, {}
    for name in _INS:
        a = np.ascontiguousarray(inputs[name])
        arrays[f"in_{name}"] = a
        args[name] = nc.dram_tensor(f"in_{name}", a.shape, F32, kind="ExternalInput").ap()
    arrays["in_tables"] = shape_tables()
    args["tables"] = nc.dram_tensor("in_tables", (P, C_ALL), F32, kind="ExternalInput").ap()
    for name, shape in _OUTS:
        outs[name] = nc.dram_tensor(f"out_{name}", shape, F32, kind="ExternalOutput").ap()
    trunk_kernel(nc, args, outs)
    r = _run(nc, [arrays], core_ids=[0])
    return tuple(r.results[0][f"out_{name}"] for name, _ in _OUTS)
```

```python
from contextlib import ExitStack

import numpy as np
import concourse.bass as bass
from concourse import mybir

F32 = mybir.dt.float32
F32R = mybir.dt.float32r
ALU = mybir.AluOpType
ACT = mybir.ActivationFunctionType
AX = mybir.AxisListType

P = 128
D = 1024
KT = D // P
L = 2
G = 2
AH, AQK, AV = 4, 64, 128
BH, BNOPE, BROPE, BV = 4, 64, 32, 64
BQK = BNOPE + BROPE
BQL, BKVL = 256, 128
CCH, TAPS = 256, 31
PAD = TAPS // 2
POOLS = (2, 4, 8, 16)
DG, DCH = 64, 256
FFN, NE, ED = 2816, 8, 3584
EPS = 1e-6
GRID_W, THETA = 64, 10000.0

CQ, CK, CV, CBQ, CKV, CPE, CC, CD = 0, 512, 1024, 1536, 1792, 1920, 1952, 2464
CGATE = 2720
IN_CHUNKS = [(CC, 512), (CD, 256), (CBQ, 416), (CQ, 512), (CK, 512), (CV, 512)]
IN_C, IN_D, IN_B, IN_Q, IN_K, IN_V = range(6)
GATE_OF = [6, 4, 0, 2]
BR_ORDER = [2, 3, 1, 0]
GATE_CHUNKS = [(CGATE + D * b + 512 * i, 512) for b in BR_ORDER for i in range(2)]

RAW, HI = 6, 3
TW = 2048

N_BR = [2, 1, 1, 1]
N_OUT = 4


def mixed(units, extra):
    out, k = [], 0
    for i, u in enumerate(units):
        out.append(u)
        upto = len(extra) * (i + 1) // len(units)
        out += extra[k:upto]
        k = upto
    return out


def mixer_units(l):
    ada = [("ada", 0, c) for c in range(4, 12)] + [("ada", 1, c) for c in range(12)] if l == 0 else []
    ins = [("in", l, c) for c in range(6)]
    gate = [[("gate", l, 2 * j), ("gate", l, 2 * j + 1)] for j in range(4)]
    cut = [0, ADA_CUT[0], ADA_CUT[1], ADA_CUT[2], 20]
    part = [ada[cut[j]:cut[j + 1]] for j in range(4)]
    out = ins + mixed(gate[0], part[0])
    for j in range(4):
        if j:
            out += mixed(gate[j], part[j])
        out.append(("br", l, BR_ORDER[j]))
    return out


ADA_CUT = (2, 9, 14)
PRELUDE = [("ada", 0, c) for c in range(4)]
FCH = [(512 * j, 512) for j in range(5)] + [(2560, 256)]
N_FFN_UP = 5 * 4 + 2
N_FFN_DN = FFN // 256
N_FFN = N_FFN_UP + N_FFN_DN
ECH = [(512 * j, 512) for j in range(ED // 512)]
JOBS = NE + 3
N_EXP_UP = 4 * len(ECH)
N_EXP_DN = ED // 256
N_EXP = N_EXP_UP + N_EXP_DN


def stream_plan():
    first, number, t = {}, {}, 0
    for l in range(L):
        for u in (PRELUDE if l == 0 else []) + mixer_units(l):
            first[u] = t
            if u[0] != "br":
                number[u] = len(number)
            t += N_BR[u[2]] if u[0] == "br" else 2
        first["out", l] = t
        t += N_OUT
        first["ffn", l] = t
        if l == 0:
            t += N_FFN
    return first, number


FIRST, NUMBER = stream_plan()


def t_branch(l, b):
    return FIRST["br", l, b]


def t_branch_end(l, b):
    return FIRST["br", l, b] + N_BR[b]


def t_out(l):
    return FIRST["out", l]


def t_ffn(l):
    return FIRST["ffn", l]


ADA_COLS = {}
for _u in sorted(NUMBER, key=NUMBER.get):
    if _u[0] == "ada" and _u[2] // 2 not in (2, 5):
        ADA_COLS[_u] = len(ADA_COLS) + 1


def last_unit(l, b):
    order = mixer_units(l)
    return order[order.index(("br", l, b)) - 1]


def n_out(u):
    return 2 * (NUMBER[u] + 1)


def tile_floats(t):
    for l in range(L):
        for c, (_, width) in enumerate(IN_CHUNKS):
            if FIRST["in", l, c] <= t < FIRST["in", l, c] + 2:
                return 4 * width
    return TW


FILL = {
    "c_in": (2, 2), "c_glu": (2, 2), "d_pd": (1, 1), "c_conv": (6, 6), "c_ln": (3, 2), "c_op": (3, 2),
    "b_z0": (2, 1), "b_zT0": (0, 0), "b_up0": (4, 1), "b_T0": (1, 0), "b_sm0": (3, 1), "b_pT0": (1, 0), "b_o0": (1, 0),
    "b_z1": (2, 1), "b_zT1": (1, 0), "b_up1": (3, 1), "b_T1": (1, 0), "b_sm1": (3, 1), "b_pT1": (1, 1), "b_o1": (1, 0),
    "a_n0": (3, 1), "a_T0": (1, 0), "a_sm0": (3, 1), "a_wT0": (1, 0), "a_o0": (3, 1),
    "a_n1": (4, 1), "a_T1": (2, 0), "a_sm1": (3, 1), "a_wT1": (2, 1), "a_o1": (2, 1),
}


class Units:

    def __init__(self, units):
        self.todo = [(u, FIRST[u] + i, i == 0, i == 1) if u[0] != "br" else (u, FIRST[u], True, True)
                     for u in units for i in range(1 if u[0] == "br" else 2)]

    def take(self, n):
        out = []
        while self.todo and self.todo[0][0][0] != "br" and len(out) < n:
            out.append(self.todo.pop(0))
        return out

    def product(self, b):
        out = self.take(len(self.todo))
        if b is not None:
            assert self.todo.pop(0)[0][2] == b
        return out


C_ID, C_POOL, C_RA, C_RB, C_SEL, C_SELG, C_SELB, C_TRI = 0, 128, 640, 768, 832, 834, 1090, 1138
C_N = 1262
C_IOTA, C_BEFORE, C_ALL = C_N, C_N + P, C_N + 2 * P


def shape_tables():
    t = np.zeros((P, C_ALL), np.float32)
    t[:, C_ID:C_ID + P] = np.eye(P, dtype=np.float32)
    for i, w in enumerate(POOLS):
        left, right = w // 2, w - 1 - w // 2
        for q in range(P):
            lo, hi = max(q - left, 0), min(q + right + 1, P)
            t[lo:hi, C_POOL + i * P + q] = np.float32(1) / np.float32(hi - lo)
            t[q, C_POOL + i * P + q] -= np.float32(1)
    for base, dim in ((C_RA, AQK), (C_RB, BROPE)):
        nf = dim // 4
        freqs = np.float32(THETA) ** (-np.arange(nf, dtype=np.float32) / np.float32(nf))
        tok = np.arange(P)
        row, col = (tok // GRID_W).astype(np.float32), (tok % GRID_W).astype(np.float32)
        ang = np.concatenate([row[:, None] * freqs, col[:, None] * freqs], axis=1).astype(np.float32)
        cos, sin = np.cos(ang).astype(np.float32), np.sin(ang).astype(np.float32)
        t[:, base:base + dim] = np.repeat(cos, 2, axis=1)
        t[:, base + dim:base + 2 * dim:2] = -sin
        t[:, base + dim + 1:base + 2 * dim:2] = sin
    for g in range(G):
        for r in (g, g + 2):
            t[r, C_SEL + g] = 1
            for i in range(4):
                t[32 * i + r, C_SELG + g * P:C_SELG + (g + 1) * P] = 1
        for r in (g, g + 2):
            t[64 + r, C_SEL + g] = 1
    for j in range(12):
        for l in range(L):
            t[32 * l + j, C_SELB + 4 * j:C_SELB + 4 * j + 2] = 1
    for e in range(NE):
        t[:, C_TRI + e * NE:C_TRI + e * NE + e] = 1
    t[:, C_IOTA:C_IOTA + P] = np.arange(P)
    t[:, C_BEFORE:C_BEFORE + P] = np.triu(np.ones((P, P)), 1)
    return t


def trunk_kernel(nc, T, OUT):
    with ExitStack() as ctx:
        top = [-(-nc.sbuf_base // 32) * 32]

        def place(name, shape, dt=F32, at=None):
            size = 4 * int(np.prod(shape[1:]))
            off = top[0] if at is None else at
            if at is None:
                top[0] += -(-size // 32) * 32
            return nc.alloc_sbuf_tensor_at(name, shape, dt, offset=off)

        tab = place("tab", [P, C_N])
        colp = place("colp", [P, L, 82])
        ccol = place("ccol", [P, 16])
        sil = place("sil", [P, 2, 16])
        ada_hl = place("ada_hl", [P, 4 * KT + P], F32R)
        ada_h0 = place("ada_h0", [P, 4 * KT + P], F32R)
        gains = place("gains", [P, 1600])
        modcol = place("modcol", [P, L, 4, KT, G])
        grow = place("grow", [P, L, 512])
        adarow = place("adarow", [P, 512])
        stat = place("stat", [P, 128])
        x = place("x", [P, G, D])
        hT_hi = place("hT_hi", [P, KT, G, P], F32R)
        hT_lo = place("hT_lo", [P, KT, G, P], F32R)
        raw_at = top[0]
        raw = place("raw", [P, RAW, TW])
        lo = place("lo", [P, RAW, TW], F32R, at=raw_at)
        hi = place("hi", [P, HI, TW], F32R)
        region = top[0]

        gates_at = top[0]
        gates = place("gates", [P, G, 4 * D])
        proj_at = top[0]
        proj = place("proj", [P, G, CGATE])
        rowp = place("rowp", [P, L, P], at=proj_at)
        brT_hi = place("brT_hi", [P, 4, G, P], F32R)
        brT_lo = place("brT_lo", [P, 4, G, P], F32R)
        u_at = top[0]
        tmp1 = place("tmp1", [P, 1024])
        tmp2 = place("tmp2", [P, 1024])
        prob = place("prob", [P, 2048], at=u_at)
        q_at = top[0]
        qT = place("qT", [P, 4, P])
        kT = place("kT", [P, 4, 2, P])
        wT = place("wT", [P, 4, 2, P])
        o_sb = place("o_sb", [P, 512], at=q_at)
        kc_at = top[0]
        k_c = place("k_c", [P, 512])
        v_c = place("v_c", [P, 512])
        top[0] = kc_at + 4608
        qk96 = place("qk96", [P, 12, BQK], at=kc_at)
        v_b = place("v_b", [P, 2, BH, BV])
        uq_w = place("uq_w", [P, 2, BH * BQK])
        ukv_w = place("ukv_w", [P, 512])
        dg_w = place("dg_w", [P, 2, DG], at=kc_at + 4096)
        ckv_c = place("ckv_c", [P, BKVL])
        kpe_c = place("kpe_c", [P, BROPE])
        glu_p = place("glu_p", [P, 2, G, P + 2 * PAD], at=q_at)
        conv = place("conv", [P, 2, G, P], at=q_at + 4 * 2 * G * (P + 2 * PAD))
        lnz = place("lnz", [P, G, CCH], at=q_at + 8192)
        pdT = place("pdT", [P, G, 2, P], at=kc_at)
        hdT = place("hdT", [P, 2, G, P], at=kc_at + 2048)
        end_mix = top[0]

        top[0] = region
        xsq = place("xsq", [P, G, D])
        diag = place("diag", [P, G, P])
        top[0] = region
        hidT_hi = place("hidT_hi", [P, FFN // P, G, P], F32R)
        hidT_lo = place("hidT_lo", [P, FFN // P, G, P], F32R)
        hfT = place("hfT", [P, G, KT, P])
        hfT_at = top[0]
        silu_s = place("silu_s", [P, G, 512])
        hid = place("hid", [P, G, 512])
        gbc = place("gbc", [P, G, D])
        top[0] = region
        hidE_hi = place("hidE_hi", [P, ED // P, P], F32R)
        hidE_lo = place("hidE_lo", [P, ED // P, P], F32R)
        xg_hi = place("xg_hi", [P, KT, P], F32R)
        xg_lo = place("xg_lo", [P, KT, P], F32R)
        pick = place("pick", [P, G, P], F32R)
        pickT = place("pickT", [P, G, P], F32R)
        assert top[0] <= hfT_at
        top[0] = hfT_at + 4 * (2 * G * 512 + G * D)
        silu_e = place("silu_e", [P, 2, 512], at=hfT_at)
        hid_e = place("hid_e", [P, 2, 512], at=hfT_at + 4096)
        yacc = place("yacc", [P, G, D])
        ye_hi = place("ye_hi", [P, D], F32R)
        ye_lo = place("ye_lo", [P, D], F32R)
        etab = place("etab", [P, 2 * P])
        router = place("router", [P, KT, NE])
        rtmp = place("rtmp", [P, G, 320])
        job_pos = place("job_pos", [P, G, JOBS + 1])
        job_comb = place("job_comb", [P, G, JOBS + 1])
        job_int = place("job_int", [P, 4], mybir.dt.int32)
        ones = place("ones", [P, P])
        assert max(top[0], end_mix) <= nc.sbuf_usable_end, (top[0], end_mix, nc.sbuf_usable_end)

        B = ctx.enter_context(nc.psum_tensor("B", [P, 4, 512], F32))
        X = ctx.enter_context(nc.psum_tensor("X", [P, 4, 512], F32))

        ident = tab[:, C_ID:C_ID + P]
        mg = [gates[:, g, 2 * D:3 * D] for g in range(G)]
        GAIN = {}
        at = 0
        for name, n in (("qk", 128), ("lam", 256), ("sub", 128), ("bql", 256), ("bkvl", 128),
                        ("bqk", 192), ("lng", 256), ("lnb", 256)):
            GAIN[name] = gains[:, at:at + n]
            at += n
        ssq = stat[:, 0:2]
        rstd = stat[:, 2:4]
        neg_half = stat[:, 4:20]
        nst16 = stat[:, 20:36]
        rst16 = stat[:, 36:52]
        mx = stat[:, 52:60]
        nmx = stat[:, 60:68]
        rsum = stat[:, 68:76]
        rinv = stat[:, 76:84]
        lam2 = stat[:, 84:86]
        lamx = stat[:, 86:88]
        neglam = stat[:, 88:89]
        zsum = stat[:, 92:94]
        bnst = stat[:, 96:108]
        mv = stat[:, 108:112]
        rln = stat[:, 112:114]

        S = {}
        for name in (
            "tab_in c_in rows_in x_in router_in prm_in0 prm_in1 adab_in kv_in0 kv_in1 bw_in0 bw_in1 kv_stored ckv_stored y_stored "
            "raw_in0 raw_in1 raw_in2 raw_in3 raw_in4 raw_in5 hi_ready lo_ready tile_used "
            "dve_order pool_order "
            "cols_psum cols_sb sil_th ada_st ada_row ada_cols mod_ready "
            "sumsq rstd_ready diag_ready xn_T hf_ready hf1_ready hT_hi_ready hT_lo_ready half_set group_0_done "
            "unit_out "
            "a_sq a_nst a_rstd a_qk a_roped a_T a_T_sb a_scores a_nmx a_exp a_w a_wT a_wT_sb a_o a_osq a_ost "
            "a_orstd a_on a_oT lam_p lam_e lam_ready "
            "b_zsq b_zrstd b_z b_zT b_zT_sb b_up b_up_sb b_heads b_kpe b_sq b_nst b_rstd b_qk b_T b_T_sb b_scores b_nmx "
            "b_exp b_p b_pT b_pT_sb b_o b_o_sb b_oT "
            "c_th c_glu c_T c_T_sb c_conv c_back c_mv c_rstd c_z c_zth c_act c_zT glu_zero "
            "d_pd d_pd_sb d_hd d_hd_sb "
            "br_hi br_lo br_used a_gated mg_ready mg_T gb_psum gb_sb x_ready "
            "silu_ready hid_ready hid_T hid_hi hid_lo r_psum r_diff r_exp r_mask r_pos jobs_ready "
            "h_tok h_tok_hi h_tok_lo pick_ready pickT_psum pickT_sb xg_psum xg_ready e_silu e_hid e_hidT e_hid_hi e_hid_lo ye_hi_ready ye_lo_ready ys_psum ys_used"
        ).split():
            S[name] = ctx.enter_context(nc.semaphore(name))
        RAW_IN = [S[f"raw_in{s}"] for s in range(RAW)]
        block = ctx.enter_context(nc.Block())

        def quarter(buf, q):
            return buf[:, 4 * (q // 2):4 * (q // 2) + 4, q % 2, :]

        def x_bank(q):
            return X[:, 2 * (q % 2) + q // 2, :]

        def w_tile(w, k0, nk, c0, width):
            return w[k0 * P:(k0 + nk) * P, c0:c0 + width].rearrange("(k p) n -> p k n", p=P)

        def unit_tiles(u):
            kind, l, c = u
            if kind == "br":
                w = T[("a_w_o", "b_w_o", "c_w_o", "d_w_o")[c]][l]
                return [w_tile(w, 2 * i, 2, 0, D) for i in range(N_BR[c])]
            if kind == "ada":
                w, c0, width = T["ada_w"][l], 512 * c, 512
            else:
                w = T["w_in"][l]
                c0, width = (IN_CHUNKS if kind == "in" else GATE_CHUNKS)[c]
            return [w_tile(w, 4 * half, 4, c0, width) for half in range(2)]

        def layer_tiles(l):
            for u in (PRELUDE if l == 0 else []) + mixer_units(l):
                yield from unit_tiles(u)
            for i in range(N_OUT):
                yield w_tile(T["w_out"][l], 2 * i, 2, 0, D)

        def load_rows(eng, l):
            items = [(0, 8, T["norm1_g"][l].rearrange("(r p) -> r p", p=P)),
                     (8, 8, T["norm2_g"][l].rearrange("(r p) -> r p", p=P)),
                     (16, 2, T["c_dw_b"][l].rearrange("(r p) -> r p", p=P)),
                     (18, 2, T["d_scale"][l].rearrange("(r p) -> r p", p=P)),
                     (20, 62, T["c_dw"][l].rearrange("k (r p) -> (k r) p", p=P))]
            for r0, n, ap in items:
                eng.dma_start(rowp[r0:r0 + n, l, :], ap).then_inc(S["rows_in"], 16)

        def ffn_tiles():
            for c0, width in FCH:
                for w in ("ffn_w1", "ffn_w3"):
                    nk = TW // width
                    for i in range(KT // nk):
                        yield w_tile(T[w][0], nk * i, nk, c0, width)
            for i in range(N_FFN_DN):
                yield w_tile(T["ffn_w2"][0], 2 * i, 2, 0, D)

        def tile_view(buf, slot, ap):
            _, nk, width = ap.shape
            return buf[:, slot, 0:nk * width].rearrange("p (k n) -> p k n", n=width)

        @block.sync
        def _(sp):
            t = 0

            def load(ap, t, e=None):
                s = t % RAW
                if e is None:
                    if t >= RAW:
                        sp.wait_ge(S["tile_used"], t - RAW + 1)
                else:
                    sp.wait_ge(S["tile_used"], e * N_EXP + (t - RAW + 1))
                sp.dma_start(tile_view(raw, s, ap), ap).then_inc(RAW_IN[s], 16)

            for r0, v in ((96, T["c_ctx"]), (104, T["c"][0])):
                sp.dma_start(rowp[r0:r0 + 8, 0, :], v.rearrange("(r p) -> r p", p=P)).then_inc(S["c_in"], 16)
            sp.dma_start(tab[:], T["tables"][:, 0:C_N]).then_inc(S["tab_in"], 16)
            for l in range(L):
                for ap in layer_tiles(l):
                    if t == HI:
                        sp.dma_start(x[:, 0, :], T["x_prompt"][0]).then_inc(S["x_in"], 16)
                        sp.dma_start(x[:, 1, :], T["x_sample"][0]).then_inc(S["x_in"], 16)
                    load(ap, t)
                    t += 1
                if l == 0:
                    for ap in ffn_tiles():
                        load(ap, t)
                        t += 1
            w1 = T["moe_w1"].rearrange("a e k n -> (a e k) n")
            w3 = T["moe_w3"].rearrange("a e k n -> (a e k) n")
            w2 = T["moe_w2"].rearrange("a e k n -> (a e k) n")

            def load_expert(job, expert):
                tt = t
                for c0, width in ECH:
                    for w in (w1, w3):
                        for half in range(2):
                            rows = w[bass.ds(expert * D + half * 512, 512), c0:c0 + width]
                            load(rows.rearrange("(k p) n -> p k n", p=P), tt, job)
                            tt += 1
                for i in range(N_EXP_DN):
                    rows = w2[bass.ds(expert * ED + i * 256, 256), :]
                    load(rows.rearrange("(k p) n -> p k n", p=P), tt, job)
                    tt += 1

            with sp.Fori(0, NE) as e:
                load_expert(e, e)
            sp.wait_ge(S["jobs_ready"], 1)
            n_jobs = sp.value_load(job_int[0:1, 0:1], min_val=NE, max_val=JOBS)
            for k in range(JOBS - NE):
                with sp.If(n_jobs > NE + k):
                    load_expert(NE + k, sp.value_load(job_int[0:1, 1 + k:2 + k], min_val=0, max_val=NE - 1))

        @block.gpsimd
        def _(pool):
            order = [0]

            def chain(ins):
                order[0] += 1
                ins.then_inc(S["pool_order"], 1)
                pool.wait_ge(S["pool_order"], order[0])

            def row(ap):
                return ap.partition_broadcast(P)

            pool.memset(neg_half, -0.5).then_inc(S["half_set"], 1)
            pool.wait_ge(S["half_set"], 1)

            def load_layer(l):
                at = 0
                for name, n in (("a_q_norm", 64), ("a_k_norm", 64), ("a_lambda", 256), ("a_sub_norm", 128),
                                ("b_q_lora_norm", 256), ("b_kv_lora_norm", 128), ("b_q_norm", 96),
                                ("b_k_norm", 96), ("c_ln_g", 256), ("c_ln_b", 256)):
                    src = T[name][l]
                    if len(src.shape) == 2:
                        src = src.rearrange("a n -> (a n)")
                    pool.dma_start(gains[:, at:at + n], row(src)).then_inc(S[f"prm_in{l}"], 16)
                    at += n

            def load_b_weights(l):
                pool.dma_start(uq_w[:], T["b_w_uq"][l].rearrange("(k p) n -> p k n", p=P)).then_inc(S[f"bw_in{l}"], 16)
                pool.dma_start(ukv_w[:], T["b_w_ukv"][l]).then_inc(S[f"bw_in{l}"], 16)
                for i in range(4):
                    pool.dma_start(dg_w[64 * (i % 2):64 * (i % 2) + 64, i // 2, :],
                                   T["d_w_group"][l, i]).then_inc(S[f"bw_in{l}"], 16)
                pool.dma_start(ckv_c[:], T["cache_b_ckv"][0, l]).then_inc(S[f"bw_in{l}"], 16)
                pool.dma_start(kpe_c[:], T["cache_b_kpe"][0, l]).then_inc(S[f"bw_in{l}"], 16)

            def load_kv(l):
                pool.dma_start(k_c[:], T["cache_a_k"][0, l].rearrange("t h d -> t (h d)")).then_inc(S[f"kv_in{l}"], 16)
                pool.dma_start(v_c[:], T["cache_a_v"][0, l].rearrange("t h d -> t (h d)")).then_inc(S[f"kv_in{l}"], 16)

            def power(out, in_, width, inv_n):
                chain(pool.tensor_scalar(out, in_, inv_n, EPS, ALU.mult, ALU.add))
                return pool.tensor_tensor(out, out, neg_half[:, 0:width], ALU.pow)

            def norm(i):
                g = i % G
                pool.wait_ge(S["sumsq"], i + 1)
                power(rstd[:, g:g + 1], ssq[:, g:g + 1], 1, 1.0 / D).then_inc(S["rstd_ready"], 1)

            for l in range(L):
                for g in range(G):
                    norm(4 * l + g)
                if l == 0:
                    load_layer(0)
                    load_b_weights(0)
                pool.wait_ge(S["c_mv"], l + 1)
                for g in range(G):
                    ins = power(rln[:, g:g + 1], mv[:, 2 * g + 1:2 * g + 2], 1, 1.0)
                    if g == G - 1:
                        ins.then_inc(S["c_rstd"], 1)
                    else:
                        chain(ins)
                for g in range(G):
                    u = l * G + g
                    pool.wait_ge(S["b_zsq"], 2 * u + 2)
                    chain(pool.tensor_scalar(zsum[:, 0:1], zsum[:, 0:1], float(BKVL) / BQL, None, ALU.mult))
                    power(zsum, zsum, 2, 1.0 / BKVL).then_inc(S["b_zrstd"], 1)
                    if g == 0:
                        pool.wait_ge(S["unit_out"], n_out(("in", l, IN_B)))
                        pool.dma_start(OUT["kpe"][0, l], proj[:, 0, CPE:CPE + BROPE]).then_inc(S["ckv_stored"], 16)
                        pool.wait_ge(S["b_z"], u + 1)
                        pool.dma_start(OUT["ckv"][0, l], proj[:, 0, CKV:CKV + BKVL]).then_inc(S["ckv_stored"], 16)
                    nh = 8 if g == 0 else 12
                    pool.wait_ge(S["b_nst"], u + 1)
                    power(rst16[:, 0:nh], nst16[:, 0:nh], nh, 1.0 / BQK).then_inc(S["b_rstd"], 1)
                pool.wait_ge(S["b_T"], 2 * l + 2)
                load_kv(l)
                for g in range(G):
                    u = l * G + g
                    pool.wait_ge(S["a_nst"], u + 1)
                    power(rst16, nst16, 16, 1.0 / AQK).then_inc(S["a_rstd"], 1)
                    if g == 0:
                        pool.wait_ge(S["unit_out"], n_out(("in", l, IN_V)))
                        pool.dma_start(OUT["av"][0, l].rearrange("t h d -> t (h d)"),
                                       proj[:, 0, CV:CV + 512]).then_inc(S["kv_stored"], 16)
                        pool.wait_ge(S["a_qk"], u + 1)
                        pool.dma_start(OUT["ak"][0, l].rearrange("t h d -> t (h d)"),
                                       proj[:, 0, CK:CK + 512]).then_inc(S["kv_stored"], 16)
                    pool.wait_ge(S["a_ost"], u + 1)
                    power(rst16[:, 0:4], nst16[:, 0:4], 4, 1.0 / AV).then_inc(S["a_orstd"], 1)
                if l == 0:
                    pool.wait_ge(S["a_on"], 2)
                    load_layer(1)
                    load_b_weights(1)
                pool.wait_ge(S["kv_stored"], 32 * (l + 1))
                pool.wait_ge(S["ckv_stored"], 32 * (l + 1))
                for g in range(G):
                    norm(4 * l + 2 + g)
                if l == 1:
                    pool.dma_start(router[:], T["moe_router"][0].rearrange("(k p) e -> p k e", p=P)).then_inc(
                        S["router_in"], 16)
                    pool.dma_start(etab[:], T["tables"][:, C_IOTA:C_ALL]).then_inc(S["router_in"], 16)
            pool.wait_ge(S["x_ready"], 7)
            pool.dma_start(OUT["y_prompt"][0], x[:, 0, :]).then_inc(S["y_stored"], 16)
            pool.wait_ge(S["x_ready"], 8)
            pool.dma_start(OUT["y_sample"][0], x[:, 1, :]).then_inc(S["y_stored"], 16)
            pool.wait_ge(S["kv_stored"], 32 * L)
            pool.wait_ge(S["ckv_stored"], 32 * L)
            pool.wait_ge(S["y_stored"], 32)

        @block.scalar
        def _(act):
            split_next = [0]
            def split_hi(t, e=None):
                s, h = t % RAW, t % HI
                if e is None:
                    act.wait_ge(RAW_IN[s], 16 * (t // RAW + 1))
                    if t >= HI:
                        act.wait_ge(S["tile_used"], t - HI + 1)
                else:
                    act.wait_ge(RAW_IN[s], e * (16 * N_EXP // RAW) + 16 * (t // RAW + 1))
                    act.wait_ge(S["tile_used"], e * N_EXP + (t - HI + 1))
                n = tile_floats(t)
                act.copy(hi[:, h, 0:n], raw[:, s, 0:n]).then_inc(S["hi_ready"], 1)

            def split_to(t):
                while split_next[0] < t:
                    split_hi(split_next[0])
                    split_next[0] += 1

            def norm_sums(i):
                g = i % G
                if i % 4 >= 2:
                    act.wait_ge(S["x_ready"], 4 * (i // 4) + 1 + g)
                elif i < 4:
                    act.wait_ge(S["x_in"], 32)
                else:
                    act.wait_ge(S["x_ready"], 4 * (i // 4) - 2 + 1 + g)
                act.activation(xsq[:, g, :], x[:, g, :], ACT.Square,
                               accum_out=ssq[:, g:g + 1]).then_inc(S["sumsq"], 1)

            def norm_operand(i):
                n, l, which = i // 2, i // 4, i % 4 // 2
                act.wait_ge(S["mod_ready"], n + 1)
                for q in range(4):
                    if q % 2:
                        act.wait_ge(S["xn_T"], 4 * n + q + 1)
                        for k in range(4):
                            kk = 4 * (q // 2) + k
                            ins = act.activation(hfT[:, 1, kk, :], x_bank(q)[:, k * P:(k + 1) * P], ACT.Identity,
                                                 scale=modcol[:, l, 2 * which + 1, kk, 1:2],
                                                 bias=modcol[:, l, 2 * which, kk, 1:2])
                        ins.then_inc(S["hf1_ready"], 1)
                    if i == 6:
                        continue
                    if q % 2:
                        act.wait_ge(S["hf1_ready"], 2 * n + q // 2 + 1)
                    else:
                        act.wait_ge(S["hf_ready"], 2 * n + q // 2 + 1)
                    act.copy(quarter(hT_hi, q), hfT[:, q % 2, 4 * (q // 2):4 * (q // 2) + 4, :]).then_inc(
                        S["hT_hi_ready"], 1)

            def ada_cols_out(u):
                _, lu, c = u
                n = NUMBER[u]
                act.wait_ge(S["ada_cols"], ADA_COLS[u])
                slot = {0: 0, 1: 1, 3: 2, 4: 3}[c // 2]
                act.copy(modcol[:, lu, slot, 4 * (c % 2):4 * (c % 2) + 4, :],
                         B[:, 2 * (n % 2) + 1, 0:8].rearrange("p (k g) -> p k g", g=G)).then_inc(S["unit_out"], 2)

            def unit_evac(u):
                kind, lu, c = u
                n = NUMBER[u]
                act.wait_ge(S["tile_used"], FIRST[u] + 2)
                if kind == "ada":
                    row = B[0:4, 2 * (n % 2), :]
                    if c // 2 in (2, 5):
                        r = 32 * ((c // 2 == 5) * 2 + c % 2)
                        act.copy(grow[r:r + 4, lu, :], row).then_inc(S["unit_out"], 2)
                    else:
                        act.copy(adarow[64:68, :], row).then_inc(S["ada_row"], 1)
                    return
                for g in range(G):
                    bank = B[:, 2 * (n % 2) + g, :]
                    if kind == "in":
                        c0, width = IN_CHUNKS[c]
                        act.copy(proj[:, g, c0:c0 + width], bank[:, 0:width]).then_inc(S["unit_out"], 1)
                    else:
                        gc = GATE_CHUNKS[c][0] - CGATE
                        act.activation(gates[:, g, gc:gc + 512], bank, ACT.Tanh, scale=0.5).then_inc(S["unit_out"], 1)

            full, rows = [None], [None]

            def evac_pending():
                if full[0]:
                    unit_evac(full[0])
                    rows[0] = full[0] if full[0] in ADA_COLS else None
                    full[0] = None

            def cols_pending():
                if rows[0]:
                    ada_cols_out(rows[0])
                    rows[0] = None

            def run(tiles):
                for u, t, first, last in tiles:
                    split_to(t + HI)
                    if first:
                        evac_pending()
                    else:
                        cols_pending()
                    if last:
                        full[0] = u

            def finish_units():
                evac_pending()
                cols_pending()

            for l in range(L):
                act.dma_start(adarow[32 * l:32 * l + 12, :], T["ada_b"][l].rearrange("(r n) -> r n", n=512)).then_inc(
                    S["adab_in"], 16)
            for l in range(L):
                load_rows(act, l)
            for l in range(L):
                if l == 0:
                    act.wait_ge(S["cols_psum"], 1)
                    act.copy(ccol[:], X[:, 0, 0:16]).then_inc(S["cols_sb"], 1)
                    act.wait_ge(S["cols_sb"], 1)
                    act.activation(sil[:, 0, :], ccol[:], ACT.Tanh, scale=0.5).then_inc(S["sil_th"], 1)
                    split_to(HI)
                    prelude = Units(PRELUDE)
                    run(prelude.take(2))
                    for g in range(G):
                        norm_sums(g)
                    run(prelude.take(1))
                    act.wait_ge(S["cols_psum"], 2)
                    act.copy(colp[:], X[:, 3, 0:82 * L].rearrange("p (l n) -> p l n", l=L)).then_inc(S["cols_sb"], 1)
                    run(prelude.take(5))
                    split_to(8 + HI)
                    finish_units()
                else:
                    for g in range(G):
                        norm_sums(4 * l + g)
                norm_operand(4 * l)

                units = Units(mixer_units(l))

                def fill(step):
                    run(units.take(FILL[step][l]))

                def branch_product(b):
                    run(units.product(b))
                    finish_units()
                    split_to(t_branch(l, b) + HI)

                fill("c_in")
                evac_pending()
                act.wait_ge(S["unit_out"], n_out(("in", l, IN_C)))
                for g in range(G):
                    act.activation(tmp2[:, g * 256:(g + 1) * 256], proj[:, g, CC + CCH:CC + 2 * CCH], ACT.Tanh,
                                   scale=0.5).then_inc(S["c_th"], 1)
                fill("c_glu")
                evac_pending()
                act.wait_ge(S["c_T"], l + 1)
                act.wait_ge(S["glu_zero"], l + 1)
                for g in range(G):
                    act.activation(glu_p[:, :, g, PAD:PAD + P],
                                   X[:, 0, g * 256:(g + 1) * 256].rearrange("p (c t) -> p c t", c=2), ACT.Copy,
                                   scale=0.5).then_inc(S["c_T_sb"], 1)
                act.wait_ge(S["d_pd"], l + 1)
                act.copy(pdT[:].rearrange("p g k t -> p (g k t)"), X[:, 3, :]).then_inc(S["d_pd_sb"], 1)
                fill("d_pd")
                act.wait_ge(S["d_hd"], l + 1)
                for k in range(2):
                    ins = act.activation(hdT[:, k, :, :],
                                         X[:, 0, :].rearrange("p (g k t) -> p k g t", g=G, k=2)[:, k],
                                         ACT.Copy, scale=colp[:, l, 18 + k:19 + k])
                    ins.then_inc(S["d_hd_sb"], 1)
                act.wait_ge(S["d_hd_sb"], 2 * l + 2)
                for g in range(G):
                    act.copy(brT_hi[:, 2:4, g, :], hdT[:, :, g, :]).then_inc(S["br_hi"], 1)
                fill("c_conv")
                fill("c_ln")
                act.wait_ge(S["c_z"], l + 1)
                act.activation(tmp2[:, 0:512], lnz[:].rearrange("p g n -> p (g n)"), ACT.Tanh,
                               scale=0.5).then_inc(S["c_zth"], 1)
                fill("c_op")
                act.wait_ge(S["c_zT"], l + 1)
                for g in range(G):
                    act.activation(brT_hi[:, 0:2, g, :],
                                   X[:, 2 + g, 0:256].rearrange("p (h t) -> p h t", h=2), ACT.Copy,
                                   scale=0.5).then_inc(S["br_hi"], 1)
                act.wait_ge(S["unit_out"], n_out(("in", l, IN_B)))
                for g in range(G):
                    u = l * G + g
                    nk = 1 + g
                    act.activation(tmp1[:, 0:BQL], proj[:, g, CBQ:CBQ + BQL], ACT.Square,
                                   accum_out=zsum[:, 0:1]).then_inc(S["b_zsq"], 1)
                    act.activation(tmp1[:, BQL:BQL + BKVL], proj[:, g, CKV:CKV + BKVL], ACT.Square,
                                   accum_out=zsum[:, 1:2]).then_inc(S["b_zsq"], 1)
                    fill(f"b_z{g}")
                    act.wait_ge(S["b_zT"], u + 1)
                    zT = wT[:].rearrange("p a b t -> p (a b) t")[:, 0:4, :]
                    act.copy(zT[:, 0:3 + g, :], X[:, 0, 0:(3 + g) * P].rearrange("p (j t) -> p j t", t=P)).then_inc(
                        S["b_zT_sb"], 1)
                    fill(f"b_zT{g}")
                    act.wait_ge(S["b_up"], u + 1)
                    act.copy(qk96[:, 0:4, :], X[:, 1, 0:384].rearrange("p (h d) -> p h d", h=4))
                    for j in range(nk):
                        kv = X[:, 2 + j, :].rearrange("p (h d) -> p h d", h=4)
                        act.copy(qk96[:, 4 + 4 * j:8 + 4 * j, 0:BNOPE], kv[:, :, 0:BNOPE])
                        ins = act.copy(v_b[:, j, :, :], kv[:, :, BNOPE:BNOPE + BV])
                    ins.then_inc(S["b_heads"], 1)
                    act.wait_ge(S["b_heads"], u + 1)
                    act.wait_ge(S["b_kpe"], u + 1)
                    nh = 4 + 4 * nk
                    act.activation(prob[:, 0:nh * BQK], qk96[:, 0:nh, :].rearrange("p h d -> p (h d)"),
                                   ACT.Square).then_inc(S["b_sq"], 1)
                    branch_product(2 if g == 0 else 3)
                    fill(f"b_up{g}")
                    act.wait_ge(S["b_T"], u + 1)
                    act.copy(qT[0:BQK, :, :], X[0:BQK, 0, :].rearrange("p (h t) -> p h t", h=4))
                    for j in range(nk):
                        ins = act.copy(kT[0:BQK, :, j, :], X[0:BQK, 1 + j, :].rearrange("p (h t) -> p h t", h=4))
                    ins.then_inc(S["b_T_sb"], 1)
                    fill(f"b_T{g}")
                    act.wait_ge(S["b_nmx"], u + 1)
                    Xs = X[:, 0:2, :].rearrange("p b (h k) -> p (b h) k", k=256)
                    pv = prob[:].rearrange("p (h k) -> p h k", k=256)
                    for h in range(BH):
                        ins = act.activation(pv[:, h, 0:nk * P], Xs[:, h, 0:nk * P], ACT.Exp, bias=nmx[:, h:h + 1],
                                             scale=BQK ** -0.5, accum_out=rsum[:, h:h + 1])
                    ins.then_inc(S["b_exp"], 1)
                    fill(f"b_sm{g}")
                    act.wait_ge(S["b_pT"], u + 1)
                    act.copy(wT[:, :, 0:nk, :],
                             X[:, 2:4, :].rearrange("p b (h j t) -> p (b h) j t", h=2, j=2)[:, :, 0:nk, :]).then_inc(
                        S["b_pT_sb"], 1)
                    fill(f"b_pT{g}")
                    act.wait_ge(S["b_o"], u + 1)
                    act.copy(o_sb[:, 0:256], X[:, 0, 0:256]).then_inc(S["b_o_sb"], 1)
                    fill(f"b_o{g}")
                    act.wait_ge(S["b_oT"], u + 1)
                    if g == 0:
                        act.wait_ge(S["tile_used"], t_branch_end(l, 2))
                    act.copy(brT_hi[:, 0:2, g, :], X[:, 1, 0:256].rearrange("p (h t) -> p h t", h=2)).then_inc(
                        S["br_hi"], 1)
                act.wait_ge(S["unit_out"], n_out(("in", l, IN_K)))
                for g in range(G):
                    u = l * G + g
                    nk = 1 + g
                    act.activation(tmp1[:], proj[:, g, 0:1024], ACT.Square).then_inc(S["a_sq"], 1)
                    if g == 0:
                        act.wait_ge(S["lam_p"], l + 1)
                        act.activation(lamx, lam2, ACT.Exp).then_inc(S["lam_e"], 1)
                        branch_product(1)
                    fill(f"a_n{g}")
                    act.wait_ge(S["a_T"], u + 1)
                    act.copy(qT[:], X[:, 0, :].rearrange("p (h t) -> p h t", h=4))
                    for j in range(nk):
                        ins = act.copy(kT[:, :, j, :], X[:, 1 + j, :].rearrange("p (h t) -> p h t", h=4))
                    ins.then_inc(S["a_T_sb"], 1)
                    fill(f"a_T{g}")
                    act.wait_ge(S["a_nmx"], u + 1)
                    Xs = X[:, :, :].rearrange("p b (h k) -> p (b h) k", k=256)
                    pv = prob[:].rearrange("p (h k) -> p h k", k=256)
                    for h in range(8):
                        ins = act.activation(pv[:, h, 0:nk * P], Xs[:, h, 0:nk * P], ACT.Exp, bias=nmx[:, h:h + 1],
                                             scale=AQK ** -0.5, accum_out=rsum[:, h:h + 1])
                    ins.then_inc(S["a_exp"], 1)
                    fill(f"a_sm{g}")
                    act.wait_ge(S["a_wT"], u + 1)
                    act.copy(wT[:, :, 0:nk, :],
                             X[:, 0:2, :].rearrange("p b (h j t) -> p (b h) j t", h=2, j=2)[:, :, 0:nk, :]).then_inc(
                        S["a_wT_sb"], 1)
                    fill(f"a_wT{g}")
                    act.wait_ge(S["a_o"], u + 1)
                    act.activation(tmp1[:, 0:512], X[:, 2, :], ACT.Square).then_inc(S["a_osq"], 1)
                    fill(f"a_o{g}")
                    act.wait_ge(S["a_oT"], u + 1)
                    if g == 0:
                        act.wait_ge(S["tile_used"], t_branch_end(l, 1))
                    act.copy(brT_hi[:, :, g, :], X[:, 3, :].rearrange("p (h t) -> p h t", h=4)).then_inc(S["br_hi"], 1)
                branch_product(0)
                split_to(t_out(l) + HI - 1)
                for q in range(4):
                    act.wait_ge(S["mg_T"], 4 * l + q + 1)
                    act.activation(quarter(hT_hi, q), x_bank(q).rearrange("p (k t) -> p k t", t=P), ACT.Copy,
                                   scale=0.5).then_inc(S["hT_hi_ready"], 1)

                def gate_rows(which, bank=X):
                    act.wait_ge(S["gb_psum"], 2 * l + which + 1)
                    for g in range(G):
                        act.copy(gbc[:, g, :], bank[:, 2 * g:2 * g + 2, :].rearrange("p b n -> p (b n)")).then_inc(
                            S["gb_sb"], 1)

                split_to(t_out(l) + N_OUT)
                gate_rows(0)
                if l == 0:
                    split_to(t_ffn(0) + HI)
                for g in range(G):
                    norm_sums(4 * l + 2 + g)
                norm_operand(4 * l + 2)

                def hid_hi(cnt, j, width):
                    act.wait_ge(S["hid_T"], cnt)
                    nb = width // P
                    for g in range(G):
                        act.copy(hidT_hi[:, 4 * j:4 * j + nb, g, :],
                                 X[:, g, 0:width].rearrange("p (k t) -> p k t", t=P)).then_inc(S["hid_hi"], 1)

                if l == 0:
                    tf = t_ffn(0)
                    split_to(tf + HI)
                    for j, (c0, width) in enumerate(FCH):
                        w1_end = tf + 4 * j + (2 if width == 512 else 1)
                        w3_end = tf + 4 * j + (4 if width == 512 else 2)
                        split_to(w1_end + HI)
                        act.wait_ge(S["tile_used"], w1_end)
                        if j:
                            act.wait_ge(S["hid_ready"], 2 * j)
                        for g in range(G):
                            act.activation(silu_s[:, g, 0:width], B[:, g, 0:width], ACT.Silu).then_inc(
                                S["silu_ready"], 1)
                        split_to(w3_end + HI)
                        hid_hi(j + 1, j, width)
                    split_to(tf + N_FFN_UP + HI)
                    gate_rows(1)
                    split_to(tf + N_FFN + HI)
                else:
                    gate_rows(1, B)
                    act.wait_ge(S["r_diff"], 1)
                    act.activation(rtmp[:, :, 80:81], rtmp[:, :, 81:82], ACT.Exp).then_inc(S["r_exp"], 1)
                    for g in range(G):
                        act.wait_ge(S["h_tok"], g + 1)
                        act.copy(hT_hi[:, :, g, :],
                                 B[:, 2 * g:2 * g + 2, :].rearrange("p b (k t) -> p (b k) t", t=P)).then_inc(
                            S["h_tok_hi"], 1)

                    def gathered_hi(count):
                        act.wait_ge(S["xg_psum"], count)
                        act.copy(xg_hi[:], B[:, 0:2, :].rearrange("p b (k t) -> p (b k) t", t=P)).then_inc(
                            S["xg_ready"], 1)

                    gathered_hi(2)
                    t0e = t_ffn(1)
                    nch = len(ECH)
                    act.wait_ge(S["jobs_ready"], 1)
                    n_jobs = act.value_load(job_int[0:1, 0:1], min_val=NE, max_val=JOBS)
                    with act.Fori(0, n_jobs) as e:
                        nxt = [t0e]

                        def esplit(upto):
                            while nxt[0] < min(upto, t0e + N_EXP):
                                split_hi(nxt[0], e)
                                nxt[0] += 1

                        def hid_hi_e(j):
                            act.wait_ge(S["e_hidT"], e * nch + (j + 1))
                            act.copy(hidE_hi[:, 4 * j:4 * j + 4, :],
                                     X[:, j % 2, :].rearrange("p (k t) -> p k t", t=P)).then_inc(S["e_hid_hi"], 1)

                        esplit(t0e + HI)
                        act.wait_ge(S["tile_used"], e * N_EXP + t0e)
                        act.copy(ye_hi[:], X[:, 2:4, :].rearrange("p b n -> p (b n)")).then_inc(S["ye_hi_ready"], 1)
                        for j in range(nch):
                            esplit(t0e + 4 * j + 2 + HI)
                            act.wait_ge(S["tile_used"], e * N_EXP + (t0e + 4 * j + 2))
                            if j >= 2:
                                act.wait_ge(S["e_hid"], e * nch + (j - 1))
                            act.activation(silu_e[:, j % 2, :], B[:, 2 * (j % 2), :], ACT.Silu).then_inc(S["e_silu"], 1)
                            if j:
                                hid_hi_e(j - 1)
                            esplit(t0e + 4 * j + 4 + HI)
                            if j == 2:
                                act.wait_ge(S["pickT_psum"], e + 1)
                                act.copy(pickT[:], X[:, 2, 0:256].rearrange("p (g t) -> p g t", g=G)).then_inc(
                                    S["pickT_sb"], 1)
                        hid_hi_e(nch - 1)
                        gathered_hi(e * 2 + 4)
                        esplit(t0e + N_EXP)
                    act.wait_ge(S["tile_used"], n_jobs * N_EXP + t0e)
                    act.copy(ye_hi[:], X[:, 2:4, :].rearrange("p b n -> p (b n)")).then_inc(S["ye_hi_ready"], 1)

        @block.vector
        def _(dve):
            split_next = [0]
            order = [0]

            def chain(ins, back=0):
                order[0] += 1
                ins.then_inc(S["dve_order"], 1)
                dve.wait_ge(S["dve_order"], order[0] - back)

            def split_lo(t, e=None):
                s, h = t % RAW, t % HI
                dve.wait_ge(S["hi_ready"], t + 1 if e is None else e * N_EXP + (t + 1))
                n = tile_floats(t)
                dve.tensor_tensor(lo[:, s, 0:n], raw[:, s, 0:n], hi[:, h, 0:n].bitcast(F32), ALU.subtract).then_inc(
                    S["lo_ready"], 1)

            def split_to(t):
                while split_next[0] < t:
                    split_lo(split_next[0])
                    split_next[0] += 1

            def bc(ap, n):
                return ap.unsqueeze(2).broadcast_to([P, ap.shape[1], n])

            def norm_scale(i):
                g = i % G
                dve.wait_ge(S["rstd_ready"], i + 1)
                if i < G:
                    dve.wait_ge(S["tab_in"], 16)
                dve.tensor_scalar(diag[:, g, :], ident, rstd[:, g:g + 1], None, ALU.mult).then_inc(S["diag_ready"], 1)

            def norm_modulate(i):
                l, which = i // 4, i % 4 // 2
                dve.wait_ge(S["unit_out"], n_out(("ada", l, 9 if which else 3)))
                gcol = colp[:, l, 8 * which:8 * which + 8].unsqueeze(2).broadcast_to([P, KT, G])
                sc = modcol[:, l, 2 * which + 1, :, :]
                dve.scalar_tensor_tensor(sc, sc, 1.0, gcol, ALU.add, ALU.mult).then_inc(S["mod_ready"], 1)
                dve.wait_ge(S["mod_ready"], 2 * l + which + 1)
                n = i // 2

                def modulate(half):
                    dve.wait_ge(S["xn_T"], 4 * n + 2 * half + 1)
                    for k in range(4 * half, 4 * half + 4):
                        ins = dve.tensor_scalar(hfT[:, 0, k, :], X[:, half, (k % 4) * P:(k % 4 + 1) * P],
                                                modcol[:, l, 2 * which + 1, k, 0:1], modcol[:, l, 2 * which, k, 0:1],
                                                ALU.mult, ALU.add)
                    ins.then_inc(S["hf_ready"], 1)

                def operand_lo(q):
                    dve.wait_ge(S["hT_hi_ready"], 12 * l + 8 * which + q + 1)
                    dve.tensor_tensor(quarter(hT_lo, q), hfT[:, q % 2, 4 * (q // 2):4 * (q // 2) + 4, :],
                                      quarter(hT_hi, q).bitcast(F32), ALU.subtract).then_inc(S["hT_lo_ready"], 1)

                if i == 6:
                    modulate(0)
                    modulate(1)
                    return
                modulate(0)
                operand_lo(0)
                modulate(1)
                for q in (1, 2, 3):
                    operand_lo(q)

            def run(tiles):
                for u, t, first, last in tiles:
                    split_to(t + HI)

            for l in range(L):
                if l == 0:
                    dve.memset(ada_hl[:].bitcast(F32), 0.0).then_inc(S["ada_st"], 1)
                    dve.memset(ada_h0[:].bitcast(F32), 0.0).then_inc(S["ada_st"], 1)
                    dve.wait_ge(S["ada_st"], 2)
                    dve.wait_ge(S["sil_th"], 1)
                    chain(dve.scalar_tensor_tensor(sil[:, 1, :], sil[:, 0, :], 1.0, ccol[:], ALU.add, ALU.mult))
                    chain(dve.tensor_scalar(sil[:, 0, :], sil[:, 1, :], 0.5, None, ALU.mult))
                    src = sil[:, 0, :].rearrange("p (g k) -> p k g", g=G)
                    hl = ada_hl[:, 0:4 * KT].rearrange("p (k v) -> p k v", v=4)
                    h0 = ada_h0[:, 0:4 * KT].rearrange("p (k v) -> p k v", v=4)
                    chain(dve.tensor_copy(hl[:, :, 0:2], src))
                    dve.tensor_copy(h0[:, :, 0:2], src).then_inc(S["ada_st"], 1)
                    dve.tensor_tensor(hl[:, :, 2:4], src, hl[:, :, 0:2].bitcast(F32), ALU.subtract).then_inc(
                        S["ada_st"], 1)
                    split_to(HI)
                for g in range(G):
                    norm_scale(4 * l + g)
                if l == 0:
                    run(Units(PRELUDE).take(8))
                    split_to(8 + HI)
                norm_modulate(4 * l)
                units = Units(mixer_units(l))

                def fill(step):
                    run(units.take(FILL[step][l]))

                def merged_lo(q):
                    dve.wait_ge(S["hT_hi_ready"], 12 * l + 4 + q + 1)
                    dve.scalar_tensor_tensor(quarter(hT_lo, q), x_bank(q).rearrange("p (k t) -> p k t", t=P), 0.5,
                                             quarter(hT_hi, q).bitcast(F32), ALU.mult, ALU.subtract).then_inc(
                        S["hT_lo_ready"], 1)

                def branch_product(b):
                    run(units.product(b))
                    split_to(t_branch_end(l, b) + (1 if b == 0 else 0))
                    dve.wait_ge(S["unit_out"], n_out(("gate", l, GATE_OF[b] + 1)))
                    n = BR_ORDER.index(b)
                    if b == 0:
                        for q in range(4):
                            if q == 0:
                                dve.wait_ge(S["group_0_done"], 6 * l + n + 1)
                            if q == 1:
                                dve.wait_ge(S["tile_used"], t_branch_end(l, b))
                            cs = slice(512 * (q // 2), 512 * (q // 2) + 512)
                            gt = gates[:, q % 2, cs]
                            ins = dve.scalar_tensor_tensor(gt, gt, 1.0, B[:, 2 * (q % 2) + q // 2, :], ALU.add, ALU.mult)
                            ins.then_inc(S["a_gated"], 1)
                            dve.wait_ge(S["a_gated"], 4 * l + q + 1)
                            if q >= 2:
                                dve.sem_inc(S["br_used"], 1)
                            dve.tensor_tensor(mg[q % 2][:, cs], mg[q % 2][:, cs], gt, ALU.add).then_inc(
                                S["mg_ready"], 1)
                            if q == 2:
                                merged_lo(0)
                        return
                    for g in range(G):
                        if g == 0:
                            dve.wait_ge(S["group_0_done"], 6 * l + n + 1)
                        else:
                            dve.wait_ge(S["tile_used"], t_branch_end(l, b))
                        gt = gates[:, g, b * D:(b + 1) * D]
                        dve.scalar_tensor_tensor(gt, gt, 1.0, B[:, 2 * g:2 * g + 2, :].rearrange("p b n -> p (b n)"),
                                                 ALU.add, ALU.mult).then_inc(S["br_used"], 1)
                    dve.wait_ge(S["br_used"], 8 * l + 2 * n + 2)
                    if b != 2:
                        for g in range(G):
                            ins = dve.tensor_tensor(mg[g], mg[g], gates[:, g, b * D:(b + 1) * D], ALU.add)
                        chain(ins)

                dve.memset(glu_p[:], 0.0).then_inc(S["glu_zero"], 1)
                fill("c_in")
                for g in range(G):
                    dve.wait_ge(S["c_th"], 2 * l + g + 1)
                    dve.scalar_tensor_tensor(tmp2[:, g * 256:(g + 1) * 256], tmp2[:, g * 256:(g + 1) * 256], 1.0,
                                             proj[:, g, CC:CC + CCH], ALU.add, ALU.mult).then_inc(S["c_glu"], 1)
                fill("c_glu")
                lam_init = 0.8 - 0.6 * float(np.exp(-0.3 * l))
                dve.wait_ge(S[f"prm_in{l}"], 160)
                lm = GAIN["lam"].rearrange("p (a b d) -> p a b d", a=2, b=2)
                chain(dve.tensor_tensor(tmp1[:, 0:128].rearrange("p (a d) -> p a d", a=2), lm[:, :, 0, :],
                                        lm[:, :, 1, :], ALU.mult))
                dve.tensor_reduce(lam2, tmp1[:, 0:128].rearrange("p (a d) -> p a d", a=2), AX.X, ALU.add).then_inc(
                    S["lam_p"], 1)
                chain(dve.tensor_scalar(GAIN["sub"], GAIN["sub"], 1.0 - lam_init, None, ALU.mult))
                dve.wait_ge(S["c_T_sb"], 2 * (l + 1))
                tiles = units.take(FILL["d_pd"][l]) + units.take(FILL["c_conv"][l])
                for c in range(2):
                    chain(dve.tensor_scalar(conv[:, c, :, :], glu_p[:, c, :, 0:P], colp[:, l, 20 + c:21 + c],
                                            colp[:, l, 16 + c:17 + c], ALU.mult, ALU.add), back=c)
                for k in range(1, TAPS):
                    for c in range(2):
                        w = colp[:, l, 20 + 2 * k + c:21 + 2 * k + c]
                        ins = dve.scalar_tensor_tensor(conv[:, c, :, :], glu_p[:, c, :, k:k + P], w, conv[:, c, :, :],
                                                       ALU.mult, ALU.add)
                        if k == TAPS - 1 and c == 1:
                            ins.then_inc(S["c_conv"], 1)
                        else:
                            chain(ins, back=1)
                    if k % 4 == 2:
                        run(tiles[:1])
                        tiles = tiles[1:]
                run(tiles)
                for g in range(G):
                    dve.wait_ge(S["br_hi"], 8 * l + g + 1)
                    dve.tensor_tensor(brT_lo[:, 2:4, g, :], hdT[:, :, g, :], brT_hi[:, 2:4, g, :].bitcast(F32),
                                      ALU.subtract).then_inc(S["br_lo"], 1)
                fill("c_ln")
                dve.wait_ge(S["c_back"], l + 1)
                for g in range(G):
                    ins = dve.bn_stats(bnst[:, 6 * g:6 * g + 6], X[:, 1, g * 256:(g + 1) * 256])
                chain(ins)
                for g in range(G):
                    ins = dve.bn_aggr(mv[:, 2 * g:2 * g + 2], bnst[:, 6 * g:6 * g + 6])
                ins.then_inc(S["c_mv"], 1)
                dve.wait_ge(S["c_rstd"], l + 1)
                for g in range(G):
                    ins = dve.tensor_scalar(lnz[:, g, :], X[:, 1, g * 256:(g + 1) * 256], mv[:, 2 * g:2 * g + 1],
                                            rln[:, g:g + 1], ALU.subtract, ALU.mult)
                chain(ins)
                chain(dve.tensor_tensor(lnz[:], lnz[:], GAIN["lng"].unsqueeze(1).broadcast_to([P, G, CCH]), ALU.mult))
                dve.tensor_tensor(lnz[:], lnz[:], GAIN["lnb"].unsqueeze(1).broadcast_to([P, G, CCH]),
                                  ALU.add).then_inc(S["c_z"], 1)
                dve.wait_ge(S["c_zth"], l + 1)
                dve.scalar_tensor_tensor(lnz[:].rearrange("p g n -> p (g n)"), tmp2[:, 0:512], 1.0,
                                         lnz[:].rearrange("p g n -> p (g n)"), ALU.add, ALU.mult).then_inc(
                    S["c_act"], 1)
                fill("c_op")
                for g in range(G):
                    dve.wait_ge(S["br_hi"], 8 * l + 2 + g + 1)
                    dve.scalar_tensor_tensor(brT_lo[:, 0:2, g, :],
                                             X[:, 2 + g, 0:256].rearrange("p (h t) -> p h t", h=2), 0.5,
                                             brT_hi[:, 0:2, g, :].bitcast(F32), ALU.mult, ALU.subtract).then_inc(
                        S["br_lo"], 1)
                for g in range(G):
                    u = l * G + g
                    nk = 1 + g
                    dve.wait_ge(S["b_zrstd"], u + 1)
                    dve.scalar_tensor_tensor(proj[:, g, CBQ:CBQ + BQL], proj[:, g, CBQ:CBQ + BQL], zsum[:, 0:1],
                                             GAIN["bql"], ALU.mult, ALU.mult)
                    dve.scalar_tensor_tensor(proj[:, g, CKV:CKV + BKVL], proj[:, g, CKV:CKV + BKVL], zsum[:, 1:2],
                                             GAIN["bkvl"], ALU.mult, ALU.mult).then_inc(S["b_z"], 1)
                    fill(f"b_z{g}")
                    fill(f"b_zT{g}")
                    dve.wait_ge(S["b_up"], u + 1)
                    if g == 0:
                        dve.wait_ge(S[f"bw_in{l}"], 128)
                    for j in range(nk):
                        kpe = proj[:, g, CPE:CPE + BROPE] if j == 0 else kpe_c[:]
                        ins = dve.tensor_copy(qk96[:, 4 + 4 * j:8 + 4 * j, BNOPE:BQK],
                                              kpe.unsqueeze(1).broadcast_to([P, BH, BROPE]))
                    ins.then_inc(S["b_kpe"], 1)
                    nh = 4 + 4 * nk
                    dve.wait_ge(S["b_sq"], u + 1)
                    dve.tensor_reduce(nst16[:, 0:nh], prob[:, 0:nh * BQK].rearrange("p (h d) -> p h d", d=BQK), AX.X,
                                      ALU.add).then_inc(S["b_nst"], 1)
                    branch_product(2 if g == 0 else 3)
                    dve.wait_ge(S["b_rstd"], u + 1)
                    chain(dve.tensor_tensor(qk96[:, 0:nh, :], qk96[:, 0:nh, :], bc(rst16[:, 0:nh], BQK), ALU.mult))
                    gn = GAIN["bqk"].rearrange("p (a d) -> p a d", a=2)
                    dve.tensor_tensor(qk96[:, 0:4, :], qk96[:, 0:4, :], gn[:, 0:1, :].broadcast_to([P, 4, BQK]),
                                      ALU.mult)
                    ins = dve.tensor_tensor(qk96[:, 4:nh, :], qk96[:, 4:nh, :],
                                            gn[:, 1:2, :].broadcast_to([P, nh - 4, BQK]), ALU.mult)
                    if g == 0:
                        ins.then_inc(S["b_qk"], 1)
                    else:
                        chain(ins)
                        tail = qk96[:, 0:8, BNOPE:BQK]
                        cos = tab[:, C_RB:C_RB + BROPE].unsqueeze(1).broadcast_to([P, 8, BROPE])
                        sin = tab[:, C_RB + BROPE:C_RB + 2 * BROPE].rearrange("p (f i) -> p f i", i=2)
                        tc = prob[:, 1280:1536].rearrange("p (h d) -> p h d", d=BROPE)
                        ts = prob[:, 1536:1792].rearrange("p (h f i) -> p h f i", f=16, i=2)
                        t4 = tail.rearrange("p h (f i) -> p h f i", i=2)
                        dve.tensor_tensor(tc, tail, cos, ALU.mult)
                        for i in range(2):
                            ins = dve.tensor_tensor(ts[:, :, :, i], t4[:, :, :, 1 - i],
                                                    sin[:, :, i].unsqueeze(1).broadcast_to([P, 8, 16]), ALU.mult)
                        chain(ins)
                        dve.tensor_tensor(tail, tc, prob[:, 1536:1792].rearrange("p (h d) -> p h d", d=BROPE),
                                          ALU.add).then_inc(S["b_qk"], 1)
                    fill(f"b_up{g}")
                    fill(f"b_T{g}")
                    dve.wait_ge(S["b_scores"], u + 1)
                    Xs = X[:, 0:2, :].rearrange("p b (h k) -> p (b h) k", k=256)
                    chain(dve.tensor_reduce(mx[:, 0:4], Xs[:, :, 0:nk * P], AX.X, ALU.max))
                    dve.tensor_scalar(nmx[:, 0:4], mx[:, 0:4], -(BQK ** -0.5), None, ALU.mult).then_inc(S["b_nmx"], 1)
                    dve.wait_ge(S["b_exp"], u + 1)
                    chain(dve.reciprocal(rinv[:, 0:4], rsum[:, 0:4]))
                    pv = prob[:].rearrange("p (h k) -> p h k", k=256)
                    dve.tensor_tensor(pv[:, 0:4, 0:nk * P], pv[:, 0:4, 0:nk * P], bc(rinv[:, 0:4], nk * P),
                                      ALU.mult).then_inc(S["b_p"], 1)
                    fill(f"b_sm{g}")
                    fill(f"b_pT{g}")
                    fill(f"b_o{g}")
                    dve.wait_ge(S["br_hi"], 8 * l + 4 + g + 1)
                    dve.tensor_tensor(brT_lo[:, 0:2, g, :], X[:, 1, 0:256].rearrange("p (h t) -> p h t", h=2),
                                      brT_hi[:, 0:2, g, :].bitcast(F32), ALU.subtract).then_inc(S["br_lo"], 1)
                for g in range(G):
                    u = l * G + g
                    nk = 1 + g
                    qk = proj[:, g, 0:1024].rearrange("p (h d) -> p h d", d=AQK)
                    t1 = tmp1[:].rearrange("p (h d) -> p h d", d=AQK)
                    t2 = tmp2[:].rearrange("p (h d) -> p h d", d=AQK)
                    dve.wait_ge(S["a_sq"], u + 1)
                    dve.tensor_reduce(nst16, t1, AX.X, ALU.add).then_inc(S["a_nst"], 1)
                    if g == 0:
                        dve.wait_ge(S["lam_e"], l + 1)
                        chain(dve.tensor_tensor(neglam, lamx[:, 1:2], lamx[:, 0:1], ALU.subtract))
                        chain(dve.tensor_scalar(neglam, neglam, -lam_init, None, ALU.add))
                        branch_product(1)
                    dve.wait_ge(S["a_rstd"], u + 1)
                    chain(dve.tensor_tensor(t2, qk, bc(rst16, AQK), ALU.mult))
                    gn = GAIN["qk"].rearrange("p (a d) -> p a d", a=2)
                    for a in range(2):
                        ins = dve.tensor_tensor(qk[:, 8 * a:8 * a + 8, :], t2[:, 8 * a:8 * a + 8, :],
                                                gn[:, a:a + 1, :].broadcast_to([P, 8, AQK]), ALU.mult)
                    ins.then_inc(S["a_qk"], 1)
                    if g:
                        dve.wait_ge(S["a_qk"], u + 1)
                    if g == 1:
                        cos = tab[:, C_RA:C_RA + AQK].unsqueeze(1).broadcast_to([P, 16, AQK])
                        sin = tab[:, C_RA + AQK:C_RA + 2 * AQK].rearrange("p (f i) -> p f i", i=2)
                        dve.tensor_tensor(t1, qk, cos, ALU.mult)
                        q4 = proj[:, g, 0:1024].rearrange("p (h f i) -> p h f i", f=32, i=2)
                        t4 = tmp2[:].rearrange("p (h f i) -> p h f i", f=32, i=2)
                        for i in range(2):
                            ins = dve.tensor_tensor(t4[:, :, :, i], q4[:, :, :, 1 - i],
                                                    sin[:, :, i].unsqueeze(1).broadcast_to([P, 16, 32]), ALU.mult)
                        chain(ins)
                        dve.tensor_tensor(qk, t1, t2, ALU.add).then_inc(S["a_roped"], 1)
                    fill(f"a_n{g}")
                    fill(f"a_T{g}")
                    dve.wait_ge(S["a_scores"], u + 1)
                    Xs = X[:, :, :].rearrange("p b (h k) -> p (b h) k", k=256)
                    chain(dve.tensor_reduce(mx, Xs[:, :, 0:nk * P], AX.X, ALU.max))
                    dve.tensor_scalar(nmx, mx, -(AQK ** -0.5), None, ALU.mult).then_inc(S["a_nmx"], 1)
                    dve.wait_ge(S["a_exp"], u + 1)
                    chain(dve.reciprocal(rinv, rsum))
                    chain(dve.tensor_scalar(rinv[:, 4:8], rinv[:, 4:8], neglam, None, ALU.mult))
                    pv = prob[:].rearrange("p (h k) -> p h k", k=256)
                    chain(dve.tensor_tensor(pv[:, :, 0:nk * P], pv[:, :, 0:nk * P], bc(rinv, nk * P), ALU.mult))
                    dve.tensor_tensor(pv[:, 0:4, 0:nk * P], pv[:, 0:4, 0:nk * P], pv[:, 4:8, 0:nk * P],
                                      ALU.add).then_inc(S["a_w"], 1)
                    fill(f"a_sm{g}")
                    fill(f"a_wT{g}")
                    dve.wait_ge(S["a_osq"], u + 1)
                    dve.tensor_reduce(nst16[:, 0:4], tmp1[:, 0:512].rearrange("p (h d) -> p h d", d=AV), AX.X,
                                      ALU.add).then_inc(S["a_ost"], 1)
                    dve.wait_ge(S["a_orstd"], u + 1)
                    ov = o_sb[:].rearrange("p (h d) -> p h d", d=AV)
                    chain(dve.tensor_tensor(ov, X[:, 2, :].rearrange("p (h d) -> p h d", d=AV), bc(rst16[:, 0:4], AV),
                                            ALU.mult))
                    dve.tensor_tensor(ov, ov, GAIN["sub"].unsqueeze(1).broadcast_to([P, 4, AV]), ALU.mult).then_inc(
                        S["a_on"], 1)
                    fill(f"a_o{g}")
                    dve.wait_ge(S["br_hi"], 8 * l + 6 + g + 1)
                    dve.tensor_tensor(brT_lo[:, :, g, :], X[:, 3, :].rearrange("p (h t) -> p h t", h=4),
                                      brT_hi[:, :, g, :].bitcast(F32), ALU.subtract).then_inc(S["br_lo"], 1)

                branch_product(0)
                for q in (1, 2, 3):
                    merged_lo(q)
                split_to(t_out(l) + N_OUT)

                def residual(which):
                    for g in range(G):
                        dve.wait_ge(S["gb_sb"], 2 * (2 * l + which) + g + 1)
                        if g == 0 and (which == 0 or l == 0):
                            dve.wait_ge(S["group_0_done"], 6 * l + 5 + which)
                        elif which == 0:
                            dve.wait_ge(S["tile_used"], t_out(l) + N_OUT)
                        elif l == 0:
                            dve.wait_ge(S["tile_used"], t_ffn(0) + N_FFN)
                        src = B[:, 2 * g:2 * g + 2, :].rearrange("p b n -> p (b n)") if which == 0 or l == 0 \
                            else yacc[:, g, :]
                        chain(dve.tensor_tensor(gbc[:, g, :], gbc[:, g, :], src, ALU.mult))
                        dve.tensor_tensor(x[:, g, :], x[:, g, :], gbc[:, g, :], ALU.add).then_inc(S["x_ready"], 1)
                        dve.wait_ge(S["x_ready"], 4 * l + 2 * which + g + 1)

                if l == 0:
                    split_to(t_ffn(0) + HI - 1)
                residual(0)
                for g in range(G):
                    norm_scale(4 * l + 2 + g)
                norm_modulate(4 * l + 2)

                if l == 0:
                    tf = t_ffn(0)
                    for j, (c0, width) in enumerate(FCH):
                        w3_end = tf + 4 * j + (4 if width == 512 else 2)
                        split_to(w3_end + HI - 1)
                        dve.wait_ge(S["tile_used"], w3_end)
                        for g in range(G):
                            dve.wait_ge(S["silu_ready"], 2 * j + g + 1)
                            dve.tensor_tensor(hid[:, g, 0:width], silu_s[:, g, 0:width], B[:, 2 + g, 0:width],
                                              ALU.mult).then_inc(S["hid_ready"], 1)
                        nb = width // P
                        for g in range(G):
                            dve.wait_ge(S["hid_hi"], 2 * j + g + 1)
                            dve.tensor_tensor(hidT_lo[:, 4 * j:4 * j + nb, g, :],
                                              X[:, g, 0:width].rearrange("p (k t) -> p k t", t=P),
                                              hidT_hi[:, 4 * j:4 * j + nb, g, :].bitcast(F32), ALU.subtract).then_inc(
                                S["hid_lo"], 1)
                    split_to(tf + N_FFN + HI - 1)
                    residual(1)
                else:
                    dve.memset(ones[:], 1.0).then_inc(S["r_mask"], 1)
                    dve.memset(pickT[:].bitcast(F32), 0.0).then_inc(S["ys_used"], 1)
                    dve.memset(yacc[:], 0.0).then_inc(S["ys_used"], 1)
                    dve.wait_ge(S["r_psum"], 2)
                    lg = rtmp[:, :, 0:8]
                    chain(dve.tensor_copy(lg, X[:, 0:2, 0:8]))
                    cmp = rtmp[:, :, 128:192].rearrange("p g (e j) -> p g e j", j=8)
                    cm2 = rtmp[:, :, 192:256].rearrange("p g (e j) -> p g e j", j=8)
                    four = [P, G, 8, 8]
                    lj = lg.unsqueeze(2).broadcast_to(four)
                    le = lg.unsqueeze(3).broadcast_to(four)
                    tri = tab[:, C_TRI:C_TRI + 64].rearrange("p (e j) -> p e j", j=8)
                    dve.tensor_tensor(cmp, lj, le, ALU.is_gt)
                    chain(dve.tensor_tensor(cm2, lj, le, ALU.is_equal))
                    chain(dve.tensor_tensor(cm2, cm2, tri.unsqueeze(1).broadcast_to(four), ALU.mult))
                    chain(dve.tensor_tensor(cmp, cmp, cm2, ALU.add))
                    rank = rtmp[:, :, 8:16]
                    chain(dve.tensor_reduce(rank, cmp, AX.X, ALU.add))
                    first, second, mask = rtmp[:, :, 16:24], rtmp[:, :, 24:32], rtmp[:, :, 48:56]
                    dve.tensor_scalar(mask, rank, 1.0, None, ALU.is_le).then_inc(S["r_mask"], 1)
                    dve.tensor_scalar(first, rank, 0.0, None, ALU.is_equal)
                    chain(dve.tensor_scalar(second, rank, 1.0, None, ALU.is_equal))
                    chain(dve.tensor_tensor(rtmp[:, :, 32:40], second, first, ALU.subtract))
                    chain(dve.tensor_tensor(rtmp[:, :, 32:40], rtmp[:, :, 32:40], lg, ALU.mult))
                    dve.tensor_reduce(rtmp[:, :, 81:82], rtmp[:, :, 32:40], AX.X, ALU.add).then_inc(S["r_diff"], 1)
                    dve.wait_ge(S["r_exp"], 1)
                    ex, w1, w2 = rtmp[:, :, 80:81], rtmp[:, :, 82:83], rtmp[:, :, 83:84]
                    comb = rtmp[:, :, 88:96]
                    chain(dve.tensor_scalar(w1, ex, 1.0, None, ALU.add))
                    chain(dve.reciprocal(w1, w1))
                    chain(dve.tensor_tensor(w2, ex, w1, ALU.mult))
                    dve.tensor_tensor(first, first, w1.broadcast_to([P, G, 8]), ALU.mult)
                    chain(dve.tensor_tensor(second, second, w2.broadcast_to([P, G, 8]), ALU.mult))
                    chain(dve.tensor_tensor(comb, first, second, ALU.add))
                    dve.wait_ge(S["router_in"], 32)
                    pc = rtmp[:, :, 56:64]
                    dve.memset(job_pos[:, :, JOBS:JOBS + 1], -1.0)
                    dve.memset(job_comb[:, :, 0:1], 0.0)
                    dve.tensor_copy(job_comb[:, :, 1:1 + NE], comb)
                    dve.wait_ge(S["r_pos"], 1)
                    chain(dve.scalar_tensor_tensor(pc, X[:, 0:2, 16:24], 1.0, mask, ALU.add, ALU.mult))
                    chain(dve.tensor_scalar(job_pos[:, :, 0:NE], pc, 1.0, None, ALU.subtract))
                    dve.tensor_scalar(pc, pc, 129.0, None, ALU.subtract)
                    over, orank = rtmp[:, 0, 96:104], rtmp[:, 0, 104:112]
                    cmp1 = rtmp[:, 0, 128:192].rearrange("p (e j) -> p e j", j=8)
                    chain(dve.tensor_scalar(over, X[:, 2, 16:24], float(P), None, ALU.is_gt))
                    chain(dve.tensor_tensor(cmp1, over.unsqueeze(1).broadcast_to([P, 8, 8]), tri, ALU.mult))
                    chain(dve.tensor_reduce(orank, cmp1, AX.X, ALU.add))
                    fint = rtmp[:, 1, 105:109]
                    dve.tensor_reduce(fint[:, 0:1], over, AX.X, ALU.add)
                    K = JOBS - NE
                    sel = rtmp[:, 0, 192:192 + 8 * K].rearrange("p (k e) -> p k e", e=8)
                    some = rtmp[:, 1, 100:100 + K]
                    both = rtmp[:, :, 256:256 + 8 * K].rearrange("p g (k e) -> p g k e", e=8)
                    shape = [P, G, K, 8]
                    chain(dve.tensor_tensor(sel, orank.unsqueeze(1).broadcast_to([P, K, 8]),
                                            etab[:, 0:K].unsqueeze(2).broadcast_to([P, K, 8]), ALU.is_equal))
                    chain(dve.tensor_tensor(sel, sel, over.unsqueeze(1).broadcast_to([P, K, 8]), ALU.mult))
                    chain(dve.tensor_scalar(fint[:, 0:1], fint[:, 0:1], float(NE), None, ALU.add))
                    chain(dve.tensor_reduce(some, sel, AX.X, ALU.add))
                    jp = job_pos[:, :, NE:NE + K]
                    chain(dve.tensor_tensor(both, sel.unsqueeze(1).broadcast_to(shape),
                                            pc.unsqueeze(2).broadcast_to(shape), ALU.mult))
                    chain(dve.tensor_reduce(jp, both, AX.X, ALU.add))
                    chain(dve.tensor_scalar(some, some, 1.0, None, ALU.subtract))
                    chain(dve.tensor_tensor(jp, jp, some.unsqueeze(1).broadcast_to([P, G, K]), ALU.add))
                    chain(dve.tensor_tensor(both, sel.unsqueeze(1).broadcast_to(shape),
                                            comb.unsqueeze(2).broadcast_to(shape), ALU.mult))
                    chain(dve.tensor_reduce(job_comb[:, :, 1 + NE:1 + NE + K], both, AX.X, ALU.add))
                    chain(dve.tensor_tensor(sel, sel, etab[:, 0:8].unsqueeze(1).broadcast_to([P, K, 8]), ALU.mult))
                    chain(dve.tensor_reduce(fint[:, 1:1 + K], sel, AX.X, ALU.add))
                    dve.tensor_copy(job_int[:], fint).then_inc(S["jobs_ready"], 1)

                    def pick_job(e):
                        for g in range(G):
                            dve.tensor_scalar(pick[:, g, :], etab[:, 0:P], job_pos[:, g, bass.ds(e, 1)], None,
                                              ALU.is_equal).then_inc(S["pick_ready"], 1)

                    def gathered_lo(count):
                        dve.wait_ge(S["xg_psum"], count)
                        dve.tensor_copy(xg_lo[:], B[:, 2:4, :].rearrange("p b (k t) -> p (b k) t", t=P)).then_inc(
                            S["xg_ready"], 1)

                    pick_job(0)
                    for g in range(G):
                        dve.wait_ge(S["h_tok_hi"], g + 1)
                        dve.tensor_tensor(hT_lo[:, :, g, :],
                                          B[:, 2 * g:2 * g + 2, :].rearrange("p b (k t) -> p (b k) t", t=P),
                                          hT_hi[:, :, g, :].bitcast(F32), ALU.subtract).then_inc(S["h_tok_lo"], 1)
                    gathered_lo(1)
                    t0e = t_ffn(1)
                    nch = len(ECH)
                    dve.wait_ge(S["jobs_ready"], 1)
                    n_jobs = dve.value_load(job_int[0:1, 0:1], min_val=NE, max_val=JOBS)

                    def output_lo(e):
                        dve.wait_ge(S["ye_hi_ready"], e + 1)
                        dve.tensor_tensor(ye_lo[:], X[:, 2:4, :].rearrange("p b n -> p (b n)"), ye_hi[:].bitcast(F32),
                                          ALU.subtract).then_inc(S["ye_lo_ready"], 1)

                    def accumulate(e):
                        for g in range(G):
                            dve.wait_ge(S["ys_psum"], e * 2 + (g + 1))
                            bank = X[:, 2:4, :] if g == 0 else X[:, 0:2, :]
                            dve.scalar_tensor_tensor(yacc[:, g, :], bank.rearrange("p b n -> p (b n)"),
                                                     job_comb[:, g, bass.ds(e, 1)], yacc[:, g, :], ALU.mult,
                                                     ALU.add).then_inc(S["ys_used"], 1)

                    with dve.Fori(0, n_jobs) as e:
                        nxt = [t0e]

                        def esplit(upto):
                            while nxt[0] < min(upto, t0e + N_EXP):
                                split_lo(nxt[0], e)
                                nxt[0] += 1

                        def hid_lo_e(j):
                            dve.wait_ge(S["e_hid_hi"], e * nch + (j + 1))
                            dve.tensor_tensor(hidE_lo[:, 4 * j:4 * j + 4, :],
                                              X[:, j % 2, :].rearrange("p (k t) -> p k t", t=P),
                                              hidE_hi[:, 4 * j:4 * j + 4, :].bitcast(F32), ALU.subtract).then_inc(
                                S["e_hid_lo"], 1)

                        esplit(t0e + HI)
                        output_lo(e)
                        for j in range(nch):
                            esplit(t0e + 4 * j + 2 + HI - 1)
                            if j:
                                hid_lo_e(j - 1)
                            esplit(t0e + 4 * j + 4 + HI - 1)
                            dve.wait_ge(S["tile_used"], e * N_EXP + (t0e + 4 * j + 4))
                            dve.wait_ge(S["e_silu"], e * nch + (j + 1))
                            if j >= 2:
                                dve.wait_ge(S["e_hidT"], e * nch + (j - 1))
                            dve.tensor_tensor(hid_e[:, j % 2, :], silu_e[:, j % 2, :], B[:, 2 * (j % 2) + 1, :],
                                              ALU.mult).then_inc(S["e_hid"], 1)
                            if j == 0:
                                accumulate(e)
                            if j == 3:
                                dve.wait_ge(S["pickT_psum"], e + 1)
                                pick_job(e + 1)
                        hid_lo_e(nch - 1)
                        gathered_lo(e * 2 + 3)
                        esplit(t0e + N_EXP)
                    output_lo(n_jobs)
                    accumulate(n_jobs)
                    dve.wait_ge(S["ys_used"], n_jobs * 2 + 4)
                    residual(1)

        @block.tensor
        def _(pe):
            def tile_done(ins):
                ins.then_inc(S["tile_used"], 1)

            def wait_tile(t, e=None):
                pe.wait_ge(S["lo_ready"], t + 1 if e is None else e * N_EXP + (t + 1))

            def parts(t, nk, width):
                h = hi[:, t % HI, 0:nk * width].rearrange("p (k n) -> p k n", n=width)
                lw = lo[:, t % RAW, 0:nk * width].rearrange("p (k n) -> p k n", n=width)
                return h, lw

            def product(out, s_hi, s_lo, w_hi, w_lo, start, stop):
                pe.matmul(out, s_hi, w_hi, start=start, stop=False)
                pe.matmul(out, s_hi, w_lo, start=False, stop=False)
                return pe.matmul(out, s_lo, w_hi, start=False, stop=stop)

            def rows_tile(t, a_hi, a_lo, banks, k0, first, last, width=512, nk=4, ready=None):
                wait_tile(t)
                wh, wl = parts(t, nk, width)
                for g in range(G):
                    if ready is not None:
                        pe.wait_ge(S["hT_lo_ready"], ready + 2 * (k0 // 4) + g + 1)
                    for k in range(nk):
                        ins = product(banks[g][:, 0:width], a_hi[:, k0 + k, g, :], a_lo[:, k0 + k, g, :], wh[:, k, :],
                                      wl[:, k, :], first and k == 0, last and k == nk - 1)
                tile_done(ins)
                return ins

            def full_tile(t, a_hi, a_lo, k0, first, last, ready=None):
                wait_tile(t)
                wh, wl = parts(t, 2, D)
                for g in range(G):
                    if ready is not None:
                        pe.wait_ge(S["hT_lo_ready"], ready + 2 * (k0 // 4) + g + 1)
                    for half in range(2):
                        for k in range(2):
                            cs = slice(512 * half, 512 * half + 512)
                            ins = product(B[:, 2 * g + half, :], a_hi[:, k0 + k, g, :], a_lo[:, k0 + k, g, :],
                                          wh[:, k, cs], wl[:, k, cs], first and k == 0, last and k == 1)
                    if last and g == 0:
                        ins.then_inc(S["group_0_done"], 1)
                tile_done(ins)

            def norm_T(i):
                for q in range(4):
                    g = q % 2
                    pe.wait_ge(S["diag_ready"], i + g + 1)
                    for k in range(4):
                        kk = 4 * (q // 2) + k
                        ins = pe.matmul(x_bank(q)[:, k * P:(k + 1) * P], x[:, g, kk * P:(kk + 1) * P], diag[:, g, :],
                                        start=True, stop=True)
                    ins.then_inc(S["xn_T"], 1)

            def unit_tile(u, t, first, last):
                kind, lu, c = u
                n = NUMBER[u]
                if first:
                    if n >= 2:
                        pe.wait_ge(S["unit_out"], 2 * (n - 1))
                    if products[0]:
                        pe.wait_ge(S["br_used"], 2 * (products[0] - 1) + n % 2 + 1)
                if kind != "ada":
                    width = (IN_CHUNKS if kind == "in" else GATE_CHUNKS)[c][1]
                    rows_tile(t, hT_hi, hT_lo, [B[:, 2 * (n % 2) + g, :] for g in range(G)], 4 * (not first), first,
                              last, width=width, ready=12 * lu if kind == "in" and c == 0 else None)
                    return
                bank = B[:, 2 * (n % 2), :]
                if first:
                    pe.matmul(bank, tab[32 * lu:32 * lu + 12, C_SELB + 4 * c:C_SELB + 4 * c + P],
                              adarow[32 * lu:32 * lu + 12, :], start=True, stop=False)
                wait_tile(t)
                wh, wl = parts(t, 4, 512)
                for k in range(4):
                    kk = 4 * (4 * (not first) + k)
                    pe.matmul(bank, ada_hl[:, kk:kk + P], wh[:, k, :], start=False, stop=False)
                    ins = pe.matmul(bank, ada_h0[:, kk:kk + P], wl[:, k, :], start=False, stop=(last and k == 3))
                tile_done(ins)

            products = [0]
            rows = [None, None]

            def turn_rows():
                u = rows[0]
                if u in ADA_COLS:
                    n = NUMBER[u]
                    pe.wait_ge(S["ada_row"], ADA_COLS[u])
                    for q in range(4):
                        ins = pe.matmul(B[:, 2 * (n % 2) + 1, 2 * q:2 * q + 2], adarow[64:68, q * P:(q + 1) * P],
                                        tab[64:68, C_SEL:C_SEL + 2], start=True, stop=True)
                    ins.then_inc(S["ada_cols"], 1)
                rows[0] = None

            def run(tiles):
                for u, t, first, last in tiles:
                    unit_tile(u, t, first, last)
                    if first:
                        turn_rows()
                    if last:
                        rows[0] = u

            for l in range(L):
                if l == 0:
                    pe.wait_ge(S["tab_in"], 16)
                    pe.wait_ge(S["c_in"], 32)
                    pe.transpose(X[:, 0, 0:16], rowp[96:112, 0, :], ident[96:112, 96:112]).then_inc(S["cols_psum"], 1)
                    pe.wait_ge(S["ada_st"], 4)
                    pe.wait_ge(S["adab_in"], 32)
                    pe.wait_ge(S["cols_sb"], 1)
                    prelude = Units(PRELUDE)
                    run(prelude.take(2))
                    pe.wait_ge(S["rows_in"], 5 * L * 16)
                    for j in range(L):
                        ins = pe.transpose(X[:, 3, 82 * j:82 * j + 82], rowp[0:82, j, :], ident[0:82, 0:82])
                    ins.then_inc(S["cols_psum"], 1)
                    run(prelude.take(4))
                    pe.wait_ge(S["cols_sb"], 2)
                else:
                    pe.wait_ge(S["x_ready"], 4)
                norm_T(4 * l)
                if l == 0:
                    run(prelude.take(2))
                    turn_rows()

                units = Units(mixer_units(l))

                def fill(step):
                    run(units.take(FILL[step][l]))

                def branch_product(b):
                    run(units.product(b))
                    turn_rows()
                    pos = BR_ORDER.index(b)
                    pe.wait_ge(S["br_lo"], 8 * l + (2, 4, 6, 8)[pos])
                    pe.wait_ge(S["unit_out"], n_out(last_unit(l, b)))
                    if products[0]:
                        pe.wait_ge(S["br_used"], 2 * products[0])
                    k0 = 2 if b == 3 else 0
                    for i in range(N_BR[b]):
                        full_tile(t_branch(l, b) + i, brT_hi, brT_lo, k0 + 2 * i, i == 0, i == N_BR[b] - 1)
                    products[0] += 1

                fill("c_in")
                fill("c_glu")
                pe.wait_ge(S["c_glu"], 2 * (l + 1))
                for g in range(G):
                    for c in range(2):
                        at = g * 256 + c * P
                        ins = pe.transpose(X[:, 0, at:at + P], tmp2[:, at:at + P], ident)
                ins.then_inc(S["c_T"], 1)
                pe.wait_ge(S["unit_out"], n_out(("in", l, IN_D)))
                for g in range(G):
                    for i in range(4):
                        r = slice(64 * (i % 2), 64 * (i % 2) + 64)
                        at = g * 256 + (i // 2) * P
                        ins = pe.matmul(X[r, 3, at:at + P], proj[:, g, CD + i * DG:CD + (i + 1) * DG],
                                        tab[:, C_POOL + i * P:C_POOL + (i + 1) * P], start=True, stop=True)
                ins.then_inc(S["d_pd"], 1)
                fill("d_pd")
                pe.wait_ge(S[f"bw_in{l}"], 128)
                pe.wait_ge(S["d_pd_sb"], l + 1)
                for g in range(G):
                    for i in range(4):
                        r = slice(64 * (i % 2), 64 * (i % 2) + 64)
                        at = g * 256 + (i // 2) * P
                        ins = pe.matmul(X[r, 0, at:at + P], dg_w[r, i // 2, :], pdT[r, g, i // 2, :], start=True,
                                        stop=True)
                ins.then_inc(S["d_hd"], 1)
                fill("c_conv")
                pe.wait_ge(S["c_conv"], l + 1)
                for g in range(G):
                    for c in range(2):
                        at = g * 256 + c * P
                        ins = pe.transpose(X[:, 1, at:at + P], conv[:, c, g, :], ident)
                ins.then_inc(S["c_back"], 1)
                fill("c_ln")
                pe.wait_ge(S["c_act"], l + 1)
                for g in range(G):
                    for c in range(2):
                        ins = pe.transpose(X[:, 2 + g, c * P:(c + 1) * P], lnz[:, g, c * P:(c + 1) * P], ident)
                ins.then_inc(S["c_zT"], 1)
                fill("c_op")
                pe.wait_ge(S[f"bw_in{l}"], 128)
                zT = wT[:].rearrange("p a b t -> p (a b) t")
                for g in range(G):
                    u = l * G + g
                    nk = 1 + g
                    fill(f"b_z{g}")
                    pe.wait_ge(S["b_z"], u + 1)
                    srcs = [proj[:, g, CBQ:CBQ + P], proj[:, g, CBQ + P:CBQ + 2 * P], proj[:, g, CKV:CKV + P]]
                    if g == 1:
                        srcs.append(ckv_c[:])
                        pe.wait_ge(S["br_lo"], 8 * l + 5)
                    for j, src in enumerate(srcs):
                        ins = pe.transpose(X[:, 0, j * P:(j + 1) * P], src, ident)
                    ins.then_inc(S["b_zT"], 1)
                    fill(f"b_zT{g}")
                    pe.wait_ge(S["b_zT_sb"], u + 1)
                    for k in range(2):
                        pe.matmul(X[:, 1, 0:384], zT[:, k, :], uq_w[:, k, :], start=(k == 0), stop=(k == 1))
                    for j in range(nk):
                        ins = pe.matmul(X[:, 2 + j, :], zT[:, 2 + j, :], ukv_w[:], start=True, stop=True)
                    ins.then_inc(S["b_up"], 1)
                    branch_product(2 if g == 0 else 3)
                    fill(f"b_up{g}")
                    pe.wait_ge(S["b_qk"], u + 1)
                    for j in range(1 + nk):
                        for h in range(4):
                            ins = pe.transpose(X[0:BQK, j, h * P:(h + 1) * P], qk96[:, 4 * j + h, :], ident)
                    ins.then_inc(S["b_T"], 1)
                    fill(f"b_T{g}")
                    pe.wait_ge(S["b_T_sb"], u + 1)
                    for h in range(4):
                        ins = pe.matmul(X[:, h // 2, (h % 2) * 256:(h % 2) * 256 + nk * P], qT[0:BQK, h, :],
                                        kT[0:BQK, h, 0:nk, :].rearrange("p j t -> p (j t)"), start=True, stop=True)
                    ins.then_inc(S["b_scores"], 1)
                    fill(f"b_sm{g}")
                    pe.wait_ge(S["b_p"], u + 1)
                    for h in range(4):
                        for j in range(nk):
                            at = ((h % 2) * 2 + j) * P
                            ins = pe.transpose(X[:, 2 + h // 2, at:at + P],
                                               prob[:, h * 256 + j * P:h * 256 + (j + 1) * P], ident)
                    ins.then_inc(S["b_pT"], 1)
                    fill(f"b_pT{g}")
                    pe.wait_ge(S["b_pT_sb"], u + 1)
                    for h in range(4):
                        for j in range(nk):
                            ins = pe.matmul(X[:, 0, h * BV:(h + 1) * BV], wT[:, h, j, :], v_b[:, j, h, :],
                                            start=(j == 0), stop=(j == nk - 1))
                    ins.then_inc(S["b_o"], 1)
                    fill(f"b_o{g}")
                    pe.wait_ge(S["b_o_sb"], u + 1)
                    for h in range(2):
                        ins = pe.transpose(X[:, 1, h * P:(h + 1) * P], o_sb[:, h * P:(h + 1) * P], ident)
                    ins.then_inc(S["b_oT"], 1)
                for g in range(G):
                    u = l * G + g
                    nk = 1 + g
                    if g == 0:
                        branch_product(1)
                    fill(f"a_n{g}")
                    pe.wait_ge(S["a_qk"], u + 1)
                    if g == 1:
                        pe.wait_ge(S["a_roped"], l + 1)
                        pe.wait_ge(S[f"kv_in{l}"], 32)
                        pe.wait_ge(S["br_lo"], 8 * l + 7)
                    for j in range(2 + g):
                        for hp in range(4):
                            src = proj[:, g, 512 * j + hp * P:512 * j + (hp + 1) * P] if j < 2 \
                                else k_c[:, hp * P:(hp + 1) * P]
                            ins = pe.transpose(X[:, j, hp * P:(hp + 1) * P], src, ident)
                    ins.then_inc(S["a_T"], 1)
                    fill(f"a_T{g}")
                    pe.wait_ge(S["a_T_sb"], u + 1)
                    for h in range(8):
                        hp, i = h // 2, h % 2
                        r = slice(64 * i, 64 * i + 64)
                        ins = pe.matmul(X[:, 2 * i + hp // 2, (hp % 2) * 256:(hp % 2) * 256 + nk * P], qT[r, hp, :],
                                        kT[r, hp, 0:nk, :].rearrange("p j t -> p (j t)"), start=True, stop=True)
                    ins.then_inc(S["a_scores"], 1)
                    fill(f"a_sm{g}")
                    pe.wait_ge(S["a_w"], u + 1)
                    for h in range(4):
                        for j in range(nk):
                            at = ((h % 2) * 2 + j) * P
                            ins = pe.transpose(X[:, h // 2, at:at + P], prob[:, h * 256 + j * P:h * 256 + (j + 1) * P],
                                               ident)
                    ins.then_inc(S["a_wT"], 1)
                    fill(f"a_wT{g}")
                    pe.wait_ge(S["a_wT_sb"], u + 1)
                    for h in range(4):
                        for j in range(nk):
                            v = proj[:, g, CV + h * AV:CV + (h + 1) * AV] if j == 0 else v_c[:, h * AV:(h + 1) * AV]
                            ins = pe.matmul(X[:, 2, h * AV:(h + 1) * AV], wT[:, h, j, :], v, start=(j == 0),
                                            stop=(j == nk - 1))
                    ins.then_inc(S["a_o"], 1)
                    fill(f"a_o{g}")
                    pe.wait_ge(S["a_on"], u + 1)
                    for h in range(4):
                        ins = pe.transpose(X[:, 3, h * P:(h + 1) * P], o_sb[:, h * P:(h + 1) * P], ident)
                    ins.then_inc(S["a_oT"], 1)
                branch_product(0)
                for q in range(4):
                    pe.wait_ge(S["mg_ready"], 4 * l + q + 1)
                    for k in range(4):
                        kk = 4 * (q // 2) + k
                        ins = pe.transpose(x_bank(q)[:, k * P:(k + 1) * P], mg[q % 2][:, kk * P:(kk + 1) * P], ident)
                    ins.then_inc(S["mg_T"], 1)

                def gate_rows(which, bank=X):
                    for g in range(G):
                        for half in range(2):
                            r = 32 * (2 * which + half)
                            ins = pe.matmul(bank[:, 2 * g + half, :], tab[r:r + 4, C_SELG + g * P:C_SELG + (g + 1) * P],
                                            grow[r:r + 4, l, :], start=True, stop=True)
                    ins.then_inc(S["gb_psum"], 1)

                for i in range(N_OUT):
                    full_tile(t_out(l) + i, hT_hi, hT_lo, 2 * i, i == 0, i == N_OUT - 1, ready=12 * l + 4)
                    if i == N_OUT - 2:
                        gate_rows(0)
                pe.wait_ge(S["gb_sb"], 4 * l + 2)
                norm_T(4 * l + 2)

                if l == 0:
                    tf = t_ffn(0)
                    for j, (c0, width) in enumerate(FCH):
                        nk = TW // width
                        n_t = KT // nk
                        for w in range(2):
                            if j:
                                if w == 0:
                                    pe.wait_ge(S["silu_ready"], 2 * j)
                                else:
                                    pe.wait_ge(S["hid_ready"], 2 * j)
                            for i in range(n_t):
                                rows_tile(tf + 4 * j + w * n_t + i, hT_hi, hT_lo, [B[:, 2 * w, :], B[:, 2 * w + 1, :]],
                                          nk * i, i == 0, i == n_t - 1, width=width, nk=nk,
                                          ready=8 if j == w == 0 else None)
                        pe.wait_ge(S["hid_ready"], 2 * j + 2)
                        if j:
                            pe.wait_ge(S["hid_lo"], 2 * j)
                        for g in range(G):
                            for k in range(width // P):
                                ins = pe.transpose(X[:, g, k * P:(k + 1) * P], hid[:, g, k * P:(k + 1) * P], ident)
                        ins.then_inc(S["hid_T"], 1)
                    pe.wait_ge(S["hid_lo"], 2 * len(FCH))
                    gate_rows(1)
                    for i in range(N_FFN_DN):
                        full_tile(tf + N_FFN_UP + i, hidT_hi, hidT_lo, 2 * i, i == 0, i == N_FFN_DN - 1)
                else:
                    pe.wait_ge(S["x_ready"], 6)
                    gate_rows(1, B)
                    pe.wait_ge(S["router_in"], 32)
                    for g in range(G):
                        if g:
                            pe.wait_ge(S["hf1_ready"], 8)
                        else:
                            pe.wait_ge(S["hf_ready"], 8)
                        for k in range(KT):
                            ins = pe.matmul(X[:, g, 0:8], hfT[:, g, k, :], router[:, k, :], start=(k == 0),
                                            stop=(k == KT - 1))
                        ins.then_inc(S["r_psum"], 1)
                    def tokens(g):
                        for k in range(KT):
                            ins = pe.transpose(B[:, 2 * g + k // 4, (k % 4) * P:(k % 4 + 1) * P], hfT[:, g, k, :],
                                               ident)
                        ins.then_inc(S["h_tok"], 1)

                    pe.wait_ge(S["gb_sb"], 8)
                    tokens(0)
                    pe.wait_ge(S["r_mask"], 2)
                    before = etab[:, P:2 * P]
                    m = [rtmp[:, g, 48:56] for g in range(G)]
                    pe.matmul(X[:, 0, 16:24], before, m[0], start=True, stop=True)
                    pe.matmul(X[:, 1, 16:24], before, m[1], start=True, stop=False)
                    pe.matmul(X[:, 1, 16:24], ones[:], m[0], start=False, stop=True)
                    pe.matmul(X[:, 2, 16:24], ones[:], m[0], start=True, stop=False)
                    pe.matmul(X[:, 2, 16:24], ones[:], m[1], start=False, stop=True).then_inc(S["r_pos"], 1)
                    tokens(1)

                    def gather(part):
                        src, b0 = (hT_lo, 2) if part == 0 else (hT_hi, 0)
                        for k in range(KT):
                            for g in range(G):
                                ins = pe.matmul(B[:, b0 + k // 4, (k % 4) * P:(k % 4 + 1) * P], src[:, k, g, :],
                                                pick[:, g, :], start=(g == 0), stop=(g == G - 1))
                        ins.then_inc(S["xg_psum"], 1)

                    pe.wait_ge(S["pick_ready"], 2)
                    pe.wait_ge(S["h_tok_lo"], 2)
                    gather(0)
                    gather(1)
                    pe.wait_ge(S["jobs_ready"], 1)
                    t0e = t_ffn(1)
                    nch = len(ECH)
                    n_jobs = pe.value_load(job_int[0:1, 0:1], min_val=NE, max_val=JOBS)

                    def scatter(e):
                        pe.wait_ge(S["ye_lo_ready"], e + 1)
                        for g in range(G):
                            b0 = 2 if g == 0 else 0
                            for half in range(2):
                                cs = slice(512 * half, 512 * half + 512)
                                pe.matmul(X[:, b0 + half, :], pickT[:, g, :], ye_hi[:, cs], start=True, stop=False)
                                ins = pe.matmul(X[:, b0 + half, :], pickT[:, g, :], ye_lo[:, cs], start=False,
                                                stop=True)
                            ins.then_inc(S["ys_psum"], 1)

                    with pe.Fori(0, n_jobs) as e:
                        def up(j, w):
                            for i in range(2):
                                t = t0e + 4 * j + 2 * w + i
                                wait_tile(t, e)
                                wh, wl = parts(t, 4, 512)
                                for k in range(4):
                                    ins = product(B[:, 2 * (j % 2) + w, :], xg_hi[:, 4 * i + k, :],
                                                  xg_lo[:, 4 * i + k, :], wh[:, k, :], wl[:, k, :],
                                                  i == 0 and k == 0, i == 1 and k == 3)
                                tile_done(ins)

                        def turn(j):
                            pe.wait_ge(S["e_hid"], e * nch + (j + 1))
                            if j >= 2:
                                pe.wait_ge(S["e_hid_lo"], e * nch + (j - 1))
                            for k in range(4):
                                ins = pe.transpose(X[:, j % 2, k * P:(k + 1) * P], hid_e[:, j % 2, k * P:(k + 1) * P],
                                                   ident)
                            ins.then_inc(S["e_hidT"], 1)

                        pe.wait_ge(S["xg_ready"], e * 2 + 2)
                        for j in range(nch):
                            if j >= 2:
                                pe.wait_ge(S["e_hid"], e * nch + (j - 1))
                            up(j, 0)
                            if j == 1:
                                pe.wait_ge(S["ys_used"], e * 2 + 4)
                            if j:
                                turn(j - 1)
                            up(j, 1)
                            if j == 0:
                                scatter(e)
                            if j == 1:
                                for g in range(G):
                                    ins = pe.transpose(X[:, 2, g * P:(g + 1) * P], pick[:, g, :].bitcast(F32), ident)
                                ins.then_inc(S["pickT_psum"], 1)
                        pe.wait_ge(S["pick_ready"], e * 2 + 4)
                        gather(0)
                        turn(nch - 1)
                        gather(1)
                        pe.wait_ge(S["pickT_sb"], e + 1)
                        for i in range(N_EXP_DN):
                            if i % 2 == 0:
                                pe.wait_ge(S["e_hid_lo"], e * nch + (i // 2 + 1))
                            t = t0e + N_EXP_UP + i
                            wait_tile(t, e)
                            wh, wl = parts(t, 2, D)
                            for half in range(2):
                                for k in range(2):
                                    cs = slice(512 * half, 512 * half + 512)
                                    ins = product(X[:, 2 + half, :], hidE_hi[:, 2 * i + k, :], hidE_lo[:, 2 * i + k, :],
                                                  wh[:, k, cs], wl[:, k, cs], i == 0 and k == 0,
                                                  i == N_EXP_DN - 1 and k == 1)
                            tile_done(ins)
                    scatter(n_jobs)


_INS = ['x_prompt', 'x_sample', 'cache_a_k', 'cache_a_v', 'cache_b_ckv', 'cache_b_kpe', 'c', 'c_ctx', 'ada_w', 'ada_b',
        'norm1_g', 'norm2_g', 'w_in', 'a_q_norm', 'a_k_norm', 'a_lambda', 'a_sub_norm', 'a_w_o', 'b_q_lora_norm',
        'b_kv_lora_norm', 'b_w_uq', 'b_w_ukv', 'b_q_norm', 'b_k_norm', 'b_w_o', 'c_dw', 'c_dw_b', 'c_ln_g', 'c_ln_b',
        'c_w_o', 'd_w_group', 'd_scale', 'd_w_o', 'w_out', 'ffn_w1', 'ffn_w3', 'ffn_w2', 'moe_router', 'moe_w1',
        'moe_w3', 'moe_w2']
_OUTS = [("y_prompt", (1, 128, 1024)), ("y_sample", (1, 128, 1024)), ("ak", (1, 2, 128, 8, 64)),
         ("av", (1, 2, 128, 4, 128)), ("ckv", (1, 2, 128, 128)), ("kpe", (1, 2, 128, 32))]


def kernel(**inputs):
    import concourse.bacc as _bacc
    from concourse.bass_utils import run_bass_kernel_spmd as _run

    nc = _bacc.Bacc("TRN2", target_bir_lowering=False, num_devices=1)
    arrays, args, outs = {}, {}, {}
    for name in _INS:
        a = np.ascontiguousarray(inputs[name])
        arrays[f"in_{name}"] = a
        args[name] = nc.dram_tensor(f"in_{name}", a.shape, F32, kind="ExternalInput").ap()
    arrays["in_tables"] = shape_tables()
    args["tables"] = nc.dram_tensor("in_tables", (P, C_ALL), F32, kind="ExternalInput").ap()
    for name, shape in _OUTS:
        outs[name] = nc.dram_tensor(f"out_{name}", shape, F32, kind="ExternalOutput").ap()
    trunk_kernel(nc, args, outs)
    r = _run(nc, [arrays], core_ids=[0])
    return tuple(r.results[0][f"out_{name}"] for name, _ in _OUTS)
```
